# Optimizing a Trainium2 kernel written in Bass

```python
import jax, jax.numpy as jnp
from jax import lax
import numpy as np
import math

D_MODEL = 1024
BATCH = 1
SEQ = 256
DEPTH = 1

ROPE_THETA = 10000.0
NORM_EPS = 1e-6
GN_EPS = 1e-5

RET_HEADS = 4
RET_DK = 64
RET_DV = 128
RET_CHUNK = 128

NSA_HEADS = 8
NSA_KV_HEADS = 2
NSA_DK = 64
NSA_GROUP = NSA_HEADS // NSA_KV_HEADS
CMP_BLOCK = 32
CMP_STRIDE = 16
CMP_HID = 256
SLC_BLOCK = 64
SLC_TOPK = 16
SLC_LOCAL = 2
WINDOW = 512
NSA_QBLOCK = 128
SEL_BIG = 1e9
NEG = -1e30

D_RET = RET_HEADS * RET_DV
D_NSA = NSA_HEADS * NSA_DK
D_MIX = D_RET + D_NSA

RET_QK = RET_HEADS * RET_DK
NSA_KV = NSA_KV_HEADS * NSA_DK
NSA_GATES = 3 * NSA_HEADS
SPLITS = [RET_QK, RET_QK, D_RET, D_RET, D_NSA] + [NSA_KV] * 6 + [NSA_GATES]
IN_COLS = sum(SPLITS)

D_FF = 2816
CONV_WIDTH = 3


def rms_norm(x, w):
    xf = x.astype(jnp.float32)
    y = xf * lax.rsqrt(jnp.mean(xf * xf, axis=-1, keepdims=True) + NORM_EPS)
    return (y * w.astype(jnp.float32)).astype(x.dtype)

def rope_angles(pos, dim):
    inv = 1.0 / (ROPE_THETA ** (jnp.arange(0, dim, 2, dtype=jnp.float32) / dim))
    ang = pos.astype(jnp.float32)[:, None] * inv[None, :]
    return jnp.cos(ang), jnp.sin(ang)

def apply_rope(x, cos, sin):
    x1, x2 = jnp.split(x, 2, axis=-1)
    c = cos[:, None, :]
    s = sin[:, None, :]
    return jnp.concatenate([x1 * c - x2 * s, x1 * s + x2 * c], axis=-1)

def masked_softmax(s, mask):
    s = jnp.where(mask, s, NEG)
    m = jnp.max(s, axis=-1, keepdims=True)
    e = jnp.where(mask, jnp.exp(s - m), 0.0)
    return e / jnp.maximum(jnp.sum(e, axis=-1, keepdims=True), 1e-30)

def retention(q, k, v, g, gn_w, cos, sin):
    f32 = jnp.float32
    B, S = q.shape[0], q.shape[1]
    H, C = RET_HEADS, RET_CHUNK
    N = S // C
    q = apply_rope(q.astype(f32), cos, sin)
    k = apply_rope(k.astype(f32), cos, sin) * (RET_DK ** -0.5)
    v = v.astype(f32).reshape(B, S, H, RET_DV)
    qc = q.reshape(B, N, C, H, RET_DK).transpose(0, 3, 1, 2, 4)
    kc = k.reshape(B, N, C, H, RET_DK).transpose(0, 3, 1, 2, 4)
    vc = v.reshape(B, N, C, H, RET_DV).transpose(0, 3, 1, 2, 4)
    log_gamma = jnp.log(1.0 - 2.0 ** (-5.0 - jnp.arange(H, dtype=f32)))
    i = jnp.arange(C, dtype=f32)
    diff = i[:, None] - i[None, :]
    decay = jnp.where(diff >= 0, jnp.exp(log_gamma[:, None, None] * jnp.maximum(diff, 0.0)), 0.0)
    scores = jnp.einsum('bhnid,bhnjd->bhnij', qc, kc) * decay[None, :, None]
    o_inner = jnp.einsum('bhnij,bhnje->bhnie', scores, vc)
    zeta = jnp.exp(log_gamma[:, None] * (C - 1.0 - i)[None, :])
    xi = jnp.exp(log_gamma[:, None] * (i + 1.0)[None, :])
    kv = jnp.einsum('bhnjd,bhnje->bhnde', kc * zeta[None, :, None, :, None], vc)
    chunk_decay = jnp.exp(log_gamma * C)[None, :, None, None]

    def step(state, kv_n):
        return state * chunk_decay + kv_n, state

    _, prev = lax.scan(step, jnp.zeros((B, H, RET_DK, RET_DV), f32), kv.transpose(2, 0, 1, 3, 4))
    prev = prev.transpose(1, 2, 0, 3, 4)
    o_cross = jnp.einsum('bhnid,bhnde->bhnie', qc, prev) * xi[None, :, None, :, None]
    o = (o_inner + o_cross).transpose(0, 2, 3, 1, 4).reshape(B, S, H, RET_DV)
    mu = jnp.mean(o, axis=-1, keepdims=True)
    var = jnp.mean(jnp.square(o - mu), axis=-1, keepdims=True)
    o = ((o - mu) * lax.rsqrt(var + GN_EPS)).reshape(B, S, D_RET) * gn_w.astype(f32)
    return jax.nn.silu(g.astype(f32)) * o

def compress(kv, pos_emb, w1, w2):
    B, S, G, D = kv.shape
    n_cmp = (S - CMP_BLOCK) // CMP_STRIDE + 1
    idx = (np.arange(n_cmp)[:, None] * CMP_STRIDE + np.arange(CMP_BLOCK)[None, :]).astype(np.int32)
    blocks = kv[:, idx] + pos_emb.astype(jnp.float32)[None, None, :, None, :]
    flat = blocks.transpose(0, 1, 3, 2, 4).reshape(B, n_cmp, G, CMP_BLOCK * D)
    hid = jax.nn.gelu(flat @ w1.astype(jnp.float32))
    return hid @ w2.astype(jnp.float32)

def nsa(q, k_cmp, v_cmp, k_slc, v_slc, k_win, v_win, gate_logits,
        cmp_k_pos, cmp_k_w1, cmp_k_w2, cmp_v_pos, cmp_v_w1, cmp_v_w2, cos, sin):
    f32 = jnp.float32
    B, S = q.shape[0], q.shape[1]
    G, R, D, QB = NSA_KV_HEADS, NSA_GROUP, NSA_DK, NSA_QBLOCK
    q = apply_rope(q.astype(f32), cos, sin) * (D ** -0.5)
    kc = compress(k_cmp.astype(f32), cmp_k_pos, cmp_k_w1, cmp_k_w2)
    vc = compress(v_cmp.astype(f32), cmp_v_pos, cmp_v_w1, cmp_v_w2)
    n_cmp = kc.shape[1]
    cmp_start = np.arange(n_cmp) * CMP_STRIDE
    cmp_end = (cmp_start + CMP_BLOCK - 1).astype(np.int32)
    ccos, csin = rope_angles(jnp.asarray(cmp_end), D)
    kc = apply_rope(kc, ccos, csin)
    ks = apply_rope(k_slc.astype(f32), cos, sin)
    kw = apply_rope(k_win.astype(f32), cos, sin)
    n_slc = S // SLC_BLOCK
    topk = min(SLC_TOPK, n_slc)
    slc_start = np.arange(n_slc) * SLC_BLOCK
    overlap = ((cmp_start[:, None] < slc_start[None, :] + SLC_BLOCK)
               & (cmp_start[:, None] + CMP_BLOCK > slc_start[None, :])).astype(np.float32)

    qg = q.reshape(B, S, G, R, D).transpose(0, 2, 3, 1, 4)
    kc_g = kc.transpose(0, 2, 1, 3)
    vc_g = vc.transpose(0, 2, 1, 3)
    ks_blk = ks.reshape(B, n_slc, SLC_BLOCK, G, D).transpose(0, 3, 1, 2, 4)
    vs_blk = v_slc.astype(f32).reshape(B, n_slc, SLC_BLOCK, G, D).transpose(0, 3, 1, 2, 4)
    pad = ((0, 0), (0, 0), (WINDOW, 0), (0, 0))
    kw_pad = jnp.pad(kw.transpose(0, 2, 1, 3), pad)
    vw_pad = jnp.pad(v_win.astype(f32).transpose(0, 2, 1, 3), pad)
    nqb = S // QB
    q_blocks = qg.reshape(B, G, R, nqb, QB, D).transpose(3, 0, 1, 2, 4, 5)
    bi = jnp.arange(B)[:, None, None, None]
    gi = jnp.arange(G)[None, :, None, None]
    jsl = jnp.arange(n_slc, dtype=jnp.int32)

    def block_fn(args):
        qb, blk = args
        t = blk * QB + jnp.arange(QB, dtype=jnp.int32)
        valid_c = jnp.asarray(cmp_end)[None, :] <= t[:, None]
        p_cmp = masked_softmax(jnp.einsum('bgrtd,bgnd->bgrtn', qb, kc_g), valid_c)
        o_cmp = jnp.einsum('bgrtn,bgnd->bgrtd', p_cmp, vc_g)
        imp = jnp.einsum('bgrtn,nj->bgtj', p_cmp, overlap)
        qblk = t // SLC_BLOCK
        blk_valid = jsl[None, :] <= qblk[:, None]
        forced = (jsl[None, :] == 0) | (blk_valid & (jsl[None, :] > qblk[:, None] - SLC_LOCAL))
        score = jnp.where(forced, SEL_BIG, jnp.where(blk_valid, imp, -SEL_BIG))
        _, sel = lax.top_k(score, topk)
        kg = ks_blk[bi, gi, sel]
        vg = vs_blk[bi, gi, sel]
        tok = sel[..., None] * SLC_BLOCK + jnp.arange(SLC_BLOCK, dtype=jnp.int32)
        smask = (tok <= t[None, None, :, None, None]).reshape(B, G, 1, QB, topk * SLC_BLOCK)
        s_slc = jnp.einsum('bgrtd,bgtksd->bgrtks', qb, kg).reshape(B, G, R, QB, topk * SLC_BLOCK)
        p_slc = masked_softmax(s_slc, smask).reshape(B, G, R, QB, topk, SLC_BLOCK)
        o_slc = jnp.einsum('bgrtks,bgtksd->bgrtd', p_slc, vg)
        kwb = lax.dynamic_slice_in_dim(kw_pad, blk * QB, WINDOW + QB, axis=2)
        vwb = lax.dynamic_slice_in_dim(vw_pad, blk * QB, WINDOW + QB, axis=2)
        kpos = blk * QB - WINDOW + jnp.arange(WINDOW + QB, dtype=jnp.int32)
        wmask = (kpos[None, :] <= t[:, None]) & (kpos[None, :] > t[:, None] - WINDOW) & (kpos[None, :] >= 0)
        p_win = masked_softmax(jnp.einsum('bgrtd,bgsd->bgrts', qb, kwb), wmask)
        o_win = jnp.einsum('bgrts,bgsd->bgrtd', p_win, vwb)
        return o_cmp, o_slc, o_win

    o_cmp, o_slc, o_win = lax.map(block_fn, (q_blocks, jnp.arange(nqb, dtype=jnp.int32)))

    def to_bshd(o):
        return o.transpose(1, 0, 4, 2, 3, 5).reshape(B, S, NSA_HEADS, D)

    gates = jax.nn.sigmoid(gate_logits.astype(f32)).reshape(B, S, 3, NSA_HEADS)[..., None]
    out = gates[:, :, 0] * to_bshd(o_cmp) + gates[:, :, 1] * to_bshd(o_slc) + gates[:, :, 2] * to_bshd(o_win)
    return out.reshape(B, S, D_NSA)

def conv_ffn(x, w_up, conv_w, w_down):
    u = x @ w_up
    c = u.shape[-1]
    u = lax.conv_general_dilated(u, conv_w[:, None, :].astype(u.dtype), window_strides=(1,),
                                 padding=[(CONV_WIDTH - 1, 0)],
                                 dimension_numbers=('NWC', 'WIO', 'NWC'),
                                 feature_group_count=c)
    gate, val = jnp.split(u, 2, axis=-1)
    return (jax.nn.gelu(gate) * val) @ w_down

def first_inputs(seed: int = 0) -> dict:
    key = jax.random.key(seed)
    ks = jax.random.split(key, 20)
    L = DEPTH

    def nrm(k, shape, scale):
        return jax.random.normal(k, shape, jnp.float32) * scale

    def gain(k, shape):
        return 1.0 + 0.02 * jax.random.normal(k, shape, jnp.float32)

    return {
        'x': nrm(ks[0], (BATCH, SEQ, D_MODEL), 1.0),
        'norm_mix_pre': gain(ks[1], (L, D_MODEL)),
        'w_in': nrm(ks[2], (L, D_MODEL, IN_COLS), D_MODEL ** -0.5),
        'ret_gn_w': gain(ks[3], (L, D_RET)),
        'cmp_k_pos': nrm(ks[4], (L, CMP_BLOCK, NSA_DK), 0.02),
        'cmp_k_w1': nrm(ks[5], (L, CMP_BLOCK * NSA_DK, CMP_HID), (CMP_BLOCK * NSA_DK) ** -0.5),
        'cmp_k_w2': nrm(ks[6], (L, CMP_HID, NSA_DK), CMP_HID ** -0.5),
        'cmp_v_pos': nrm(ks[7], (L, CMP_BLOCK, NSA_DK), 0.02),
        'cmp_v_w1': nrm(ks[8], (L, CMP_BLOCK * NSA_DK, CMP_HID), (CMP_BLOCK * NSA_DK) ** -0.5),
        'cmp_v_w2': nrm(ks[9], (L, CMP_HID, NSA_DK), CMP_HID ** -0.5),
        'w_out': nrm(ks[10], (L, D_MIX, D_MODEL), D_MIX ** -0.5),
        'norm_mix_post': gain(ks[11], (L, D_MODEL)),
        'norm_ffn_pre': gain(ks[12], (L, D_MODEL)),
        'ffn_w_up': nrm(ks[13], (L, D_MODEL, 2 * D_FF), D_MODEL ** -0.5),
        'ffn_conv': nrm(ks[14], (L, CONV_WIDTH, 2 * D_FF), CONV_WIDTH ** -0.5),
        'ffn_w_down': nrm(ks[15], (L, D_FF, D_MODEL), D_FF ** -0.5),
        'norm_ffn_post': gain(ks[16], (L, D_MODEL)),
    }

def first_block(x, norm_mix_pre, w_in, ret_gn_w, cmp_k_pos, cmp_k_w1, cmp_k_w2,
              cmp_v_pos, cmp_v_w1, cmp_v_w2, w_out, norm_mix_post, norm_ffn_pre,
              ffn_w_up, ffn_conv, ffn_w_down, norm_ffn_post):
    B, S, _ = x.shape
    cos, sin = rope_angles(jnp.arange(S, dtype=jnp.int32), NSA_DK)
    split_at = [int(v) for v in np.cumsum(SPLITS)[:-1]]
    for l in range(DEPTH):
        h = rms_norm(x, norm_mix_pre[l])
        proj = h @ w_in[l]
        (rq, rk, rv, rg, nq, kcm, vcm, ksl, vsl, kwn, vwn, ng) = jnp.split(proj, split_at, axis=-1)
        y_ret = retention(rq.reshape(B, S, RET_HEADS, RET_DK), rk.reshape(B, S, RET_HEADS, RET_DK),
                          rv, rg, ret_gn_w[l], cos, sin)
        kv = lambda a: a.reshape(B, S, NSA_KV_HEADS, NSA_DK)
        y_nsa = nsa(nq.reshape(B, S, NSA_HEADS, NSA_DK), kv(kcm), kv(vcm), kv(ksl), kv(vsl), kv(kwn), kv(vwn), ng,
                    cmp_k_pos[l], cmp_k_w1[l], cmp_k_w2[l], cmp_v_pos[l], cmp_v_w1[l], cmp_v_w2[l], cos, sin)
        mix = jnp.concatenate([y_ret, y_nsa], axis=-1).astype(x.dtype) @ w_out[l]
        x = x + rms_norm(mix, norm_mix_post[l])
        h = rms_norm(x, norm_ffn_pre[l])
        x = x + rms_norm(conv_ffn(h, ffn_w_up[l], ffn_conv[l], ffn_w_down[l]), norm_ffn_post[l])
    return x


HGRN_HEADS = 8
HGRN_DK = 128
HGRN_DV = D_MODEL // HGRN_HEADS
HGRN_KEY_WIDTH = HGRN_HEADS * HGRN_DK
HGRN_WIDTH = HGRN_HEADS * HGRN_DV
HGRN_CHUNK = 64

HYENA_WIDTH = D_MODEL
HYENA_SHORT = 3
HYENA_BANDS = 16
HYENA_EMB = 1 + 2 * HYENA_BANDS
HYENA_FILTER_HIDDEN = 64
HYENA_MIN_DECAY = -math.log(1e-2) / 1.5
HYENA_MAX_DECAY = -math.log(1e-2) / 0.3

PEER_HEADS = 8
PEER_NKEYS = 128
PEER_EXPERTS = PEER_NKEYS * PEER_NKEYS
PEER_QDIM = 256
PEER_TOPK = 16
PEER_TOKEN_BLOCK = 128

N_BRANCHES = 2
IN_SPLITS = (HGRN_KEY_WIDTH, 2 * HGRN_KEY_WIDTH, 3 * HGRN_KEY_WIDTH,
             3 * HGRN_KEY_WIDTH + HGRN_WIDTH, 3 * HGRN_KEY_WIDTH + 2 * HGRN_WIDTH,
             3 * HGRN_KEY_WIDTH + 2 * HGRN_WIDTH + 3 * HYENA_WIDTH)
IN_COLS_2 = 3 * HGRN_KEY_WIDTH + 2 * HGRN_WIDTH + 3 * HYENA_WIDTH + N_BRANCHES * D_MODEL
RMS_EPS = 1e-6


def rmsnorm(x, g):
    xf = x.astype(jnp.float32)
    y = xf * lax.rsqrt(jnp.mean(xf * xf, axis=-1, keepdims=True) + RMS_EPS)
    return (y * g.astype(jnp.float32)).astype(x.dtype)

def hgrn2_chunk_scan(q, k, logf, v):
    n, s, h, dk = q.shape
    dv = v.shape[-1]
    nc = s // HGRN_CHUNK

    def to_chunks(a):
        return a.reshape(n, nc, HGRN_CHUNK, h, a.shape[-1]).transpose(1, 0, 3, 2, 4)

    qc, kc, fc, vc = to_chunks(q), to_chunks(k), to_chunks(logf), to_chunks(v)
    incl = jnp.tril(jnp.ones((HGRN_CHUNK, HGRN_CHUNK), dtype=bool))[:, :, None]

    def step(state, inp):
        qb, kb, fb, vb = inp
        b = jnp.cumsum(fb, axis=2)
        b_last = b[:, :, -1:, :]
        inter = jnp.einsum('nhtk,nhkv->nhtv', qb * jnp.exp(b), state)
        diff = b[:, :, :, None, :] - b[:, :, None, :, :]
        decay = jnp.exp(jnp.where(incl, diff, -jnp.inf))
        scores = jnp.einsum('nhtk,nhsk,nhtsk->nhts', qb, kb, decay)
        intra = jnp.einsum('nhts,nhsv->nhtv', scores, vb)
        new_state = (jnp.exp(b_last[:, :, 0, :, None]) * state
                     + jnp.einsum('nhsk,nhsv->nhkv', kb * jnp.exp(b_last - b), vb))
        return new_state, inter + intra

    s0 = jnp.zeros((n, h, dk, dv), jnp.float32)
    _, out = lax.scan(step, s0, (qc, kc, fc, vc))
    return out.transpose(1, 0, 3, 2, 4).reshape(n, s, h, dv)

def centred_short_conv(x, w, b):
    L = x.shape[1]
    pad = HYENA_SHORT // 2
    xp = jnp.pad(x, ((0, 0), (pad, pad), (0, 0)))
    y = b
    for j in range(HYENA_SHORT):
        y = y + xp[:, j:j + L] * w[j]
    return y

def hyena_filters(seq_len, w1, b1, freq1, w2, b2, freq2, w3, decay_rate):
    f32 = jnp.float32
    pos = jnp.arange(seq_len, dtype=f32)
    t = pos / max(seq_len - 1, 1)
    bands = jnp.linspace(1e-4, HYENA_BANDS - 1, HYENA_BANDS, dtype=f32)
    ang = (2.0 * math.pi / seq_len) * pos[:, None] * bands[None, :]
    z = jnp.concatenate([t[:, None], jnp.cos(ang), -jnp.sin(ang)], axis=-1)
    hid = jnp.sin(freq1.astype(f32) * (z @ w1.astype(f32) + b1.astype(f32)))
    hid = jnp.sin(freq2.astype(f32) * (hid @ w2.astype(f32) + b2.astype(f32)))
    filt = (hid @ w3.astype(f32)) * jnp.exp(-t[:, None] * jnp.abs(decay_rate.astype(f32))[None, :])
    return filt[:, :HYENA_WIDTH], filt[:, HYENA_WIDTH:]

def bidirectional_fftconv(u, h_fwd, h_bwd, bias):
    L = u.shape[1]
    kern = jnp.concatenate([h_fwd, jnp.zeros_like(h_fwd[:1]), h_bwd[1:][::-1]], axis=0)
    uf32 = u.astype(jnp.float32)
    uf = jnp.fft.rfft(uf32, n=2 * L, axis=1)
    kf = jnp.fft.rfft(kern, n=2 * L, axis=0)
    y = jnp.fft.irfft(uf * kf[None], n=2 * L, axis=1)[:, :L]
    return (y + uf32 * bias.astype(jnp.float32)).astype(u.dtype)

def hybrid_mixer(xn, w_in, lb, hgrn_norm_g, conv_w, conv_b, filt_w1, filt_b1, filt_freq1,
                 filt_w2, filt_b2, filt_freq2, filt_w3, filt_decay, hyena_bias,
                 w_branch_a, w_branch_b, w_out):
    B, L, _ = xn.shape
    f32 = jnp.float32
    proj = jnp.einsum('bld,dc->blc', xn, w_in)
    q, zf_fwd, zf_bwd, inp, og, hy, gates = jnp.split(proj, IN_SPLITS, axis=-1)

    def heads(a, d):
        return a.astype(f32).reshape(B, L, HGRN_HEADS, d)

    lbh = lb.reshape(HGRN_HEADS, HGRN_DK)

    def forget(z):
        zh = heads(z, HGRN_DK)
        logf = jnp.log(lbh + (1.0 - lbh) * jax.nn.sigmoid(zh))
        k = (1.0 - lbh) * jax.nn.sigmoid(-zh)
        return logf, k

    logf_f, k_f = forget(zf_fwd)
    logf_b, k_b = forget(zf_bwd)
    qh = jax.nn.silu(heads(q, HGRN_DK))
    vh = heads(inp, HGRN_DV)
    rev = lambda a: a[:, ::-1]
    o2 = hgrn2_chunk_scan(jnp.concatenate([qh, rev(qh)], axis=0),
                          jnp.concatenate([k_f, rev(k_b)], axis=0),
                          jnp.concatenate([logf_f, rev(logf_b)], axis=0),
                          jnp.concatenate([vh, rev(vh)], axis=0))
    o = o2[:B] + rev(o2[B:])
    o = rmsnorm(o, hgrn_norm_g).reshape(B, L, HGRN_WIDTH)
    y_a = jnp.einsum('blc,cd->bld', (o * jax.nn.silu(og.astype(f32))).astype(xn.dtype), w_branch_a)

    hy = centred_short_conv(hy, conv_w, conv_b)
    x0, x1, v = jnp.split(hy, 3, axis=-1)
    h_f, h_b = hyena_filters(L, filt_w1, filt_b1, filt_freq1, filt_w2, filt_b2, filt_freq2,
                             filt_w3, filt_decay)
    y_b = x0 * bidirectional_fftconv(v * x1, h_f, h_b, hyena_bias)
    y_b = jnp.einsum('blc,cd->bld', y_b, w_branch_b)

    g_a, g_b = jnp.split(gates, N_BRANCHES, axis=-1)
    merged = jax.nn.sigmoid(g_a) * y_a + jax.nn.sigmoid(g_b) * y_b
    return jnp.einsum('bld,de->ble', merged, w_out)

def peer_ffn(xn, w_q, subkeys, u_tab, v_tab):
    B, L, D = xn.shape
    blocks = xn.reshape(-1, PEER_TOKEN_BLOCK, D)
    sk = subkeys.astype(jnp.float32)

    def block(xb):
        T = xb.shape[0]
        qh = (xb @ w_q).astype(jnp.float32).reshape(T, PEER_HEADS, 2, PEER_QDIM // 2)
        s = jnp.einsum('thpc,hpnc->thpn', qh, sk)
        s1, i1 = lax.top_k(s[:, :, 0], PEER_TOPK)
        s2, i2 = lax.top_k(s[:, :, 1], PEER_TOPK)
        cand_s = (s1[..., :, None] + s2[..., None, :]).reshape(T, PEER_HEADS, PEER_TOPK * PEER_TOPK)
        cand_i = (i1[..., :, None] * PEER_NKEYS + i2[..., None, :]).reshape(T, PEER_HEADS, PEER_TOPK * PEER_TOPK)
        top_s, pos = lax.top_k(cand_s, PEER_TOPK)
        experts = jnp.take_along_axis(cand_i, pos, axis=-1)
        g = jax.nn.softmax(top_s, axis=-1).astype(xb.dtype)
        u = jnp.take(u_tab, experts, axis=0)
        v = jnp.take(v_tab, experts, axis=0)
        act = jax.nn.gelu(jnp.einsum('td,thkd->thk', xb, u)) * g
        return jnp.einsum('thk,thkd->td', act, v)

    return lax.map(block, blocks).reshape(B, L, D)

def second_inputs(seed: int = 0) -> dict:
    key = jax.random.key(seed)
    ks = jax.random.split(key, 26)

    def nrm(k, shape, scale):
        return jax.random.normal(k, shape, jnp.float32) * scale

    decay_base = jnp.linspace(HYENA_MIN_DECAY, HYENA_MAX_DECAY, 2 * HYENA_WIDTH, dtype=jnp.float32)
    return {
        "x": nrm(ks[0], (BATCH, SEQ, D_MODEL), 1.0),
        "norm_mix_g": 1.0 + nrm(ks[1], (DEPTH, D_MODEL), 0.02),
        "w_in": nrm(ks[2], (DEPTH, D_MODEL, IN_COLS_2), D_MODEL ** -0.5),
        "hgrn_lb_logits": nrm(ks[3], (DEPTH + 1, HGRN_KEY_WIDTH), 0.1),
        "hgrn_norm_g": 1.0 + nrm(ks[4], (DEPTH, HGRN_DV), 0.02),
        "hyena_conv_w": nrm(ks[5], (DEPTH, HYENA_SHORT, 3 * HYENA_WIDTH), HYENA_SHORT ** -0.5),
        "hyena_conv_b": nrm(ks[6], (DEPTH, 3 * HYENA_WIDTH), 0.02),
        "filt_w1": nrm(ks[7], (DEPTH, HYENA_EMB, HYENA_FILTER_HIDDEN), HYENA_EMB ** -0.5),
        "filt_b1": nrm(ks[8], (DEPTH, HYENA_FILTER_HIDDEN), 0.1),
        "filt_freq1": 1.0 + nrm(ks[9], (DEPTH, HYENA_FILTER_HIDDEN), 0.02),
        "filt_w2": nrm(ks[10], (DEPTH, HYENA_FILTER_HIDDEN, HYENA_FILTER_HIDDEN), HYENA_FILTER_HIDDEN ** -0.5),
        "filt_b2": nrm(ks[11], (DEPTH, HYENA_FILTER_HIDDEN), 0.1),
        "filt_freq2": 1.0 + nrm(ks[12], (DEPTH, HYENA_FILTER_HIDDEN), 0.02),
        "filt_w3": nrm(ks[13], (DEPTH, HYENA_FILTER_HIDDEN, 2 * HYENA_WIDTH), 0.02 * HYENA_FILTER_HIDDEN ** -0.5),
        "filt_decay": decay_base[None, :] + nrm(ks[14], (DEPTH, 2 * HYENA_WIDTH), 0.1),
        "hyena_bias": nrm(ks[15], (DEPTH, HYENA_WIDTH), 0.1),
        "w_branch_a": nrm(ks[16], (DEPTH, HGRN_WIDTH, D_MODEL), HGRN_WIDTH ** -0.5),
        "w_branch_b": nrm(ks[17], (DEPTH, HYENA_WIDTH, D_MODEL), HYENA_WIDTH ** -0.5),
        "w_out": nrm(ks[18], (DEPTH, D_MODEL, D_MODEL), D_MODEL ** -0.5),
        "norm_ffn_g": 1.0 + nrm(ks[19], (DEPTH, D_MODEL), 0.02),
        "peer_w_q": nrm(ks[20], (DEPTH, D_MODEL, PEER_HEADS * PEER_QDIM), D_MODEL ** -0.5),
        "peer_subkeys": nrm(ks[21], (DEPTH, PEER_HEADS, 2, PEER_NKEYS, PEER_QDIM // 2), (PEER_QDIM // 2) ** -0.5),
        "peer_u": nrm(ks[22], (DEPTH, PEER_EXPERTS, D_MODEL), D_MODEL ** -0.5),
        "peer_v": nrm(ks[23], (DEPTH, PEER_EXPERTS, D_MODEL), 0.2),
        "norm_final_g": 1.0 + nrm(ks[24], (D_MODEL,), 0.02),
    }

def second_block(x, norm_mix_g, w_in, hgrn_lb_logits, hgrn_norm_g, hyena_conv_w, hyena_conv_b,
              filt_w1, filt_b1, filt_freq1, filt_w2, filt_b2, filt_freq2, filt_w3, filt_decay,
              hyena_bias, w_branch_a, w_branch_b, w_out, norm_ffn_g, peer_w_q, peer_subkeys,
              peer_u, peer_v, norm_final_g):
    lb_table = jnp.cumsum(jax.nn.softmax(hgrn_lb_logits.astype(jnp.float32), axis=0), axis=0)
    h = x
    for layer in range(DEPTH):
        h = h + hybrid_mixer(rmsnorm(h, norm_mix_g[layer]), w_in[layer], lb_table[layer],
                             hgrn_norm_g[layer], hyena_conv_w[layer], hyena_conv_b[layer],
                             filt_w1[layer], filt_b1[layer], filt_freq1[layer],
                             filt_w2[layer], filt_b2[layer], filt_freq2[layer],
                             filt_w3[layer], filt_decay[layer], hyena_bias[layer],
                             w_branch_a[layer], w_branch_b[layer], w_out[layer])
        h = h + peer_ffn(rmsnorm(h, norm_ffn_g[layer]), peer_w_q[layer], peer_subkeys[layer],
                         peer_u[layer], peer_v[layer])
    return rmsnorm(h, norm_final_g)


def setup_inputs(seed=0):
    out = dict(first_inputs(seed))
    for name, value in second_inputs(seed + 1).items():
        if name != "x":
            out[name + "_2"] = value
    return out


def reference(
    x, norm_mix_pre, w_in, ret_gn_w, cmp_k_pos, cmp_k_w1, cmp_k_w2, cmp_v_pos, cmp_v_w1,
    cmp_v_w2, w_out, norm_mix_post, norm_ffn_pre, ffn_w_up, ffn_conv, ffn_w_down, norm_ffn_post,
    norm_mix_g_2, w_in_2, hgrn_lb_logits_2, hgrn_norm_g_2, hyena_conv_w_2, hyena_conv_b_2,
    filt_w1_2, filt_b1_2, filt_freq1_2, filt_w2_2, filt_b2_2, filt_freq2_2, filt_w3_2,
    filt_decay_2, hyena_bias_2, w_branch_a_2, w_branch_b_2, w_out_2, norm_ffn_g_2, peer_w_q_2,
    peer_subkeys_2, peer_u_2, peer_v_2, norm_final_g_2,
):
    x = first_block(
        x, norm_mix_pre, w_in, ret_gn_w, cmp_k_pos, cmp_k_w1, cmp_k_w2, cmp_v_pos, cmp_v_w1,
        cmp_v_w2, w_out, norm_mix_post, norm_ffn_pre, ffn_w_up, ffn_conv, ffn_w_down,
        norm_ffn_post,
    )
    return second_block(
        x, norm_mix_g_2, w_in_2, hgrn_lb_logits_2, hgrn_norm_g_2, hyena_conv_w_2,
        hyena_conv_b_2, filt_w1_2, filt_b1_2, filt_freq1_2, filt_w2_2, filt_b2_2, filt_freq2_2,
        filt_w3_2, filt_decay_2, hyena_bias_2, w_branch_a_2, w_branch_b_2, w_out_2,
        norm_ffn_g_2, peer_w_q_2, peer_subkeys_2, peer_u_2, peer_v_2, norm_final_g_2,
    )


_drawn_inputs = setup_inputs


def setup_inputs(seed=0):
    import zlib

    import numpy as np

    out = dict(_drawn_inputs(seed))
    spreads = {}
    factors = {'ret_gn_w': 3.49,
     'cmp_k_pos': 46.385,
     'cmp_v_pos': 5.25,
     'norm_mix_post': 3.033,
     'norm_ffn_pre': 3.095,
     'norm_ffn_post': 4.147,
     'norm_mix_g_2': 7.52,
     'hgrn_lb_logits_2': 8.0,
     'hgrn_norm_g_2': 41.799,
     'hyena_conv_b_2': 31.188,
     'filt_w1_2': 3.268,
     'filt_b1_2': 8.0,
     'filt_freq1_2': 8.0,
     'filt_w2_2': 3.158,
     'filt_b2_2': 8.0,
     'filt_freq2_2': 8.0,
     'filt_w3_2': 2.987,
     'filt_decay_2': 8.0,
     'norm_ffn_g_2': 50.008,
     'norm_final_g_2': 22.667}
    for name, (base, spread) in spreads.items():
        noise = np.random.default_rng([zlib.crc32(name.encode()), seed]).standard_normal(out[name].shape)
        drawn = base * np.exp(spread * noise) if base else spread * noise
        out[name] = __import__('jax').numpy.asarray(drawn.astype(out[name].dtype))
    for name, factor in factors.items():
        out[name] = (out[name] * factor).astype(out[name].dtype)
    return out
```

```python
import concourse.bass as bass
from concourse import mybir
from contextlib import ExitStack

SEQ = 256
D = 1024
TOK = 2
KC = D // 128
NCMP = (SEQ - 32) // 16 + 1
RING = 6
SLOT = 2048
NSLOT = 240
W_IN, W_CMP, W_OUT, W_FFN, W_HY, W_GB, W_QZ, W_V, W_OG, W_GA, W_BB, W_BA, W_OUT2, W_Q, W_PEER = (
    0, 11, 15, 19, 52, 64, 68, 80, 84, 88, 92, 96, 100, 104, 112)
NJ = 128
NFF = 22
V_NORM, V_CONV, V_HYW, V_HYB, V_LB, V_GN = 0, 32, 164, 236, 260, 276
T_COS, T_SIN, T_DECAY, T_CAUSAL, T_KEEP, T_DROP, T_CC = 0, 64, 128, 1664, 1920, 1950, 1980
INV_2PI = 0.15915494309189535
ROUND = 12582912.0
PI2_A, PI2_B, PI2_C = 6.28125, 0.0019350051879882812, 3.019915981956e-07
SIN_MAX = 3.1415925

SEMS = """x_loaded consts_loaded cmps_loaded tab_loaded filt_loaded w3_loaded dft_loaded rows_loaded bias_loaded
 gnw_loaded levels_loaded iota_loaded sk_loaded out_stored slot_multiplied act_step dve_step pool_step
 squares_summed inv_ready rstd_ready xn_ready xn_transposed hT_act hT_dve filt_hidden filt_sine filt_window
 filt_product filt_ab kernel_spectrum p1_act p1_dve gates_product gates_ready rope_ready heads_transposed
 heads_act heads_dve silu_ready dup_ready dup_transposed blocks_ready hid_ready cmp_product vc_copied kc_ready
 fdecay_loaded filt_windowed filt_reduced spectrum_copied cmp_shifted gn_inv gn_rstd ret_normed att_rowmax
 ffn_tap ret_scores ret_decayed ret_out cmp_scores cmp_exp cmp_probs cmp_ptrans cmp_pcopied cmp_out cmp_done
 att_scores att_max att_exp att_transposed att_copied_act att_copied_dve att_out att_done mix_transposed
 mixT_act mixT_dve post_squares post_inv post_rstd post_done wrow_free ffn_gated ffn_conv_act ffn_conv_dve
 ffn_gelu""".split()


SEMS2 = """x_final ones_ready yb_ready scanned level_eq level_ek level_exp level_ready level_product level_act level_dve
 h_ready wq_taken ba_taken bb_taken channels_taken hy_dve hy_act hy_tap u_ready u_transposed ut_act ut_dve
 u_spectrum u_spectrum_copied v_copied y_spectrum y_product o_product o_copied o_squared o_sums o_ready
 o_inverse o_rstd merged_ready mixer_added sim_product sim_copied routes_ready routes_transposed routes_copied
 routes_shifted routes_exp onehots onehot_j gate_product gated pt_act pt_dve pt_transposed peer_added
 lb_shifted lb_exp lb_ready logs_ready keys_ready db_start gates2_ready""".split()


def build(nc, dram):
    fp32 = mybir.dt.float32
    u32 = mybir.dt.uint32
    ALU = mybir.AluOpType
    ACT = mybir.ActivationFunctionType
    AX = mybir.AxisListType.X
    V, A, P = nc.vector, nc.scalar, nc.gpsimd

    ctx = ExitStack()
    with ctx:
        def sb(name, shape, dt=fp32):
            return ctx.enter_context(nc.sbuf_tensor(name, shape, dt))

        S = {name: ctx.enter_context(nc.semaphore(name)) for name in SEMS + SEMS2}
        arrived = [ctx.enter_context(nc.semaphore(f"slot_arrived_{n}")) for n in range(RING)]

        ring = sb("ring", [128, RING, SLOT])
        big = sb("big", [128, 32768])
        x = sb("x", [128, TOK, D])
        hT = sb("hT", [128, KC, SEQ])
        ident = sb("identity", [128, 128])
        wrow = sb("wrow", [128, D])
        vecs = sb("vecs", [128, 277])
        aux = sb("aux", [128, 2300])
        stat = sb("stat", [128, 192])
        ps = ctx.enter_context(nc.psum_tensor("ps", [128, 8, 512], fp32))

        def area(off, *dims):
            n = 1
            for d in dims:
                n *= d
            v = big[:, off:off + n]
            if len(dims) == 2:
                v = v.rearrange("p (a b) -> p a b", a=dims[0])
            if len(dims) == 3:
                v = v.rearrange("p (a b c) -> p a b c", a=dims[0], b=dims[1])
            if len(dims) == 4:
                v = v.rearrange("p (a b c d) -> p a b c d", a=dims[0], b=dims[1], c=dims[2])
            return v

        KR, KI = area(0, 2, D), area(2048, 2, D)
        P1 = area(4096, TOK, 2840)
        RT = area(9776, 20, SEQ)
        R = area(14896, TOK, 20, 64)
        RA, RB = area(17456, 20, 32), area(18096, 20, 32)
        RC, RD = area(18736, 20, 32), area(19376, 20, 32)
        xn = area(20016, TOK, D)
        SCR = 22064
        FH = area(SCR, TOK, 2048)
        FW = area(SCR + 4096, TOK, 2048)
        FAB = area(SCR + 4096, 2, TOK, D)
        DF1 = area(SCR + 8192, 4, 256)
        DUP = area(SCR, TOK, 4, 2, 64)
        BLK = area(SCR + 1024, 2, 16, 30)
        HID = area(SCR + 1984, 2, 2, 30)
        KCR = area(SCR + 2104, 30)
        KCT = area(SCR + 2134, 30)
        VC = area(SCR + 2164, 2, 64)
        SD = area(SCR + 2304, 4, 384)
        SM = area(SCR + 3840, 2, 4, 256)
        ET = area(SCR + 5888, 2, 1024)
        CE = area(SCR + 7936, TOK, 8, NCMP)
        CET = area(SCR + 8176, TOK * 8 * 128)
        mix = area(14896, TOK, D)
        mixT = area(17456, KC, SEQ)
        gn = area(20016, TOK * 4, 128)
        gn2 = area(17456, TOK * 4, 128)
        cosT = aux[:, T_COS:T_COS + 64].rearrange("p (t c) -> p t c", t=2)
        sinT = aux[:, T_SIN:T_SIN + 64].rearrange("p (t c) -> p t c", t=2)
        decay = aux[:, T_DECAY:T_DECAY + 1536].rearrange("p (h c) -> p h c", h=4)
        keep = aux[:, T_KEEP:T_KEEP + 30].rearrange("p (t c) -> p t c", t=2)
        drop = aux[:, T_DROP:T_DROP + 30].rearrange("p (t c) -> p t c", t=2)
        cmps = area(SCR + 8192, 608)
        w2k = cmps[:, 32:160].rearrange("p (h c) -> p h c", h=2)
        w2r = cmps[:, 160:288].rearrange("p (h c) -> p h c", h=2)
        w2v = cmps[:, 288:416].rearrange("p (h c) -> p h c", h=2)
        wng = cmps[:, 416:608].rearrange("p (k c) -> p k c", k=8)
        ZT = area(SCR + 9216, 258)
        FT = area(SCR + 9474, 132)
        FHID = area(SCR + 9606, 2, 256)
        FTMP = area(SCR + 10118, 2, 256)
        W3 = area(9776, 2048)
        gnw = area(21040, 512)
        ST_SQ, ST_INV, ST_RSTD = 0, 2, 4
        ST_GSUM, ST_GMEAN, ST_GVAR, ST_GRSTD = 8, 16, 24, 32
        ST_CMAX, ST_CSUM, ST_CREC, ST_MAX, ST_NMAX, ST_SUM, ST_REC = 40, 56, 72, 88, 96, 104, 136
        CONV = area(SCR, 3, 2, 256)
        HACT = area(SCR + 1536, 4, 256)
        
        def dve_copies(u):
            return 2 * (u // 4) + max(0, u % 4 - 2)

        def Z(n, *dims):
            return area(2048 * n, *dims)

        lbs = sb("lower_bounds", [128, 40])
        LBE, LBM, LB, OML = lbs[:, 0:16].rearrange("p (c r) -> p c r", r=2), lbs[:, 16:24], lbs[:, 24:32], lbs[:, 32:40]
        levels = aux[:, 0:1024].rearrange("p (l c) -> p l c", l=8)
        ones_row, ones = aux[:, 1024:1280], aux[:, 1280:1408]
        XH = Z(2, 24, SEQ)
        X0, X1, U = Z(2, 8 * SEQ), Z(3, 8 * SEQ), Z(4, 8 * SEQ)
        UC = Z(4, 8, SEQ)
        UT = Z(3, TOK, D)
        UR, UI, YT = Z(5, 2 * D), Z(6, 2 * D), Z(7, 2 * D)
        YR, YI = Z(4, 2, D), Z(3, 2, D)
        DFT = Z(15, 8, SEQ)
        YB = Z(5, 8, SEQ)
        MERGED = Z(6, 8, SEQ)
        GB, Q, KF, KB = Z(8, 8, SEQ), Z(9, 8, SEQ), Z(10, 8, SEQ), Z(11, 8, SEQ)
        VT = Z(12, TOK, D)
        LF, LBW = Z(13, 8, SEQ), Z(14, 8, SEQ)
        OG, GA = Z(13, 8, SEQ), Z(14, 8, SEQ)
        BF, DB = Z(0, 8, SEQ), Z(1, 8, SEQ)
        LV = [Z(2, 2, 1024), Z(3, 2, 1024)]
        AT = [Z(15, 4, 2, SEQ), Z(7, 4, 2, SEQ)]
        OT = Z(4, 8, SEQ)
        SQ, RS = Z(2, 8, SEQ), Z(3, 8, SEQ)
        BTMP = Z(7, 2, 512)
        NLV = 18

        def taken(idx):
            for first, name, per in ((52, "h_ready", 1), (44, "wq_taken", 1), (40, "ba_taken", 1), (36, "bb_taken", 1),
                                     (12, "channels_taken", 1), (0, "hy_dve", 2)):
                if idx >= first:
                    return S[name], per * (idx - first + 1)

        def slot_of(idx):
            return idx + (W_HY if idx < 28 else W_OG - 28 if idx < 44 else W_Q - 44)

        def level_view(a, hg, m):
            f = a.rearrange("p h t -> p (h t)")[:, hg * 1024:(hg + 1) * 1024]
            return f.rearrange("p (n two m) -> p n two m", two=2, m=m)

        def split_view(f, m):
            return f.rearrange("p (n two m) -> p n two m", two=2, m=m)

        def level_dve(n):
            return n - n // 9

        H = area(0, NJ, SEQ)
        QT = Z(8, 16, SEQ)
        SK = Z(10, 2048)
        SC = Z(11, TOK, 16, 128)
        CS = Z(13, TOK, 8, 256)
        EQ = Z(15, 2048)
        T1V = aux[:, 0:512].rearrange("p (t g k) -> p t g k", t=2, g=16)
        T1I = aux[:, 512:1024].bitcast(u32).rearrange("p (t g k) -> p t g k", t=2, g=16)
        T1F = wrow[:, 0:512].rearrange("p (t g k) -> p t g k", t=2, g=16)
        TV = aux[:, 1024:1280].rearrange("p (g k) -> p g k", g=16)
        TP = aux[:, 1280:1536].bitcast(u32).rearrange("p (g k) -> p g k", g=16)
        PA = aux[:, 1536:2048].rearrange("p (s g) -> p s g", s=2)
        PAI = EQ[:, 0:512].bitcast(u32).rearrange("p (s g) -> p s g", s=2)
        iota = aux[:, 2048:2176]
        IX = wrow[:, 512:1024].rearrange("p (s t g) -> p s t g", s=2, t=2)
        ROUTE = wrow[:, 0:768].rearrange("p (s t) -> p s t", s=3)
        OA = aux[:, 0:1024].rearrange("p (b t i) -> p b t i", b=2, t=4)
        OB = aux[:, 1024:1536].rearrange("p (b t j) -> p b t j", b=2, t=4)
        PT = area(0, KC, SEQ)

        def pool_second(pool):
            pool.dma_start(aux[:, 0:1024], dram["levels"]).then_inc(S["levels_loaded"], 16)
            pool.dma_start(DFT.rearrange("p a b -> p (a b)"), dram["dft"]).then_inc(S["dft_loaded"], 16)
            P.memset(aux[:, 1024:1408], 1.0).then_inc(S["ones_ready"], 1)
            pool.wait_ge(S["yb_ready"], 1)
            pool.wait_ge(S["scanned"], 16)
            for n in range(NLV):
                hg, m = n // 9, 128 >> (n % 9)
                if n % 9 == 8:
                    continue
                if n >= 2:
                    pool.wait_ge(S["level_product"], n - 1)
                v = split_view(LV[n % 2][:, 1, :], m)
                f, d = level_view(BF, hg, m), level_view(DB, hg, m)
                nb = 512 // m
                P.tensor_tensor(v[:, :, 0, :], d[:, :, 1, 0:1].broadcast_to([128, nb, m]), d[:, :, 0, :],
                                ALU.subtract).then_inc(S["level_eq"], 1)
                P.tensor_tensor(v[:, :, 1, :], f[:, :, 1, :], f[:, :, 0, m - 1:m].broadcast_to([128, nb, m]),
                                ALU.subtract).then_inc(S["level_eq"], 1)
            pool.wait_ge(S["xn_transposed"], 16)
            pool.dma_start(SK, dram["subkeys"]).then_inc(S["sk_loaded"], 16)
            pool.dma_start(iota, dram["iota"]).then_inc(S["iota_loaded"], 16)
            pool.wait_ge(S["gated"], 128)
            pool.dma_start(wrow[:, :], dram["final"]).then_inc(S["rows_loaded"], 16)

        def pe_second(pe, slot, norm_transposes, wait_hT, token_product, out_product):
            def channels(idx, it=None, src=hT):
                w = slot(slot_of(idx), it)
                if idx >= 3:
                    sem, value = taken(idx - 3)
                    pe.wait_ge(sem, at(value, 6, it))
                for j in range(2):
                    for k in range(KC):
                        last = mm(ps[:, idx % 3, j * 256:(j + 1) * 256], w[:, (j * 8 + k) * 128:(j * 8 + k + 1) * 128],
                                  src[:, k, :], k == 0, k == KC - 1)
                last.then_inc(S["slot_multiplied"], 1)

            norm_transposes(2)
            wait_hT(2)
            for idx in range(6):
                channels(idx)
            for idx in range(6, 12):
                channels(idx)
            for idx in range(12, 16):
                channels(idx)
            pe.wait_ge(S["u_ready"], 1)
            for t in range(TOK):
                for c in range(KC):
                    last = nc.tensor.transpose(ps[:, 4 + 2 * t + c // 4, (c % 4) * 128:(c % 4 + 1) * 128],
                                               UC[:, c, t * 128:(t + 1) * 128], ident[:, :])
                last.then_inc(S["u_transposed"], 1)
            for idx in range(16, 20):
                channels(idx)
            pe.wait_ge(S["ut_act"], 1)
            pe.wait_ge(S["ut_dve"], 1)
            pe.wait_ge(S["dft_loaded"], 32)
            for part in range(2):
                if part:
                    pe.wait_ge(S["u_spectrum_copied"], 1)
                for ft in range(2):
                    for nh in range(2):
                        for t in range(TOK):
                            last = mm(ps[:, 4 + ft * 2 + nh, :], DFT[:, part * 2 + t, ft * 128:(ft + 1) * 128],
                                      UT[:, t, nh * 512:(nh + 1) * 512], t == 0, t == 1)
                last.then_inc(S["u_spectrum"], 1)
                for idx in range(20 + 2 * part, 22 + 2 * part):
                    channels(idx)
            for idx in range(24, 28):
                channels(idx)
            pe.wait_ge(S["u_spectrum_copied"], 2)
            token_product(W_V, 4, hT)
            token_product(W_V + 2, 6, hT)
            pe.wait_ge(S["v_copied"], 4)
            pe.wait_ge(S["y_spectrum"], 2)
            for c in range(KC):
                for n, (y, ft) in enumerate(((YR, 0), (YR, 1), (YI, 0), (YI, 1))):
                    last = mm(ps[:, 4 + c // 2, (c % 2) * 256:(c % 2 + 1) * 256], y[:, ft, c * 128:(c + 1) * 128],
                              DFT[:, 4 + n, :], n == 0, n == 3)
            last.then_inc(S["y_product"], 1)
            pe.wait_ge(S["yb_ready"], 1)

            def level(n):
                hg = n // 9
                pe.wait_ge(S["level_ready"], n + 1)
                if n >= 2:
                    if (n - 2) % 9 == 0:
                        pe.wait_ge(S["level_act"], (n - 2) // 9 + 1)
                    else:
                        pe.wait_ge(S["level_dve"], level_dve(n - 2))
                for st in range(2):
                    tt = st if n % 9 else 1 - st
                    for h in range(4):
                        keys = LV[n % 2][:, 0, h * 256 + st * 128:h * 256 + st * 128 + 128]
                        if n % 9 == 8:
                            queries = Q[:, 4 * hg + h, tt * 128:(tt + 1) * 128]
                        else:
                            queries = LV[n % 2][:, 1, h * 256 + tt * 128:h * 256 + tt * 128 + 128]
                        last = mm(ps[:, 4 + 2 * (n % 2) + st, h * 128:(h + 1) * 128], keys, queries)
                last.then_inc(S["level_product"], 1)

            def values(hg):
                if hg == 0:
                    pe.wait_ge(S["level_act"], 1)
                    pe.wait_ge(S["level_dve"], 8)
                else:
                    pe.wait_ge(S["level_act"], 2)
                    pe.wait_ge(S["level_dve"], 16)
                for pair in range(2):
                    if hg or pair:
                        pe.wait_ge(S["o_copied"], 2 * hg + pair)
                    for hh in range(2):
                        h = 2 * pair + hh
                        for st in range(2):
                            last = mm(ps[:, 3, hh * 256:(hh + 1) * 256], VT[:, st, (4 * hg + h) * 128:(4 * hg + h + 1) * 128],
                                      AT[hg][:, h, st, :], st == 0, st == 1)
                    last.then_inc(S["o_product"], 1)

            idx = 28
            for n in range(NLV):
                level(n)
                if n % 3 != 2:
                    channels(idx, src=YB if idx >= 36 else hT)
                    idx += 1
                if n == 11:
                    values(0)
            values(1)
            pe.wait_ge(S["o_squared"], 1)
            pe.wait_ge(S["level_dve"], 16)
            for h in range(8):
                last = mm(ps[:, 4 + h // 2, (h % 2) * 256:(h % 2 + 1) * 256], ones, SQ[:, h, :])
            last.then_inc(S["o_sums"], 1)
            pe.wait_ge(S["o_ready"], 1)
            for idx in range(40, 44):
                channels(idx, src=OT)
            pe.wait_ge(S["merged_ready"], 4)
            out_product(W_OUT2, MERGED)
            norm_transposes(3)
            wait_hT(3)
            for idx in range(44, 52):
                channels(idx)
            pe.wait_ge(S["wq_taken"], 8)
            pe.wait_ge(S["sk_loaded"], 16)
            for t in range(TOK):
                if t:
                    pe.wait_ge(S["sim_copied"], 1)
                for g in range(16):
                    last = mm(ps[:, 4 + g // 4, (g % 4) * 128:(g % 4 + 1) * 128], QT[:, g, t * 128:(t + 1) * 128],
                              SK[:, g * 128:(g + 1) * 128])
                last.then_inc(S["sim_product"], 1)
            def experts(s, it=None):
                channels(52 + s, it)

            for s in range(8):
                experts(s)
            with pe.Fori(0, 4) as it:
                for s in range(8, 14):
                    experts(s, it)
            pe.wait_ge(S["routes_ready"], 1)
            pe.wait_ge(S["sim_copied"], 2)
            for t in range(TOK):
                nc.tensor.transpose(ps[:, 4, t * 128:(t + 1) * 128], IX[:, 0, t, :], ident[:, :])
                nc.tensor.transpose(ps[:, 4, 256 + t * 128:256 + (t + 1) * 128], IX[:, 1, t, :], ident[:, :])
                last = nc.tensor.transpose(ps[:, 5, t * 128:(t + 1) * 128],
                                           TV[:, 8 * t:8 * t + 8, :].rearrange("p g k -> p (g k)"), ident[:, :])
            last.then_inc(S["routes_transposed"], 1)
            pe.wait_ge(S["routes_copied"], 2)

            def gates(q, parity, bank, it=None):
                pe.wait_ge(S["onehots"], at(q + 1, 12, it))
                if q >= 2:
                    pe.wait_ge(S["gated"], at(q - 1, 12, it))
                for tk in range(4):
                    last = mm(ps[:, bank, tk * 64:(tk + 1) * 64], OA[:, parity, tk, :], OB[:, parity, tk, :])
                last.then_inc(S["gate_product"], 1)

            for s in range(2):
                experts(32 + s)
                for e in range(2):
                    gates(2 * s + e, e, 3 + e)
            with pe.Fori(0, 5) as it:
                for s in range(2, 8):
                    experts(32 + s, it)
                    for e in range(2):
                        gates(2 * s + e, e, 3 + e, it)

            def down(s, it=None):
                w = slot(W_PEER + 64 + s, it)
                for jj in range(2):
                    j = at(2 * s + jj, 12, it)
                    for c in range(KC):
                        first = s == 0 and jj == 0 and it is None
                        last = mm(ps[:, 4 + c // 2, (c % 2) * 256:(c % 2 + 1) * 256],
                                  w[:, jj * 1024 + c * 128:jj * 1024 + (c + 1) * 128], H[:, j, :],
                                  first and c % 2 == 0, s == 63 and jj == 1)
                last.then_inc(S["slot_multiplied"], 1)

            pe.wait_ge(S["gated"], 64)
            pe.wait_ge(S["h_ready"], 64)
            for s in range(2):
                down(s)
                for e in range(2):
                    gates(64 + 2 * s + e, e, e)
            with pe.Fori(0, 5) as it:
                for s in range(2, 8):
                    down(s, it)
                    for e in range(2):
                        gates(64 + 2 * s + e, e, e, it)
            pe.wait_ge(S["gated"], 128)
            with pe.Fori(0, 5) as it:
                for s in range(32, 38):
                    down(s, it)
            down(62)
            down(63)
            pe.wait_ge(S["pt_act"], 1)
            pe.wait_ge(S["pt_dve"], 1)
            for t in range(TOK):
                for c in range(KC):
                    last = nc.tensor.transpose(ps[:, 2 * t + c // 4, (c % 4) * 128:(c % 4 + 1) * 128],
                                               PT[:, c, t * 128:(t + 1) * 128], ident[:, :])
                last.then_inc(S["pt_transposed"], 1)

        def act_second(act, norm_act):
            act.wait_ge(S["lb_shifted"], 1)
            A.activation(LBE, LBE, ACT.Exp).then_inc(S["lb_exp"], 1)
            norm_act(2)

            def hyena(s):
                act.wait_ge(S["slot_multiplied"], slot_of(s) + 1)
                for j in range(2):
                    c = 2 * s + j
                    A.activation(XH[:, c, :], ps[:, s % 3, j * 256:(j + 1) * 256], ACT.Identity,
                                 bias=vecs[:, V_HYB + c:V_HYB + c + 1],
                                 scale=vecs[:, V_HYW + 3 * c + 1:V_HYW + 3 * c + 2]).then_inc(S["hy_act"], 1)

            for s in range(12):
                hyena(s)

            def take(idx, dst, func, second=None):
                act.wait_ge(S["slot_multiplied"], slot_of(idx) + 1)
                src = ps[:, idx % 3, :]
                s = 2 * (idx % 4)
                if second is not None:
                    A.activation(second[:, s:s + 2, :].rearrange("p a b -> p (a b)"), src, func, scale=-1.0)
                A.activation(dst[:, s:s + 2, :].rearrange("p a b -> p (a b)"), src, func).then_inc(S["channels_taken"], 1)

            for idx in range(12, 16):
                take(idx, GB, ACT.Sigmoid)
            act.wait_ge(S["u_transposed"], 1)
            act.wait_ge(S["u_transposed"], 2)
            A.copy(UT[:, 0, :], ps[:, 4:6, :].rearrange("p a b -> p (a b)")).then_inc(S["ut_act"], 1)
            for idx in range(16, 20):
                take(idx, Q, ACT.Silu)
            act.wait_ge(S["u_spectrum"], 1)
            A.copy(UR, ps[:, 4:8, :].rearrange("p a b -> p (a b)")).then_inc(S["u_spectrum_copied"], 1)
            take(20, LF, ACT.Sigmoid, KF)
            take(21, LF, ACT.Sigmoid, KF)
            act.wait_ge(S["u_spectrum"], 2)
            A.mul(UI, ps[:, 4:8, :].rearrange("p a b -> p (a b)"), -1.0).then_inc(S["u_spectrum_copied"], 1)
            take(22, LF, ACT.Sigmoid, KF)
            take(23, LF, ACT.Sigmoid, KF)
            for idx in range(24, 28):
                take(idx, LBW, ACT.Sigmoid, KB)
            act.wait_ge(S["lb_ready"], 1)
            act.wait_ge(S["channels_taken"], 16)
            for logs in (LF, LBW):
                for c in range(8):
                    A.activation(logs[:, c, :], logs[:, c, :], ACT.Ln, bias=LB[:, c:c + 1],
                                 scale=OML[:, c:c + 1]).then_inc(S["logs_ready"], 1)
            for g in range(2):
                act.wait_ge(S["slot_multiplied"], W_V + 2 * g + 2)
                for t in range(TOK):
                    A.copy(VT[:, t, g * 512:(g + 1) * 512], ps[:, 4 + 2 * g + t, :]).then_inc(S["v_copied"], 1)
            idx = 28
            for n in range(NLV):
                if n % 9 != 8:
                    act.wait_ge(S["level_ek"], 2 * (n - n // 9) + 2)
                    act.wait_ge(S["level_eq"], 2 * (n - n // 9) + 2)
                    lv = LV[n % 2].rearrange("p a b -> p (a b)")
                    A.activation(lv, lv, ACT.Exp).then_inc(S["level_exp"], 1)
                if n % 9 == 1:
                    hg = n // 9
                    act.wait_ge(S["level_product"], n)
                    if hg == 0:
                        act.wait_ge(S["scanned"], 16)
                    b = 4 + 2 * ((n - 1) % 2)
                    for st in range(2):
                        ins = A.copy(AT[hg][:, :, st, (1 - st) * 128:(2 - st) * 128],
                                     ps[:, b + st, :].rearrange("p (h c) -> p h c", h=4))
                    ins.then_inc(S["level_act"], 1)
                if n >= 1 and (n - 1) % 3 != 2 and idx < 36:
                    if idx == 28:
                        act.wait_ge(S["scanned"], 16)
                    take(idx, OG if idx < 32 else GA, ACT.Copy)
                    idx += 1
                if n == 13:
                    for pair in range(2):
                        act.wait_ge(S["o_product"], pair + 1)
                        A.copy(OT[:, 2 * pair:2 * pair + 2, :].rearrange("p a b -> p (a b)"),
                               ps[:, 3, :]).then_inc(S["o_copied"], 1)
            act.wait_ge(S["channels_taken"], 24)
            A.activation(GA, GA, ACT.Sigmoid).then_inc(S["gates2_ready"], 1)
            A.activation(OG, OG, ACT.Silu).then_inc(S["gates2_ready"], 1)
            for pair in range(2, 4):
                act.wait_ge(S["o_product"], pair + 1)
                A.copy(OT[:, 2 * pair:2 * pair + 2, :].rearrange("p a b -> p (a b)"), ps[:, 3, :]).then_inc(S["o_copied"], 1)
            act.wait_ge(S["o_copied"], 4)
            act.wait_ge(S["level_product"], NLV)
            A.activation(SQ, OT, ACT.Square).then_inc(S["o_squared"], 1)
            act.wait_ge(S["o_inverse"], 1)
            A.activation(RS, RS, ACT.Sqrt).then_inc(S["o_rstd"], 1)
            act.wait_ge(S["mixer_added"], 2)
            norm_act(3)
            for s in range(8):
                act.wait_ge(S["slot_multiplied"], W_Q + s + 1)
                A.copy(QT[:, 2 * s:2 * s + 2, :].rearrange("p a b -> p (a b)"), ps[:, (44 + s) % 3, :]).then_inc(S["wq_taken"], 1)
            for t in range(TOK):
                act.wait_ge(S["sim_product"], t + 1)
                A.copy(SC[:, t].rearrange("p a b -> p (a b)"), ps[:, 4:8, :].rearrange("p a b -> p (a b)")).then_inc(S["sim_copied"], 1)

            def activations(s, it=None):
                act.wait_ge(S["slot_multiplied"], at(W_PEER + s + 1, 6, it))
                j = at(2 * s, 12, it)
                A.activation(H[:, bass.ds(j, 2), :].rearrange("p a b -> p (a b)"), ps[:, (52 + s) % 3, :],
                             ACT.Gelu_apprx_tanh).then_inc(S["h_ready"], 1)

            for s in range(8):
                activations(s)
            with act.Fori(0, 4) as it:
                for s in range(8, 14):
                    activations(s, it)
            act.wait_ge(S["routes_shifted"], 1)
            A.activation(TV, TV, ACT.Exp).then_inc(S["routes_exp"], 1)
            act.wait_ge(S["routes_transposed"], 1)
            A.copy(wrow[:, 0:512], ps[:, 4, :]).then_inc(S["routes_copied"], 1)
            A.copy(wrow[:, 512:768], ps[:, 5, 0:256]).then_inc(S["routes_copied"], 1)
            for s in range(32, 34):
                activations(s)
            with act.Fori(0, 5) as it:
                for s in range(34, 40):
                    activations(s, it)
            act.wait_ge(S["slot_multiplied"], NSLOT)
            A.copy(PT[:, 0:4, :].rearrange("p a b -> p (a b)"), ps[:, 4:6, :].rearrange("p a b -> p (a b)")).then_inc(S["pt_act"], 1)
            act.wait_ge(S["peer_added"], 2)
            junk = area(4096, TOK, D)
            for t in range(TOK):
                A.activation(junk[:, t, :], x[:, t, :], ACT.Square,
                             accum_out=stat[:, ST_SQ + t:ST_SQ + t + 1]).then_inc(S["squares_summed"], 1)
            act.wait_ge(S["inv_ready"], 5)
            A.activation(stat[:, ST_RSTD:ST_RSTD + 2], stat[:, ST_INV:ST_INV + 2], ACT.Sqrt).then_inc(S["rstd_ready"], 1)

        def dve_second(dve, step, inverse, norm_dve):
            logits = vecs[:, V_LB:V_LB + 16].rearrange("p (c r) -> p c r", r=2)
            step(V.tensor_tensor(LBM, logits[:, :, 0], logits[:, :, 1], ALU.max))
            V.tensor_tensor(LBE, logits, LBM.unsqueeze(2).broadcast_to([128, 8, 2]), ALU.subtract).then_inc(S["lb_shifted"], 1)
            dve.wait_ge(S["lb_exp"], 1)
            step(V.tensor_tensor(LBM, LBE[:, :, 0], LBE[:, :, 1], ALU.add))
            step(V.reciprocal(LBM, LBM))
            step(V.tensor_tensor(LB, LBE[:, :, 0], LBM, ALU.mult))
            V.tensor_scalar(OML, LB, -1.0, 1.0, ALU.mult, ALU.add).then_inc(S["lb_ready"], 1)
            norm_dve(2)
            for s in range(12):
                dve.wait_ge(S["hy_act"], 2 * s + 2)
                for tap, sem in ((0, "hy_tap"), (2, "hy_dve")):
                    for j in range(2):
                        c = 2 * s + j
                        if tap:
                            dve.wait_ge(S["hy_tap"], 2 * s + j + 1)
                        lo, hi = (1, 0) if tap == 0 else (0, 1)
                        y = XH[:, c, lo:lo + 255]
                        V.scalar_tensor_tensor(y, ps[:, s % 3, j * 256 + hi:j * 256 + hi + 255],
                                               vecs[:, V_HYW + 3 * c + tap:V_HYW + 3 * c + tap + 1], y,
                                               ALU.mult, ALU.add).then_inc(S[sem], 1)
            dve.wait_ge(S["hy_dve"], 24)
            V.tensor_tensor(U, U, X1, ALU.mult).then_inc(S["u_ready"], 1)
            dve.wait_ge(S["u_transposed"], 2)
            V.tensor_copy(UT[:, 1, :], ps[:, 6:8, :].rearrange("p a b -> p (a b)")).then_inc(S["ut_dve"], 1)
            dve.wait_ge(S["u_spectrum_copied"], 2)
            flat = lambda a: a.rearrange("p a b -> p (a b)")
            step(V.tensor_tensor(YT, UI, flat(KI), ALU.mult))
            step(V.tensor_tensor(flat(YR), UR, flat(KR), ALU.mult))
            V.tensor_tensor(flat(YR), flat(YR), YT, ALU.subtract).then_inc(S["y_spectrum"], 1)
            dve.wait_ge(S["y_spectrum"], 1)
            step(V.tensor_tensor(flat(YI), UR, flat(KI), ALU.mult))
            step(V.tensor_tensor(YT, UI, flat(KR), ALU.mult))
            V.tensor_tensor(flat(YI), flat(YI), YT, ALU.add).then_inc(S["y_spectrum"], 1)
            dve.wait_ge(S["y_spectrum"], 2)
            dve.wait_ge(S["channels_taken"], 16)
            for keys in (KF, KB):
                for c in range(8):
                    V.tensor_scalar(keys[:, c, :], keys[:, c, :], OML[:, c:c + 1], None, ALU.mult).then_inc(S["keys_ready"], 1)
            V.memset(DB[:, :, 0:1], 0.0).then_inc(S["db_start"], 1)
            dve.wait_ge(S["ones_ready"], 1)
            for c in range(8):
                dve.wait_ge(S["logs_ready"], c + 1)
                V.tensor_tensor_scan(BF[:, c, :], ones_row, LF[:, c, :], 0.0, ALU.mult, ALU.add).then_inc(S["scanned"], 1)
            for c in range(8):
                dve.wait_ge(S["logs_ready"], 9 + c)
                V.tensor_tensor_scan(DB[:, c, 1:256], ones_row[:, 0:255], LBW[:, c, 0:255], 0.0, ALU.mult,
                                     ALU.add).then_inc(S["scanned"], 1)
            dve.wait_ge(S["y_product"], 1)
            V.tensor_tensor(flat(YB), flat(ps[:, 4:8, :]), X0, ALU.mult).then_inc(S["yb_ready"], 1)
            dve.wait_ge(S["yb_ready"], 1)
            dve.wait_ge(S["keys_ready"], 16)
            dve.wait_ge(S["scanned"], 16)
            dve.wait_ge(S["db_start"], 1)
            dve.wait_ge(S["levels_loaded"], 16)

            def exponents(n):
                hg, m = n // 9, 128 >> (n % 9)
                if n >= 2:
                    dve.wait_ge(S["level_product"], n - 1)
                if n % 9 == 8:
                    V.tensor_tensor(LV[n % 2][:, 0, :], KF.rearrange("p h t -> p (h t)")[:, hg * 1024:(hg + 1) * 1024],
                                    KB.rearrange("p h t -> p (h t)")[:, hg * 1024:(hg + 1) * 1024],
                                    ALU.add).then_inc(S["level_ready"], 1)
                    return
                v = split_view(LV[n % 2][:, 0, :], m)
                f, d = level_view(BF, hg, m), level_view(DB, hg, m)
                nb = 512 // m
                V.tensor_tensor(v[:, :, 0, :], f[:, :, 0, m - 1:m].broadcast_to([128, nb, m]), f[:, :, 0, :],
                                ALU.subtract).then_inc(S["level_ek"], 1)
                V.tensor_tensor(v[:, :, 1, :], d[:, :, 1, :], d[:, :, 1, 0:1].broadcast_to([128, nb, m]),
                                ALU.subtract).then_inc(S["level_ek"], 1)

            def decayed(n):
                if n % 9 == 8:
                    return
                hg, m = n // 9, 128 >> (n % 9)
                dve.wait_ge(S["level_exp"], n - n // 9 + 1)
                v = split_view(LV[n % 2][:, 0, :], m)
                V.tensor_tensor(v[:, :, 0, :], v[:, :, 0, :], level_view(KF, hg, m)[:, :, 0, :], ALU.mult)
                V.tensor_tensor(v[:, :, 1, :], v[:, :, 1, :], level_view(KB, hg, m)[:, :, 1, :], ALU.mult)
                V.tensor_tensor(LV[n % 2][:, 1, :], LV[n % 2][:, 1, :],
                                Q.rearrange("p h t -> p (h t)")[:, hg * 1024:(hg + 1) * 1024],
                                ALU.mult).then_inc(S["level_ready"], 1)

            def select(n):
                if n % 9 == 0:
                    return
                hg = n // 9
                dve.wait_ge(S["level_product"], n + 1)
                if n % 9 >= 2:
                    dve.wait_ge(S["level_dve"], level_dve(n - 1))
                mask = levels[:, n % 9 - 1, :].bitcast(u32).unsqueeze(1).broadcast_to([128, 4, 128])
                for st in range(2):
                    last = V.copy_predicated(AT[hg][:, :, st, st * 128:(st + 1) * 128], mask,
                                             ps[:, 4 + 2 * (n % 2) + st, :].rearrange("p (h c) -> p h c", h=4))
                last.then_inc(S["level_dve"], 1)

            def branch_b(s):
                dve.wait_ge(S["slot_multiplied"], W_BB + s + 1)
                c = slice(2 * s, 2 * s + 2)
                V.tensor_tensor(flat(MERGED[:, c, :]), ps[:, (36 + s) % 3, :], flat(GB[:, c, :]), ALU.mult).then_inc(S["bb_taken"], 1)

            exponents(0)
            for n in range(NLV):
                if n + 1 < NLV and (n + 1) % 9 != 8:
                    exponents(n + 1)
                decayed(n)
                if n + 1 < NLV and (n + 1) % 9 == 8:
                    exponents(n + 1)
                if n:
                    select(n - 1)
                if n in (13, 14, 16, 17):
                    branch_b((13, 14, 16, 17).index(n))
            select(NLV - 1)
            dve.wait_ge(S["o_sums"], 1)
            step(V.tensor_scalar(flat(RS), flat(ps[:, 4:8, :]), 1.0 / 128, 1e-6, ALU.mult, ALU.add))
            V.reciprocal(flat(RS), flat(RS)).then_inc(S["o_inverse"], 1)
            dve.wait_ge(S["gates2_ready"], 2)
            step(V.scalar_tensor_tensor(flat(OT), flat(OT), vecs[:, V_GN:V_GN + 1], flat(OG), ALU.mult, ALU.mult))
            dve.wait_ge(S["o_rstd"], 1)
            V.tensor_tensor(flat(OT), flat(OT), flat(RS), ALU.mult).then_inc(S["o_ready"], 1)
            dve.wait_ge(S["bb_taken"], 4)
            for s in range(4):
                dve.wait_ge(S["slot_multiplied"], W_BA + s + 1)
                c = slice(2 * s, 2 * s + 2)
                V.tensor_tensor(BTMP[:, s % 2, :], ps[:, (40 + s) % 3, :], flat(GA[:, c, :]), ALU.mult).then_inc(S["ba_taken"], 1)
                dve.wait_ge(S["ba_taken"], s + 1)
                V.tensor_tensor(flat(MERGED[:, c, :]), flat(MERGED[:, c, :]), BTMP[:, s % 2, :],
                                ALU.add).then_inc(S["merged_ready"], 1)
            dve.wait_ge(S["slot_multiplied"], W_OUT2 + 4)
            for t in range(TOK):
                V.tensor_tensor(x[:, t, :], x[:, t, :], flat(ps[:, 4 + 2 * t:6 + 2 * t, :]), ALU.add).then_inc(S["mixer_added"], 1)
            norm_dve(3)

            def best(rows, values, indices, low=-3e38):
                for first in (0, 8):
                    for r, v, i in zip(rows, values, indices):
                        last = V.max(v[:, first:first + 8], r)
                    step(last)
                    for r, v, i in zip(rows, values, indices):
                        last = V.max_index(i[:, first:first + 8], v[:, first:first + 8], r)
                    step(last)
                    if first == 0:
                        for r, v, i in zip(rows, values, indices):
                            last = V.match_replace(r, v[:, 0:8], r, low)
                        step(last)

            for t in range(TOK):
                dve.wait_ge(S["sim_copied"], t + 1)
                g = range(16)
                best([SC[:, t, n, :] for n in g], [T1V[:, t, n, :] for n in g], [T1I[:, t, n, :] for n in g])
                halves = T1V[:, t].rearrange("p (h s) k -> p h s k", s=2)
                step(V.tensor_tensor(CS[:, t].rearrange("p h (a b) -> p h a b", a=16),
                                     halves[:, :, 0, :].unsqueeze(3).broadcast_to([128, 8, 16, 16]),
                                     halves[:, :, 1, :].unsqueeze(2).broadcast_to([128, 8, 16, 16]), ALU.add))
                g = range(8)
                best([CS[:, t, n, :] for n in g], [TV[:, 8 * t + n, :] for n in g], [TP[:, 8 * t + n, :] for n in g])
            tp = TP.rearrange("p g k -> p (g k)")
            V.tensor_scalar(PAI[:, 0, :], tp, 4, None, ALU.logical_shift_right)
            step(V.tensor_scalar(PAI[:, 1, :], tp, 15, None, ALU.bitwise_and))
            step(V.tensor_copy(PA, PAI))
            step(V.tensor_copy(T1F, T1I))
            dve.wait_ge(S["iota_loaded"], 16)
            for t in range(TOK):
                for side in range(2):
                    place = PA[:, side, t * 128:(t + 1) * 128].unsqueeze(2).broadcast_to([128, 128, 16])
                    step(V.tensor_tensor(EQ.rearrange("p (g a) -> p g a", a=16), place,
                                         iota[:, 0:16].unsqueeze(1).broadcast_to([128, 128, 16]), ALU.is_equal))
                    eq = EQ.rearrange("p (h k a) -> p h k a", h=8, k=16)
                    index = T1F[:, t].rearrange("p (h s) k -> p h s k", s=2)[:, :, side, :].unsqueeze(2).broadcast_to([128, 8, 16, 16])
                    step(V.tensor_tensor(eq, eq, index, ALU.mult))
                    step(V.tensor_reduce(IX[:, side, t, :], EQ.rearrange("p (g a) -> p g a", a=16), AX, ALU.add))
            top, total, inv = (stat[:, c:c + 16] for c in (ST_CMAX, ST_CSUM, ST_CREC))
            wide = lambda a: a.unsqueeze(2).broadcast_to([128, 16, 16])
            step(V.tensor_copy(top, TV[:, :, 0]))
            V.tensor_tensor(TV, TV, wide(top), ALU.subtract).then_inc(S["routes_shifted"], 1)
            dve.wait_ge(S["routes_exp"], 1)
            step(V.tensor_reduce(total, TV, AX, ALU.add))
            step(V.reciprocal(inv, total))
            V.tensor_tensor(TV, TV, wide(inv), ALU.mult).then_inc(S["routes_ready"], 1)
            dve.wait_ge(S["routes_copied"], 2)

            def onehots(half, q, parity, it=None):
                tok = at(4 * (q - 64 * half), 8, it)
                if q >= 2:
                    dve.wait_ge(S["gate_product"], at(q - 1, 2, it))
                first, second, gate = (ROUTE[:, n, bass.ds(tok, 4)] for n in range(3))
                V.tensor_tensor(OA[:, parity], first.unsqueeze(2).broadcast_to([128, 4, 128]),
                                iota.unsqueeze(1).broadcast_to([128, 4, 128]), ALU.is_equal)
                V.tensor_tensor(OB[:, parity], second.unsqueeze(2).broadcast_to([128, 4, 64]),
                                iota[:, 64 * half:64 * half + 64].unsqueeze(1).broadcast_to([128, 4, 64]),
                                ALU.is_equal).then_inc(S["onehot_j"], 1)
                dve.wait_ge(S["onehot_j"], at(q + 1, 2, it))
                V.tensor_tensor(OB[:, parity], OB[:, parity], gate.unsqueeze(2).broadcast_to([128, 4, 64]),
                                ALU.mult).then_inc(S["onehots"], 1)

            def gated(half, q, parity, it=None):
                tok = at(4 * (q - 64 * half), 8, it)
                dve.wait_ge(S["gate_product"], at(q + 1, 2, it))
                h = H[:, 64 * half:64 * half + 64, bass.ds(tok, 4)].rearrange("p j t -> p t j")
                bank = (parity if half else 3 + parity)
                V.tensor_tensor(h, ps[:, bank, 0:256].rearrange("p (t j) -> p t j", t=4), h, ALU.mult).then_inc(S["gated"], 1)

            for half in range(2):
                dve.wait_ge(S["h_ready"], 32 + 32 * half)
                q = 64 * half
                onehots(half, q, 0)
                onehots(half, q + 1, 1)
                gated(half, q, 0)
                with dve.Fori(0, 31) as it:
                    onehots(half, q + 2, 0, it)
                    gated(half, q + 1, 1, it)
                    onehots(half, q + 3, 1, it)
                    gated(half, q + 2, 0, it)
                gated(half, q + 63, 1)
            dve.wait_ge(S["slot_multiplied"], NSLOT)
            V.tensor_copy(flat(PT[:, 4:8, :]), flat(ps[:, 6:8, :])).then_inc(S["pt_dve"], 1)
            for t in range(TOK):
                dve.wait_ge(S["pt_transposed"], t + 1)
                V.tensor_tensor(x[:, t, :], x[:, t, :], flat(ps[:, 2 * t:2 * t + 2, :]), ALU.add).then_inc(S["peer_added"], 1)
            inverse("squares_summed", 10, "inv_ready", 5)
            dve.wait_ge(S["rstd_ready"], 5)
            dve.wait_ge(S["rows_loaded"], 48)
            for t in range(TOK):
                V.scalar_tensor_tensor(x[:, t, :], x[:, t, :], stat[:, ST_RSTD + t:ST_RSTD + t + 1], wrow[:, :],
                                       ALU.mult, ALU.mult).then_inc(S["x_final"], 1)

        block = ctx.enter_context(nc.Block())

        @block.sync
        def _(sp):
            sp.dma_start(x[:, :, :], dram["x"]).then_inc(S["x_loaded"], 16)
            sp.dma_start(ident[:, :], dram["ident"]).then_inc(S["consts_loaded"], 16)
            sp.dma_start(vecs[:, :], dram["vecs"]).then_inc(S["consts_loaded"], 16)
            for r in range(RING):
                sp.dma_start(ring[:, r, :], dram["stream"][r, :, :]).then_inc(arrived[r], 16)
            with sp.Fori(1, NSLOT // RING) as turn:
                for r in range(RING):
                    sp.wait_ge(S["slot_multiplied"], turn * RING + (r + 1 - RING))
                    sp.dma_start(ring[:, r, :], dram["stream"][turn * RING + r, :, :]).then_inc(arrived[r], 16)
            sp.wait_ge(S["x_final"], 2)
            sp.dma_start(dram["out"], x[:, :, :]).then_inc(S["out_stored"], 16)
            sp.wait_ge(S["out_stored"], 16)

        @block.gpsimd
        def _(pool):
            pool.dma_start(ZT, dram["zt"]).then_inc(S["filt_loaded"], 16)
            pool.dma_start(FT, dram["filt"]).then_inc(S["filt_loaded"], 16)
            pool.dma_start(FW[:, 0, :], dram["fdecay"]).then_inc(S["fdecay_loaded"], 16)
            pool.dma_start(aux[:, 0:2040], dram["tab1"]).then_inc(S["tab_loaded"], 16)
            pool.dma_start(W3[0:64, :], dram["w3"]).then_inc(S["w3_loaded"], 16)
            pool.dma_start(DF1.rearrange("p a b -> p (a b)"), dram["dft"][:, 0:1024]).then_inc(S["dft_loaded"], 16)
            pool.dma_start(wrow[0:1, :], dram["bias"]).then_inc(S["bias_loaded"], 16)
            pool.wait_ge(S["xn_transposed"], 4)
            pool.dma_start(gnw, dram["gnw"]).then_inc(S["gnw_loaded"], 16)

            pool.wait_ge(S["tab_loaded"], 16)
            pool.wait_ge(S["p1_act"], 3)
            steps = 0
            src = P1[:, 0, 0:1280].rearrange("p (h c) -> p h c", h=20)
            lo, hi = src[:, :, 0:32], src[:, :, 32:64]
            c = cosT[:, 0, :].unsqueeze(1).broadcast_to([128, 20, 32])
            s = sinT[:, 0, :].unsqueeze(1).broadcast_to([128, 20, 32])
            P.tensor_tensor(RC, lo, c, ALU.mult).then_inc(S["pool_step"], 1)
            P.tensor_tensor(RD, hi, s, ALU.mult).then_inc(S["pool_step"], 1)
            pool.wait_ge(S["pool_step"], 2)
            P.tensor_tensor(R[:, 0, :, 0:32], RC, RD, ALU.subtract).then_inc(S["pool_step"], 1)
            pool.wait_ge(S["pool_step"], 3)
            P.tensor_tensor(RC, lo, s, ALU.mult).then_inc(S["pool_step"], 1)
            P.tensor_tensor(RD, hi, c, ALU.mult).then_inc(S["pool_step"], 1)
            pool.wait_ge(S["pool_step"], 5)
            P.tensor_tensor(R[:, 0, :, 32:64], RC, RD, ALU.add).then_inc(S["rope_ready"], 1)
            pool.wait_ge(S["filt_ab"], 2)
            pool.wait_ge(S["p1_dve"], 3)
            for t in range(TOK):
                heads = P1[:, t, 1280:1536].rearrange("p (i c) -> p i c", i=4).unsqueeze(2).broadcast_to([128, 4, 2, 64])
                P.tensor_copy(DUP[:, t], heads).then_inc(S["dup_ready"], 1)
            pool.wait_ge(S["kernel_spectrum"], 2)
            pool.dma_start(cmps[:, :], dram["cmps"]).then_inc(S["cmps_loaded"], 16)
            pool.dma_start(wrow[:, :], dram["post1"]).then_inc(S["rows_loaded"], 16)
            pool.wait_ge(S["wrow_free"], 2)
            pool.dma_start(wrow[:, :], dram["post2"]).then_inc(S["rows_loaded"], 16)
            pool_second(pool)

        def mm(out, lhsT, rhs, start=True, stop=True):
            return nc.tensor.matmul(out, lhsT, rhs, start=start, stop=stop, skip_group_check=True)

        def at(base, step, it):
            return base if it is None else it * step + base

        @block.tensor
        def _(pe):
            def slot(n, it=None):
                pe.wait_ge(arrived[n % RING], at(16 * (n // RING + 1), 16, it))
                return ring[:, n % RING, :]

            def norm_transposes(k):
                pe.wait_ge(S["xn_ready"], 2 * k + 2)
                for c in range(KC):
                    for t in range(TOK):
                        last = nc.tensor.transpose(ps[:, c // 2, (c % 2) * 256 + t * 128:(c % 2) * 256 + t * 128 + 128],
                                                   xn[:, t, c * 128:(c + 1) * 128], ident[:, :])
                    if c % 2:
                        last.then_inc(S["xn_transposed"], 1)

            def wait_hT(k):
                pe.wait_ge(S["hT_act"], 4 * k + 4)
                pe.wait_ge(S["hT_dve"], 4 * k + 4)

            def token_product(n, bank, src, halves=2):
                for kh in range(halves):
                    w = slot(n + kh)
                    for t in range(TOK):
                        for k4 in range(4):
                            last = mm(ps[:, bank + t, :], src[:, kh * 4 + k4, t * 128:(t + 1) * 128],
                                      w[:, k4 * 512:(k4 + 1) * 512], kh == 0 and k4 == 0, kh == 1 and k4 == 3)
                    last.then_inc(S["slot_multiplied"], 1)

            pe.wait_ge(S["filt_loaded"], 32)
            mm(ps[0:64, 7, 0:256], FT[0:33, 0:64], ZT[0:33, 0:256]).then_inc(S["filt_hidden"], 1)
            pe.wait_ge(S["consts_loaded"], 32)
            norm_transposes(0)
            wait_hT(0)

            def p1_group(g):
                if g >= 2:
                    pe.wait_ge(S["p1_act"], g - 1)
                    pe.wait_ge(S["p1_dve"], g - 1)
                token_product(2 * g, 4 + 2 * (g % 2), hT)

            p1_group(0)
            pe.wait_ge(S["filt_sine"], 1)
            mm(ps[0:64, 0, 0:256], FT[0:64, 64:128], FHID[0:64, 0, :]).then_inc(S["filt_hidden"], 1)
            p1_group(1)
            pe.wait_ge(S["filt_sine"], 2)
            pe.wait_ge(S["w3_loaded"], 16)
            for pt in range(TOK):
                if pt:
                    pe.wait_ge(S["filt_windowed"], 1)
                for n in range(4):
                    last = mm(ps[:, n, :], FHID[0:64, 1, pt * 128:(pt + 1) * 128], W3[0:64, n * 512:(n + 1) * 512])
                last.then_inc(S["filt_product"], 1)
                p1_group(2 + pt)
            pe.wait_ge(S["dft_loaded"], 16)
            pe.wait_ge(S["filt_ab"], 2)
            for part in range(2):
                if part:
                    pe.wait_ge(S["spectrum_copied"], 1)
                for ft in range(2):
                    for nh in range(2):
                        for pt in range(TOK):
                            last = mm(ps[:, ft * 2 + nh, :], DF1[:, part * 2 + pt, ft * 128:(ft + 1) * 128],
                                      FAB[:, part, pt, nh * 512:(nh + 1) * 512], pt == 0, pt == 1)
                last.then_inc(S["kernel_spectrum"], 1)
                if part == 0:
                    p1_group(4)
            pe.wait_ge(S["p1_act"], 4)
            pe.wait_ge(S["p1_dve"], 4)
            w = slot(10)
            for t in range(TOK):
                for k in range(KC):
                    last = mm(ps[:, 6 + t, 0:256], hT[:, k, t * 128:(t + 1) * 128], w[:, k * 256:(k + 1) * 256],
                              k == 0, k == KC - 1)
            last.then_inc(S["slot_multiplied"], 1)
            pe.wait_ge(S["p1_act"], 5)
            pe.wait_ge(S["p1_dve"], 5)
            pe.wait_ge(S["cmps_loaded"], 16)
            for t in range(TOK):
                for k in range(KC):
                    last = mm(ps[:, 4 + t, 0:24], hT[:, k, t * 128:(t + 1) * 128], wng[:, k, :], k == 0, k == KC - 1)
            last.then_inc(S["gates_product"], 1)

            pe.wait_ge(S["rope_ready"], 2)
            pe.wait_ge(S["spectrum_copied"], 2)
            for b in range(10):
                if b >= 4:
                    pe.wait_ge(S["heads_dve"] if b % 2 else S["heads_act"], (b - 4) // 2 + 1)
                for h in range(2):
                    for t in range(TOK):
                        last = nc.tensor.transpose(ps[0:64, b % 4, h * 256 + t * 128:h * 256 + t * 128 + 128],
                                                   R[:, t, 2 * b + h, :], ident[:, :])
                last.then_inc(S["heads_transposed"], 1)
            pe.wait_ge(S["dup_ready"], 2)
            pe.wait_ge(S["gates_ready"], 1)
            for i in range(4):
                for t in range(TOK):
                    last = nc.tensor.transpose(ps[:, 4 + i // 2, (i % 2) * 256 + t * 128:(i % 2) * 256 + t * 128 + 128],
                                               DUP[:, t, i].rearrange("p a c -> p (a c)"), ident[:, :])
            last.then_inc(S["dup_transposed"], 1)
            pe.wait_ge(S["heads_act"], 5)
            pe.wait_ge(S["heads_dve"], 5)
            for h in range(4):
                mm(ps[:, h, 0:256], RT[0:64, 4 + h, 0:128], RT[0:64, h, :])
                mm(ps[:, h, 256:384], RT[0:64, 4 + h, 128:256], RT[0:64, h, 128:256]).then_inc(S["ret_scores"], 1)
            pe.wait_ge(S["blocks_ready"], 4)
            pe.wait_ge(S["p1_act"], 6)
            pe.wait_ge(S["p1_dve"], 6)
            for kv in range(2):
                for bh in range(2):
                    w = slot(W_CMP + 2 * kv + bh)
                    for half in range(2):
                        for b8 in range(8):
                            last = mm(ps[:, 6 + half, kv * 30:kv * 30 + 30],
                                      w[:, b8 * 256 + half * 128:b8 * 256 + half * 128 + 128],
                                      BLK[:, kv, bh * 8 + b8, :], bh == 0 and b8 == 0, bh == 1 and b8 == 7)
                    last.then_inc(S["slot_multiplied"], 1)
            pe.wait_ge(S["hid_ready"], 4)
            for n, w2 in enumerate((w2k, w2r)):
                for half in range(2):
                    mm(ps[0:64, 4, n * 30:n * 30 + 30], w2[:, half, :], HID[:, 0, half, :], half == 0, half == 1)
            for g in range(2):
                for half in range(2):
                    last = mm(ps[0:NCMP, 5, g * 64:g * 64 + 64], HID[:, 1, half, g * NCMP:(g + 1) * NCMP],
                              w2v[:, half, :], half == 0, half == 1)
            last.then_inc(S["cmp_product"], 1)
            pe.wait_ge(S["ret_decayed"], 4)
            for h in range(4):
                v0, v1 = (P1[:, t, 1536 + h * 128:1536 + (h + 1) * 128] for t in range(2))
                mm(ps[:, 6, h * 128:(h + 1) * 128], SD[:, h, 0:128], v0)
                mm(ps[:, 7, h * 128:(h + 1) * 128], SD[:, h, 128:256], v0, True, False)
                last = mm(ps[:, 7, h * 128:(h + 1) * 128], SD[:, h, 256:384], v1, False, True)
            last.then_inc(S["ret_out"], 1)
            pe.wait_ge(S["kc_ready"], 1)
            for t in range(TOK):
                for h in range(8):
                    last = mm(ps[:, 4, (t * 8 + h) * NCMP:(t * 8 + h + 1) * NCMP], RT[0:64, 8 + h, t * 128:(t + 1) * 128],
                              KCT[0:64, (h // 4) * NCMP:(h // 4 + 1) * NCMP])
            last.then_inc(S["cmp_scores"], 1)
            pe.wait_ge(S["cmp_probs"], 1)
            for n in range(16):
                last = nc.tensor.transpose(ps[0:NCMP, n // 4, (n % 4) * 128:(n % 4 + 1) * 128],
                                           CE[:, n // 8, n % 8, :], ident[:, :])
            last.then_inc(S["cmp_ptrans"], 1)
            pe.wait_ge(S["cmp_pcopied"], 1)
            pe.wait_ge(S["vc_copied"], 1)
            for n in range(16):
                last = mm(ps[:, 4 + n // 8, (n % 8) * 64:(n % 8 + 1) * 64], CET[0:NCMP, n * 128:(n + 1) * 128],
                          VC[0:NCMP, (n % 8) // 4, :])
            last.then_inc(S["cmp_out"], 1)

            def scores(u):
                br, qt, g = u // 4, u // 2 % 2, u % 2
                nk = 128 * (qt + 1)
                for r in range(4):
                    col = r * nk
                    last = mm(ps[:, 2 * (u % 2) + col // 512, col % 512:col % 512 + nk],
                              RT[0:64, 8 + 4 * g + r, qt * 128:(qt + 1) * 128], RT[0:64, 16 + 2 * br + g, 0:nk])
                last.then_inc(S["att_scores"], 1)

            scores(0)
            scores(1)
            pe.wait_ge(S["cmp_done"], 2)
            pe.wait_ge(S["ret_normed"], 1)
            for u in range(8):
                br, qt, g = u // 4, u // 2 % 2, u % 2
                nj = qt + 1
                pe.wait_ge(S["att_exp"], 4 * u + 4)
                if u:
                    pe.wait_ge(S["att_copied_act"], u)
                    if dve_copies(u):
                        pe.wait_ge(S["att_copied_dve"], dve_copies(u))
                for r in range(4):
                    for jt in range(nj):
                        n = r * nj + jt
                        last = nc.tensor.transpose(ps[:, 4 + n // 4, (n % 4) * 128:(n % 4 + 1) * 128],
                                                   SM[:, u % 2, r, jt * 128:(jt + 1) * 128], ident[:, :])
                last.then_inc(S["att_transposed"], 1)
                pe.wait_ge(S["att_copied_act"], u + 1)
                if dve_copies(u + 1):
                    pe.wait_ge(S["att_copied_dve"], dve_copies(u + 1))
                if g == 0 and u >= 4:
                    pe.wait_ge(S["att_done"], u // 2 - 1)
                vcol = 2560 + 128 * br + 64 * g
                for r in range(4):
                    for jt in range(nj):
                        last = mm(ps[:, 6 + u // 2 % 2, (4 * g + r) * 64:(4 * g + r + 1) * 64],
                                  ET[:, u % 2, (r * nj + jt) * 128:(r * nj + jt + 1) * 128], P1[:, jt, vcol:vcol + 64],
                                  jt == 0, jt == nj - 1)
                last.then_inc(S["att_out"], 1)
                if u + 2 < 8:
                    scores(u + 2)
            pe.wait_ge(S["att_done"], 4)
            for c in range(KC):
                for t in range(TOK):
                    last = nc.tensor.transpose(ps[:, c // 2, (c % 2) * 256 + t * 128:(c % 2) * 256 + t * 128 + 128],
                                               mix[:, t, c * 128:(c + 1) * 128], ident[:, :])
                if c % 2:
                    last.then_inc(S["mix_transposed"], 1)
            pe.wait_ge(S["mixT_act"], 2)
            pe.wait_ge(S["mixT_dve"], 2)

            def out_product(n, src):
                for nh in range(2):
                    for kh in range(2):
                        w = slot(n + 2 * nh + kh)
                        for t in range(TOK):
                            for k4 in range(4):
                                last = mm(ps[:, 4 + 2 * t + nh, :], src[:, kh * 4 + k4, t * 128:(t + 1) * 128],
                                          w[:, k4 * 512:(k4 + 1) * 512], kh == 0 and k4 == 0, kh == 1 and k4 == 3)
                        last.then_inc(S["slot_multiplied"], 1)

            out_product(W_OUT, mixT)
            norm_transposes(1)
            wait_hT(1)

            def ffn_up(i, n, it=None):
                w = slot(n, it)
                if i >= 4:
                    pe.wait_ge(S["ffn_conv_dve"], at(2 * (i - 3), 8, it))
                for j in range(2):
                    for k in range(KC):
                        last = mm(ps[:, i % 4, j * 256:(j + 1) * 256], w[:, (j * 8 + k) * 128:(j * 8 + k + 1) * 128],
                                  hT[:, k, :], k == 0, k == KC - 1)
                last.then_inc(S["slot_multiplied"], 1)

            def ffn_down(p, n, it=None):
                w = slot(n, it)
                pe.wait_ge(S["ffn_gated"], at(2 * p + 2, 4, it))
                for ii in range(2):
                    for t in range(TOK):
                        for nh in range(2):
                            last = mm(ps[:, 4 + 2 * t + nh, :], HACT[:, (2 * p + ii) % 4, t * 128:(t + 1) * 128],
                                      w[:, ii * 1024 + nh * 512:ii * 1024 + (nh + 1) * 512],
                                      p == 0 and ii == 0, p == 10 and ii == 1)
                last.then_inc(S["slot_multiplied"], 1)

            def ffn_pair(p, it=None):
                n = W_FFN + 2 + 3 * (p - 1)
                ffn_up(2 * p, n, it)
                ffn_up(2 * p + 1, n + 1, it)
                ffn_down(p - 1, n + 2, it)

            ffn_up(0, W_FFN)
            ffn_up(1, W_FFN + 1)
            ffn_pair(1)
            ffn_pair(2)
            with pe.Fori(0, 4) as it:
                ffn_pair(3, it)
                ffn_pair(4, it)
            ffn_down(10, W_FFN + 32)
            pe_second(pe, slot, norm_transposes, wait_hT, token_product, out_product)

        @block.scalar
        def _(act):
            def norm_act(k):
                for t in range(TOK):
                    A.activation(xn[:, t, :], x[:, t, :], ACT.Square,
                                 accum_out=stat[:, ST_SQ + t:ST_SQ + t + 1]).then_inc(S["squares_summed"], 1)
                act.wait_ge(S["inv_ready"], k + 1)
                A.activation(stat[:, ST_RSTD:ST_RSTD + 2], stat[:, ST_INV:ST_INV + 2], ACT.Sqrt).then_inc(S["rstd_ready"], 1)
                for c in (0, 1, 4, 5):
                    act.wait_ge(S["xn_transposed"], 4 * k + c // 2 + 1)
                    A.activation(hT[:, c, :], ps[:, c // 2, c % 2 * 256:c % 2 * 256 + 256], ACT.Copy,
                                 scale=vecs[:, V_NORM + 8 * k + c:V_NORM + 8 * k + c + 1]).then_inc(S["hT_act"], 1)

            act.wait_ge(S["fdecay_loaded"], 16)
            act.wait_ge(S["filt_loaded"], 32)
            A.activation(FW[:, 0, :], FW[:, 0, :], ACT.Abs).then_inc(S["act_step"], 1)
            act.wait_ge(S["act_step"], 1)
            A.activation(FW[:, 1, :], FW[:, 0, :], ACT.Exp, scale=ZT[:, 257:258]).then_inc(S["act_step"], 1)
            act.wait_ge(S["act_step"], 2)
            A.activation(FW[:, 0, :], FW[:, 0, :], ACT.Exp, scale=ZT[:, 256:257]).then_inc(S["filt_window"], 1)
            act.wait_ge(S["x_loaded"], 16)
            act.wait_ge(S["consts_loaded"], 32)
            norm_act(0)
            act.wait_ge(S["filt_reduced"], 1)
            A.activation(FHID[0:64, 0, :], FTMP[0:64, 0, :], ACT.Sin).then_inc(S["filt_sine"], 1)

            def p1_copy(g):
                act.wait_ge(S["slot_multiplied"], 2 * g + 2)
                A.copy(P1[:, 0, g * 512:(g + 1) * 512], ps[:, 4 + 2 * (g % 2), :]).then_inc(S["p1_act"], 1)

            p1_copy(0)
            act.wait_ge(S["filt_reduced"], 2)
            A.activation(FHID[0:64, 1, :], FTMP[0:64, 0, :], ACT.Sin).then_inc(S["filt_sine"], 1)
            p1_copy(1)
            p1_copy(2)
            p1_copy(3)
            act.wait_ge(S["kernel_spectrum"], 1)
            A.copy(KR.rearrange("p a b -> p (a b)"), ps[:, 0:4, :].rearrange("p a b -> p (a b)")).then_inc(S["spectrum_copied"], 1)
            p1_copy(4)
            act.wait_ge(S["kernel_spectrum"], 2)
            A.copy(KI.rearrange("p a b -> p (a b)"), ps[:, 0:4, :].rearrange("p a b -> p (a b)")).then_inc(S["spectrum_copied"], 1)
            act.wait_ge(S["slot_multiplied"], 11)
            A.copy(P1[:, 0, 2560:2816], ps[:, 6, 0:256]).then_inc(S["p1_act"], 1)
            act.wait_ge(S["gates_product"], 1)
            A.activation(P1[:, :, 2816:2840], ps[:, 4:6, 0:24], ACT.Sigmoid).then_inc(S["gates_ready"], 1)
            act.wait_ge(S["p1_dve"], 5)
            A.activation(P1[:, :, 2048:2560], P1[:, :, 2048:2560], ACT.Silu).then_inc(S["silu_ready"], 1)
            for b in range(0, 10, 2):
                act.wait_ge(S["heads_transposed"], b + 1)
                A.mul(RT[0:64, 2 * b:2 * b + 2, :].rearrange("p a b -> p (a b)"), ps[0:64, b % 4, :],
                      0.125 if 4 <= b < 8 else 1.0).then_inc(S["heads_act"], 1)
            act.wait_ge(S["slot_multiplied"], W_CMP + 4)
            for kv in range(2):
                for half in range(2):
                    A.activation(HID[:, kv, half, :], ps[:, 6 + half, kv * 30:kv * 30 + 30],
                                 ACT.Gelu_apprx_tanh).then_inc(S["hid_ready"], 1)
            act.wait_ge(S["cmp_product"], 1)
            A.copy(VC[0:NCMP].rearrange("p a b -> p (a b)"), ps[0:NCMP, 5, 0:128]).then_inc(S["vc_copied"], 1)
            act.wait_ge(S["cmp_shifted"], 1)
            A.activation(CE, CE, ACT.Exp).then_inc(S["cmp_exp"], 1)
            act.wait_ge(S["gn_inv"], 1)
            A.activation(stat[:, ST_GRSTD:ST_GRSTD + 8], stat[:, ST_GVAR:ST_GVAR + 8], ACT.Sqrt).then_inc(S["gn_rstd"], 1)
            act.wait_ge(S["cmp_ptrans"], 1)
            A.copy(CET[0:NCMP, :], ps[0:NCMP, 0:4, :].rearrange("p a b -> p (a b)")).then_inc(S["cmp_pcopied"], 1)

            def exps(u):
                qt = u // 2 % 2
                act.wait_ge(S["att_max"], u + 1)
                for r in range(4):
                    col = ST_SUM + 8 * (u // 2) + 4 * (u % 2) + r
                    e = SM[:, u % 2, r, 0:128 * (qt + 1)]
                    A.activation(e, e, ACT.Exp, bias=stat[:, ST_NMAX + 4 * (u % 2) + r:ST_NMAX + 4 * (u % 2) + r + 1],
                                 accum_out=stat[:, col:col + 1]).then_inc(S["att_exp"], 1)

            exps(0)
            for u in range(8):
                if u + 1 < 8:
                    exps(u + 1)
                act.wait_ge(S["att_transposed"], u + 1)
                A.copy(ET[:, u % 2, 0:512], ps[:, 4, :]).then_inc(S["att_copied_act"], 1)
            for b in (0, 2):
                act.wait_ge(S["mix_transposed"], b + 1)
                A.copy(mixT[:, 2 * b:2 * b + 2, :].rearrange("p a b -> p (a b)"), ps[:, b, :]).then_inc(S["mixT_act"], 1)

            def post_act(k, n):
                act.wait_ge(S["slot_multiplied"], n)
                for t in range(TOK):
                    A.activation(xn[:, t, :], ps[:, 4 + 2 * t:6 + 2 * t, :].rearrange("p a b -> p (a b)"), ACT.Square,
                                 accum_out=stat[:, ST_SQ + t:ST_SQ + t + 1]).then_inc(S["post_squares"], 1)
                act.wait_ge(S["post_inv"], k + 1)
                A.activation(stat[:, ST_RSTD:ST_RSTD + 2], stat[:, ST_INV:ST_INV + 2], ACT.Sqrt).then_inc(S["post_rstd"], 1)

            post_act(0, W_OUT + 4)
            act.wait_ge(S["post_done"], 2)
            norm_act(1)

            def ffn_act(i, n, it=None):
                act.wait_ge(S["slot_multiplied"], at(n + 1, 6, it))
                if i >= 2:
                    act.wait_ge(S["ffn_gated"], at(i - 1, 4, it))
                for j in range(2):
                    col = at(V_CONV + (j * NFF + i) * 3 + 2, 12, it)
                    A.activation(CONV[:, i % 2, j, :], ps[:, i % 4, j * 256:(j + 1) * 256], ACT.Copy,
                                 scale=vecs[:, bass.ds(col, 1)]).then_inc(S["ffn_conv_act"], 1)
                act.wait_ge(S["ffn_conv_dve"], at(2 * i + 1, 8, it))
                A.activation(CONV[:, i % 2, 0, :], CONV[:, i % 2, 0, :], ACT.Gelu_apprx_tanh).then_inc(S["ffn_gelu"], 1)

            def ffn_act_pair(p, it=None):
                n = W_FFN + 2 + 3 * (p - 1)
                ffn_act(2 * p, n, it)
                ffn_act(2 * p + 1, n + 1, it)

            ffn_act(0, W_FFN)
            ffn_act(1, W_FFN + 1)
            ffn_act_pair(1)
            ffn_act_pair(2)
            with act.Fori(0, 4) as it:
                ffn_act_pair(3, it)
                ffn_act_pair(4, it)
            post_act(1, W_FFN + 33)
            act.wait_ge(S["post_done"], 4)
            act_second(act, norm_act)

        @block.vector
        def _(dve):
            steps = [0]

            def step(instruction):
                steps[0] += 1
                instruction.then_inc(S["dve_step"], 1)
                dve.wait_ge(S["dve_step"], steps[0])

            def inverse(squares, n_squares, done, n_done):
                dve.wait_ge(S[squares], n_squares)
                step(V.tensor_scalar(stat[:, ST_INV:ST_INV + 2], stat[:, ST_SQ:ST_SQ + 2], 1.0 / D, 1e-6, ALU.mult, ALU.add))
                V.reciprocal(stat[:, ST_INV:ST_INV + 2], stat[:, ST_INV:ST_INV + 2]).then_inc(S[done], 1)

            def norm_dve(k):
                inverse("squares_summed", 2 * k + 2, "inv_ready", k + 1)
                dve.wait_ge(S["rstd_ready"], k + 1)
                for t in range(TOK):
                    V.tensor_scalar(xn[:, t, :], x[:, t, :], stat[:, ST_RSTD + t:ST_RSTD + t + 1], None,
                                    ALU.mult).then_inc(S["xn_ready"], 1)
                for c in (2, 3, 6, 7):
                    dve.wait_ge(S["xn_transposed"], 4 * k + c // 2 + 1)
                    V.tensor_scalar(hT[:, c, :], ps[:, c // 2, c % 2 * 256:c % 2 * 256 + 256], vecs[:, V_NORM + 8 * k + c:V_NORM + 8 * k + c + 1],
                                    None, ALU.mult).then_inc(S["hT_dve"], 1)

            def reduce_angle(src, layer):
                y, k = FTMP[0:64, 0, :], FTMP[0:64, 1, :]
                b, f = (FT[0:64, 128 + 2 * layer + n:129 + 2 * layer + n] for n in range(2))
                step(V.tensor_scalar(y, src, b, f, ALU.add, ALU.mult))
                step(V.tensor_scalar(k, y, INV_2PI, ROUND, ALU.mult, ALU.add))
                step(V.tensor_scalar(k, k, -ROUND, None, ALU.add))
                for part in (PI2_A, PI2_B, PI2_C):
                    step(V.scalar_tensor_tensor(y, k, -part, y, ALU.mult, ALU.add))
                V.tensor_scalar(y, y, SIN_MAX, -SIN_MAX, ALU.min, ALU.max).then_inc(S["filt_reduced"], 1)

            dve.wait_ge(S["filt_hidden"], 1)
            reduce_angle(ps[0:64, 7, 0:256], 0)
            dve.wait_ge(S["x_loaded"], 16)
            dve.wait_ge(S["consts_loaded"], 32)
            norm_dve(0)

            def p1_copy(g):
                dve.wait_ge(S["slot_multiplied"], 2 * g + 2)
                V.tensor_copy(P1[:, 1, g * 512:(g + 1) * 512], ps[:, 5 + 2 * (g % 2), :]).then_inc(S["p1_dve"], 1)

            dve.wait_ge(S["filt_sine"], 1)
            p1_copy(0)
            dve.wait_ge(S["filt_hidden"], 2)
            reduce_angle(ps[0:64, 0, 0:256], 1)
            p1_copy(1)
            dve.wait_ge(S["filt_window"], 1)
            for pt in range(TOK):
                dve.wait_ge(S["filt_product"], pt + 1)
                V.tensor_tensor(FH[:, pt, :], ps[:, 0:4, :].rearrange("p a b -> p (a b)"), FW[:, pt, :],
                                ALU.mult).then_inc(S["filt_windowed"], 1)
                p1_copy(2 + pt)
            dve.wait_ge(S["filt_windowed"], 2)
            dve.wait_ge(S["bias_loaded"], 16)
            step(V.memset(FH[0:1, 0, D:2 * D], 0.0))
            step(V.tensor_tensor(FH[0:1, 0, 0:D], FH[0:1, 0, 0:D], wrow[0:1, :], ALU.add))
            V.tensor_tensor(FAB[:, 0], FH[:, :, 0:D], FH[:, :, D:2 * D], ALU.add).then_inc(S["filt_ab"], 1)
            V.tensor_tensor(FAB[:, 1], FH[:, :, D:2 * D], FH[:, :, 0:D], ALU.subtract).then_inc(S["filt_ab"], 1)
            dve.wait_ge(S["tab_loaded"], 16)
            dve.wait_ge(S["p1_dve"], 3)
            src = P1[:, 1, 0:1280].rearrange("p (h c) -> p h c", h=20)
            lo, hi = src[:, :, 0:32], src[:, :, 32:64]
            c = cosT[:, 1, :].unsqueeze(1).broadcast_to([128, 20, 32])
            s = sinT[:, 1, :].unsqueeze(1).broadcast_to([128, 20, 32])
            V.tensor_tensor(RA, lo, c, ALU.mult)
            step(V.tensor_tensor(RB, hi, s, ALU.mult))
            step(V.tensor_tensor(R[:, 1, :, 0:32], RA, RB, ALU.subtract))
            V.tensor_tensor(RA, lo, s, ALU.mult)
            step(V.tensor_tensor(RB, hi, c, ALU.mult))
            V.tensor_tensor(R[:, 1, :, 32:64], RA, RB, ALU.add).then_inc(S["rope_ready"], 1)
            p1_copy(4)
            dve.wait_ge(S["slot_multiplied"], 11)
            V.tensor_copy(P1[:, 1, 2560:2816], ps[:, 7, 0:256]).then_inc(S["p1_dve"], 1)
            for b in range(1, 10, 2):
                dve.wait_ge(S["heads_transposed"], b + 1)
                V.tensor_scalar(RT[0:64, 2 * b:2 * b + 2, :].rearrange("p a b -> p (a b)"), ps[0:64, b % 4, :],
                                0.125 if 4 <= b < 8 else 1.0, None, ALU.mult).then_inc(S["heads_dve"], 1)
            dve.wait_ge(S["dup_transposed"], 1)
            dve.wait_ge(S["cmps_loaded"], 16)
            for kv in range(2):
                for a in range(2):
                    rows = slice(a * 64, a * 64 + 64)
                    tokens = ps[rows, 4 + kv, :].rearrange("p (g n b) -> p g n b", g=2, b=16)[:, :, a:a + NCMP, :]
                    pos = cmps[rows, kv * 16:kv * 16 + 16].unsqueeze(1).unsqueeze(1).broadcast_to([64, 2, NCMP, 16])
                    V.tensor_tensor(BLK[rows, kv].rearrange("p b (g n) -> p g n b", g=2), tokens, pos,
                                    ALU.add).then_inc(S["blocks_ready"], 1)
            for h in range(4):
                dve.wait_ge(S["ret_scores"], h + 1)
                V.tensor_tensor(SD[:, h, :], ps[:, h, 0:384], decay[:, h, :], ALU.mult).then_inc(S["ret_decayed"], 1)
            dve.wait_ge(S["cmp_product"], 1)
            V.tensor_tensor(KCR[0:64, :], ps[0:64, 4, 30:60], aux[0:64, T_CC + 30:T_CC + 60], ALU.mult)
            step(V.tensor_tensor(KCT[0:64, :], ps[0:64, 4, 0:30], aux[0:64, T_CC:T_CC + 30], ALU.mult))
            V.tensor_tensor(KCT[0:64, :], KCT[0:64, :], KCR[0:64, :], ALU.add).then_inc(S["kc_ready"], 1)
            dve.wait_ge(S["ret_out"], 1)
            o = ps[:, 6:8, :].rearrange("p a (h c) -> p (a h) c", h=4)

            def over(col, n, width):
                return stat[:, col:col + n].unsqueeze(2).broadcast_to([128, n, width])

            step(V.tensor_reduce(stat[:, ST_GSUM:ST_GSUM + 8], o, AX, ALU.add))
            step(V.tensor_scalar(stat[:, ST_GMEAN:ST_GMEAN + 8], stat[:, ST_GSUM:ST_GSUM + 8], 1.0 / 128, None, ALU.mult))
            V.tensor_tensor(gn, o, over(ST_GMEAN, 8, 128), ALU.subtract).then_inc(S["ret_normed"], 1)
            dve.wait_ge(S["cmp_scores"], 1)
            step(V.tensor_tensor(CE.rearrange("p t h n -> p t h n"),
                                 ps[:, 4, 0:240].rearrange("p (t h n) -> p t h n", t=2, h=8),
                                 drop.unsqueeze(2).broadcast_to([128, 2, 8, NCMP]), ALU.add))
            ce = CE.rearrange("p t h n -> p (t h) n")
            step(V.tensor_reduce(stat[:, ST_CMAX:ST_CMAX + 16], ce, AX, ALU.max))
            V.tensor_tensor(ce, ce, over(ST_CMAX, 16, NCMP), ALU.subtract).then_inc(S["cmp_shifted"], 1)
            step(V.tensor_tensor(gn2, gn, gn, ALU.mult))
            step(V.tensor_reduce(stat[:, ST_GVAR:ST_GVAR + 8], gn2, AX, ALU.add))
            step(V.tensor_scalar(stat[:, ST_GVAR:ST_GVAR + 8], stat[:, ST_GVAR:ST_GVAR + 8], 1.0 / 128, 1e-5, ALU.mult, ALU.add))
            V.reciprocal(stat[:, ST_GVAR:ST_GVAR + 8], stat[:, ST_GVAR:ST_GVAR + 8]).then_inc(S["gn_inv"], 1)
            dve.wait_ge(S["cmp_exp"], 1)
            V.tensor_tensor(CE, CE, keep.unsqueeze(2).broadcast_to([128, 2, 8, NCMP]), ALU.mult).then_inc(S["cmp_probs"], 1)
            dve.wait_ge(S["cmp_probs"], 1)
            step(V.tensor_reduce(stat[:, ST_CSUM:ST_CSUM + 16], ce, AX, ALU.add))
            step(V.tensor_scalar(stat[:, ST_CSUM:ST_CSUM + 16], stat[:, ST_CSUM:ST_CSUM + 16], 1e-30, None, ALU.max))
            step(V.reciprocal(stat[:, ST_CREC:ST_CREC + 16], stat[:, ST_CSUM:ST_CSUM + 16]))
            dve.wait_ge(S["gates_ready"], 1)
            step(V.tensor_tensor(stat[:, ST_CREC:ST_CREC + 16].rearrange("p (t h) -> p t h", t=2),
                                 stat[:, ST_CREC:ST_CREC + 16].rearrange("p (t h) -> p t h", t=2),
                                 P1[:, :, 2816:2824], ALU.mult))
            dve.wait_ge(S["gn_rstd"], 1)
            step(V.tensor_tensor(gn, gn, over(ST_GRSTD, 8, 128), ALU.mult))
            dve.wait_ge(S["gnw_loaded"], 16)
            g2 = gn.rearrange("p (t h) c -> p t (h c)", t=2)
            step(V.tensor_tensor(g2, g2, gnw.unsqueeze(1).broadcast_to([128, 2, 512]), ALU.mult))
            dve.wait_ge(S["silu_ready"], 1)
            V.tensor_tensor(mix[:, :, 0:512], g2, P1[:, :, 2048:2560], ALU.mult)

            causal = aux[:, T_CAUSAL:T_CAUSAL + 256]

            def maxima(u):
                qt = u // 2 % 2
                nk = 128 * (qt + 1)
                dve.wait_ge(S["att_scores"], u + 1)
                if u >= 2:
                    dve.wait_ge(S["att_transposed"], u - 1)
                for r in range(4):
                    col = r * nk
                    m = ST_MAX + 4 * (u % 2) + r
                    V.tensor_tensor_reduce(out=SM[:, u % 2, r, 0:nk],
                                           in0=ps[:, 2 * (u % 2) + col // 512, col % 512:col % 512 + nk],
                                           in1=causal[:, 256 - nk:256], scale=1.0, scalar=-3e38, op0=ALU.add, op1=ALU.max,
                                           accum_out=stat[:, m:m + 1]).then_inc(S["att_rowmax"], 1)
                dve.wait_ge(S["att_rowmax"], 4 * u + 4)
                m = 4 * (u % 2)
                V.tensor_scalar(stat[:, ST_NMAX + m:ST_NMAX + m + 4], stat[:, ST_MAX + m:ST_MAX + m + 4], -1.0, None,
                                ALU.mult).then_inc(S["att_max"], 1)

            maxima(0)
            dve.wait_ge(S["cmp_out"], 1)
            for t in range(TOK):
                V.tensor_tensor(mix[:, t, 512:1024].rearrange("p (h c) -> p h c", h=8),
                                ps[:, 4 + t, :].rearrange("p (h c) -> p h c", h=8),
                                over(ST_CREC + 8 * t, 8, 64), ALU.mult).then_inc(S["cmp_done"], 1)
            maxima(1)
            for u in range(8):
                if u // 2 % 2:
                    dve.wait_ge(S["att_transposed"], u + 1)
                    V.tensor_copy(ET[:, u % 2, 512:1024], ps[:, 5, :]).then_inc(S["att_copied_dve"], 1)
                if u + 2 < 8:
                    maxima(u + 2)
                if u % 2:
                    n = u // 2
                    qt, branch = n % 2, 1 + n // 2
                    rec, tmp = ST_REC + 8 * n, gn2[:, 0:4, :].rearrange("p a b -> p (a b)")
                    dve.wait_ge(S["att_exp"], 4 * u + 4)
                    step(V.reciprocal(stat[:, rec:rec + 8], stat[:, ST_SUM + 8 * n:ST_SUM + 8 * n + 8]))
                    step(V.tensor_tensor(stat[:, rec:rec + 8], stat[:, rec:rec + 8],
                                         P1[:, qt, 2816 + 8 * branch:2824 + 8 * branch], ALU.mult))
                    dve.wait_ge(S["att_out"], u + 1)
                    step(V.tensor_tensor(tmp.rearrange("p (h c) -> p h c", h=8),
                                         ps[:, 6 + n % 2, :].rearrange("p (h c) -> p h c", h=8), over(rec, 8, 64), ALU.mult))
                    dve.wait_ge(S["cmp_done"], 2)
                    V.tensor_tensor(mix[:, qt, 512:1024], mix[:, qt, 512:1024], tmp, ALU.add).then_inc(S["att_done"], 1)
                    dve.wait_ge(S["att_done"], n + 1)
            for b in (1, 3):
                dve.wait_ge(S["mix_transposed"], b + 1)
                V.tensor_copy(mixT[:, 2 * b:2 * b + 2, :].rearrange("p a b -> p (a b)"), ps[:, b, :]).then_inc(S["mixT_dve"], 1)

            def post_dve(k):
                inverse("post_squares", 2 * k + 2, "post_inv", k + 1)
                dve.wait_ge(S["rows_loaded"], 16 * k + 16)
                dve.wait_ge(S["post_rstd"], k + 1)
                for t in range(TOK):
                    V.scalar_tensor_tensor(xn[:, t, :], ps[:, 4 + 2 * t:6 + 2 * t, :].rearrange("p a b -> p (a b)"),
                                           stat[:, ST_RSTD + t:ST_RSTD + t + 1], wrow[:, :], ALU.mult,
                                           ALU.mult).then_inc(S["wrow_free"], 1)
                for t in range(TOK):
                    dve.wait_ge(S["wrow_free"], 2 * k + t + 1)
                    V.tensor_tensor(x[:, t, :], x[:, t, :], xn[:, t, :], ALU.add).then_inc(S["post_done"], 1)

            post_dve(0)
            norm_dve(1)

            def ffn_dve(i, it=None):
                dve.wait_ge(S["ffn_conv_act"], at(2 * i + 2, 8, it))
                for tap in (1, 0):
                    s = 2 - tap
                    for j in range(2):
                        col = at(V_CONV + (j * NFF + i) * 3 + tap, 12, it)
                        y = CONV[:, i % 2, j, s:256]
                        if tap == 0:
                            dve.wait_ge(S["ffn_tap"], at(2 * i + j + 1, 8, it))
                        V.scalar_tensor_tensor(y, ps[:, i % 4, j * 256:j * 256 + 256 - s], vecs[:, bass.ds(col, 1)], y,
                                               ALU.mult, ALU.add).then_inc(S["ffn_tap"] if tap else S["ffn_conv_dve"], 1)
                dve.wait_ge(S["ffn_gelu"], at(i + 1, 4, it))
                dve.wait_ge(S["ffn_conv_dve"], at(2 * i + 2, 8, it))
                V.tensor_tensor(HACT[:, i % 4, :], CONV[:, i % 2, 0, :], CONV[:, i % 2, 1, :],
                                ALU.mult).then_inc(S["ffn_gated"], 1)

            for i in range(6):
                ffn_dve(i)
            with dve.Fori(0, 4) as it:
                for i in range(6, 10):
                    ffn_dve(i, it)
            post_dve(1)
            dve_second(dve, step, inverse, norm_dve)



def shape_constants():
    import numpy as np
    f32 = np.float32
    t = np.arange(SEQ)
    inv = 1.0 / (10000.0 ** (np.arange(0, 64, 2) / 64.0))
    ang = t[:, None] * inv[None, :]
    cos = np.cos(ang).reshape(2, 128, 32).transpose(1, 0, 2)
    sin = np.sin(ang).reshape(2, 128, 32).transpose(1, 0, 2)
    decay = np.zeros((128, 4, 384))
    j, i = np.arange(128)[:, None], np.arange(256)[None, :]
    for h in range(4):
        lg = np.log(1.0 - 2.0 ** (-5.0 - h))
        full = np.where(i >= j, np.exp(lg * np.maximum(i - j, 0)), 0.0) * 64 ** -0.5
        decay[:, h, :256] = full
        decay[:, h, 256:] = full[:, :128]
    r = np.arange(128)
    tri = np.where(r[None, :] <= r[:, None], 0.0, -1e30)
    causal = np.concatenate([np.zeros((128, 128)), tri], 1)
    end = np.arange(NCMP) * 16 + 31
    keep = (end[None, None, :] <= (r[:, None] + 128 * np.arange(2)[None, :])[:, :, None]).astype(float)
    drop = np.where(keep > 0, 0.0, -1e30)
    cang = inv[:, None] * end[None, :]
    ccos = np.tile(np.cos(cang), (2, 2))
    csin = np.concatenate([-np.tile(np.sin(cang), (1, 2)), np.tile(np.sin(cang), (1, 2))], 0)
    cc = np.zeros((128, 60)); cc[:64, :30] = ccos; cc[:64, 30:] = csin
    tab1 = np.concatenate([a.reshape(128, -1) for a in (cos, sin, decay, causal, keep, drop, cc)], 1).astype(f32)
    ident = np.eye(128, dtype=f32)
    th = 2 * np.pi * np.outer(np.arange(256), np.arange(256) + 0.5) / 512
    def split(m):
        return m.reshape(2, 128, 256).transpose(1, 0, 2).reshape(128, 512)
    dft = np.concatenate([split(np.cos(th)), split(np.sin(th)), split(np.cos(th).T / 256), split(-np.sin(th).T / 256)], 1).astype(f32)
    bands = np.linspace(1e-4, 15, 16, dtype=f32).astype(float)
    fa = (2.0 * np.pi / SEQ) * t[:, None] * bands[None, :]
    tt = t / (SEQ - 1)
    z = np.concatenate([tt[:, None], np.cos(fa), -np.sin(fa)], 1)
    zt = np.zeros((128, 256 + 2)); zt[:33, :256] = z.T
    zt[:, 256:] = -tt.reshape(2, 128).T
    lv = np.zeros((128, 8, 128))
    for n, m in enumerate((64, 32, 16, 8, 4, 2, 1)):
        same = (r[:, None] // (2 * m)) == (r[None, :] // (2 * m))
        lv[:, n] = same & ((r[:, None] // m) != (r[None, :] // m))
    lv[:, 7] = np.eye(128)
    iota = np.tile(np.arange(128), (128, 1))
    return {"tab1": tab1, "ident": ident, "dft": dft, "zt": zt.astype(f32),
            "levels": lv.reshape(128, -1).astype(f32), "iota": iota.astype(f32)}


def lay_out(a):
    import numpy as np
    f32 = np.float32

    def token_major(w):
        n = w.shape[1] // 512
        return w.reshape(2, 4, 128, n, 512).transpose(3, 0, 2, 1, 4).reshape(2 * n, 128, 2048)

    def channel_major(w):
        n = w.shape[1] // 256
        return w.reshape(8, 128, n, 2, 128).transpose(2, 1, 3, 0, 4).reshape(n, 128, 2048)

    w = a["w_in"][0]
    c = np.cumsum([0, 256, 256, 512, 512, 512] + [128] * 6 + [24])
    rq, rk, rv, rg, nq, kcm, vcm, ksl, vsl, kwn, vwn, ng = [w[:, c[i]:c[i + 1]] for i in range(12)]
    head = np.concatenate([rq, rk, nq, ksl, kwn, kcm, vcm, rv, rg], 1)
    tail = np.concatenate([vsl, vwn], 1).reshape(8, 128, 256).transpose(1, 0, 2).reshape(1, 128, 2048)
    cmp1 = [a[n][0].reshape(2, 2, 8, 64, 256).transpose(1, 0, 3, 2, 4).reshape(2, 128, 2048)
            for n in ("cmp_k_w1", "cmp_v_w1")]
    up = a["ffn_w_up"][0].reshape(8, 128, 2, 22, 128).transpose(3, 1, 2, 0, 4).reshape(22, 128, 2048)
    down = a["ffn_w_down"][0].reshape(11, 2, 128, 1024).transpose(0, 2, 1, 3).reshape(11, 128, 2048)
    ffn = [up[0:2]]
    for p in range(1, 11):
        ffn += [up[2 * p:2 * p + 2], down[p - 1:p]]
    ffn += [down[10:11]]
    w2 = a["w_in_2"][0]
    q, zf, zb, inp, og, hy, gates = [w2[:, i:j] for i, j in ((0, 1024), (1024, 2048), (2048, 3072), (3072, 4096),
                                                             (4096, 5120), (5120, 8192), (8192, 10240))]
    peer_u = a["peer_u_2"][0].reshape(128, 64, 2, 8, 128).transpose(1, 4, 2, 3, 0).reshape(64, 128, 2048)
    peer_v = a["peer_v_2"][0].reshape(128, 64, 2048).transpose(1, 0, 2)
    stream = np.concatenate([token_major(head), tail] + cmp1 + [token_major(a["w_out"][0])] + ffn
                            + [channel_major(hy), channel_major(gates[:, 1024:]), channel_major(q), channel_major(zf),
                               channel_major(zb), token_major(inp), channel_major(og), channel_major(gates[:, :1024]),
                               channel_major(a["w_branch_b_2"][0]), channel_major(a["w_branch_a_2"][0]),
                               token_major(a["w_out_2"][0]), channel_major(a["peer_w_q_2"][0]), peer_u, peer_v], 0)

    def cols(v, n):
        return v.reshape(-1, n, 128).transpose(2, 1, 0).reshape(128, -1)

    pos = [a[n][0].reshape(2, 16, 64).transpose(0, 2, 1).reshape(128, 16) for n in ("cmp_k_pos", "cmp_v_pos")]
    w2k, w2v = a["cmp_k_w2"][0].reshape(2, 128, 64), a["cmp_v_w2"][0].reshape(2, 128, 64)
    w2r = np.concatenate([w2k[:, :, 32:], w2k[:, :, :32]], 2)
    filt = np.zeros((128, 132), f32)
    filt[:33, 0:64] = a["filt_w1_2"][0]
    filt[:64, 64:128] = a["filt_w2_2"][0]
    for n, name in enumerate(("filt_b1_2", "filt_freq1_2", "filt_b2_2", "filt_freq2_2")):
        filt[:64, 128 + n] = a[name][0]
    vecs = np.concatenate([
        cols(a["norm_mix_pre"][0], 8), cols(a["norm_ffn_pre"][0], 8), cols(a["norm_mix_g_2"][0], 8),
        cols(a["norm_ffn_g_2"][0], 8), cols(a["ffn_conv"][0], 44), cols(a["hyena_conv_w_2"][0], 24),
        cols(a["hyena_conv_b_2"][0], 24), cols(a["hgrn_lb_logits_2"], 8), a["hgrn_norm_g_2"][0].reshape(128, 1)], 1)
    cmps = np.concatenate(pos + [m.transpose(1, 0, 2).reshape(128, 128) for m in (w2k, w2r, w2v)]
                          + [ng.reshape(8, 128, 24).transpose(1, 0, 2).reshape(128, 192)], 1)
    rows = {n: np.broadcast_to(a[k].reshape(1, -1), (128, a[k].size)) for n, k in
            (("post1", "norm_mix_post"), ("post2", "norm_ffn_post"), ("final", "norm_final_g_2"), ("gnw", "ret_gn_w"),
             ("fdecay", "filt_decay_2"))}
    return {"x": a["x"][0].reshape(2, 128, 1024).transpose(1, 0, 2), "stream": stream, "vecs": vecs, "cmps": cmps,
            "filt": filt, "w3": a["filt_w3_2"][0], "bias": a["hyena_bias_2"].reshape(1, 1024),
            "subkeys": a["peer_subkeys_2"][0].transpose(3, 0, 1, 2).reshape(128, 2048), **rows}


def kernel(**inputs):
    import numpy as np
    import concourse.bacc as bacc
    from concourse import mybir
    from concourse.bass_utils import run_bass_kernel_spmd

    arrays = lay_out({k: np.asarray(v) for k, v in inputs.items()})
    arrays.update(shape_constants())
    nc = bacc.Bacc("TRN2", target_bir_lowering=False, num_devices=1)
    sent, dram = {}, {}
    for name, value in arrays.items():
        value = np.ascontiguousarray(value)
        sent[f"in_{name}"] = value
        dram[name] = nc.dram_tensor(f"in_{name}", value.shape, mybir.dt.float32, kind="ExternalInput").ap()
    dram["out"] = nc.dram_tensor("out_y", (128, 2, 1024), mybir.dt.float32, kind="ExternalOutput").ap()
    build(nc, dram)
    y = run_bass_kernel_spmd(nc, [sent], core_ids=[0]).results[0]["out_y"]
    return np.asarray(y).reshape(128, 2, 1024).transpose(1, 0, 2).reshape(1, 256, 1024)
```

```python
import concourse.bass as bass
from concourse import mybir
from contextlib import ExitStack

SEQ = 256
D = 1024
TOK = 2
KC = D // 128
NCMP = (SEQ - 32) // 16 + 1
RING = 6
HALF = 1024
NSLOT = 240
W_IN, W_CMP, W_OUT, W_FFN, W_HY, W_GB, W_QZ, W_V, W_OG, W_GA, W_BB, W_BA, W_OUT2, W_Q, W_PEER = (
    0, 11, 15, 19, 52, 64, 68, 80, 84, 88, 92, 96, 100, 104, 112)
WHOLE = (2 * W_CMP, 2 * (W_CMP + 4))
FIRST = {"norm0": 0, "mixed": 8, "norm1": 12, "norm2": 20, "hyena": 28, "hgrn": 29, "merged": 33, "norm3": 37,
         "experts": 45}
NJ = 128
NFF = 22
V_NORM, V_CONV, V_HYW, V_HYB, V_LB, V_GN = 0, 32, 164, 236, 260, 276
T_COS, T_SIN, T_DECAY, T_CAUSAL, T_KEEP, T_DROP, T_CC = 0, 64, 128, 1664, 1920, 1950, 1980
INV_2PI = 0.15915494309189535
ROUND = 12582912.0
PI2_A, PI2_B, PI2_C = 6.28125, 0.0019350051879882812, 3.019915981956e-07
SIN_MAX = 3.1415925

SEMS = """x_loaded consts_loaded cmps_loaded tab_loaded filt_loaded w3_loaded dft_loaded rows_loaded gnw_loaded split_hi
 split_lo ut_copied pt_copied gate_rest operand_hi ident_loaded gate_weights_ready gates_sigmoid
 gates_transposed o_scale operand_lo ffn_product ffn_rounded x_stored x_reloaded levels_loaded sk_loaded
 out_stored half_multiplied act_step dve_step pool_step squares_summed inv_ready rstd_ready xn_ready
 xn_transposed filt_hidden filt_sine filt_window filt_product filt_ab kernel_spectrum p1_act p1_dve
 gates_product gates_ready rope_ready heads_transposed heads_act heads_dve silu_ready dup_ready dup_transposed
 blocks_ready hid_ready cmp_product vc_copied kc_ready fdecay_loaded filt_windowed filt_reduced spectrum_copied
 cmp_shifted gn_inv gn_rstd ret_normed att_rowmax ffn_tap ret_scores ret_decayed ret_out cmp_scores cmp_exp
 cmp_probs cmp_ptrans cmp_pcopied cmp_out cmp_done att_scores att_max att_exp att_transposed att_copied_act
 att_copied_dve att_out att_done mix_transposed post_squares post_inv post_rstd post_done wrow_free ffn_gated
 ffn_conv_act ffn_conv_dve ffn_gelu""".split()


SEMS2 = """x_final ones_ready yb_ready scanned level_eq level_ek level_exp level_ready level_product level_act level_dve
 h_ready wq_taken ba_taken bb_taken channels_taken hy_dve hy_act hy_tap u_ready u_transposed u_spectrum
 u_spectrum_copied v_copied y_spectrum y_product o_product o_copied o_squared o_sums o_ready o_inverse o_rstd
 merged_ready mixer_added sim_product sim_copied routes_ready routes_transposed routes_copied routes_shifted
 routes_exp onehots onehot_j gate_product gated pt_transposed peer_added lb_shifted lb_exp lb_ready logs_ready
 keys_ready gates2_ready""".split()


def build(nc, dram):
    fp32 = mybir.dt.float32
    u32 = mybir.dt.uint32
    ALU = mybir.AluOpType
    ACT = mybir.ActivationFunctionType
    AX = mybir.AxisListType.X
    V, A, P = nc.vector, nc.scalar, nc.gpsimd

    ctx = ExitStack()
    with ctx:
        def sb(name, shape, dt=fp32):
            return ctx.enter_context(nc.sbuf_tensor(name, shape, dt))

        S = {name: ctx.enter_context(nc.semaphore(name)) for name in SEMS + SEMS2}
        arrived = [ctx.enter_context(nc.semaphore(f"slot_arrived_{n}")) for n in range(RING)]

        f32r = mybir.dt.float32r

        bf16 = mybir.dt.bfloat16

        def over_memory(name, base, shape, dtype=f32r):
            return nc.alloc_sbuf_tensor_at(name, shape, dtype, offset=base)

        first_free = (nc.sbuf_base + 31) // 32 * 32
        ring = sb("ring", [128, RING, HALF])
        ring_lo = over_memory("ring_lo", first_free, [128, RING, HALF])
        ring_hi = sb("ring_hi", [128, RING, HALF], f32r)
        x_at = (nc.sbuf_base + 31) // 32 * 32
        x = sb("x", [128, TOK, D])
        h_hi = over_memory("h_hi", x_at, [128, KC, SEQ])
        h_lo = sb("h_lo", [128, KC, SEQ], f32r)
        big_at = (nc.sbuf_base + 31) // 32 * 32
        big = sb("big", [128, 32768])
        ident = sb("identity", [128, 128])
        wrow_at = (nc.sbuf_base + 31) // 32 * 32
        wrow = sb("wrow", [128, D])
        vecs_at = (nc.sbuf_base + 31) // 32 * 32
        vecs = sb("vecs", [128, 277])
        aux_at = (nc.sbuf_base + 31) // 32 * 32
        aux = sb("aux", [128, 2300])
        stat = sb("stat", [128, 192])
        ps = ctx.enter_context(nc.psum_tensor("ps", [128, 8, 512], fp32))

        def area(off, *dims):
            n = 1
            for d in dims:
                n *= d
            v = big[:, off:off + n]
            if len(dims) == 2:
                v = v.rearrange("p (a b) -> p a b", a=dims[0])
            if len(dims) == 3:
                v = v.rearrange("p (a b c) -> p a b c", a=dims[0], b=dims[1])
            if len(dims) == 4:
                v = v.rearrange("p (a b c d) -> p a b c d", a=dims[0], b=dims[1], c=dims[2])
            return v

        KR, KI = area(0, 2, D), area(2048, 2, D)
        P1 = area(4096, TOK, 2840)
        RT = area(9776, 20, SEQ)
        R = area(14896, TOK, 20, 64)
        RA, RB = area(17456, 20, 32), area(18096, 20, 32)
        RC, RD = area(18736, 20, 32), area(19376, 20, 32)
        xn = area(20016, TOK, D)
        SCR = 22064
        FH = area(SCR, TOK, 2048)
        FW = area(SCR + 4096, TOK, 2048)
        FAB = area(SCR + 4096, 2, TOK, D)
        DF1 = area(SCR + 8192, 4, 256)
        DUP = area(SCR, TOK, 4, 2, 64)
        BLK = area(SCR + 1024, 2, 16, 30)
        HID = area(SCR + 1984, 2, 2, 30)
        KCR = area(SCR + 2104, 30)
        KCT = area(SCR + 2134, 30)
        VC = area(SCR + 2164, 2, 64)
        SD = area(SCR + 2304, 4, 384)
        SM = area(SCR + 3840, 2, 4, 256)
        ET = area(SCR + 5888, 2, 1024)
        CE = area(SCR + 7936, TOK, 8, NCMP)
        CET = area(SCR + 8176, TOK * 8 * 128)
        mix = area(14896, TOK, D)
        gn = area(20016, TOK * 4, 128)
        gn2 = area(17456, TOK * 4, 128)
        cosT = aux[:, T_COS:T_COS + 64].rearrange("p (t c) -> p t c", t=2)
        sinT = aux[:, T_SIN:T_SIN + 64].rearrange("p (t c) -> p t c", t=2)
        decay = aux[:, T_DECAY:T_DECAY + 1536].rearrange("p (h c) -> p h c", h=4)
        keep = aux[:, T_KEEP:T_KEEP + 30].rearrange("p (t c) -> p t c", t=2)
        drop = aux[:, T_DROP:T_DROP + 30].rearrange("p (t c) -> p t c", t=2)
        cmps = area(SCR + 8192, 416)
        w2k = cmps[:, 32:160].rearrange("p (h c) -> p h c", h=2)
        w2r = cmps[:, 160:288].rearrange("p (h c) -> p h c", h=2)
        w2v = cmps[:, 288:416].rearrange("p (h c) -> p h c", h=2)
        ZT = area(SCR + 9216, 258)
        FT = area(SCR + 9474, 132)
        FHID = area(SCR + 9606, 2, 256)
        FTMP = area(SCR + 10118, 2, 256)
        W3 = area(9776, 2048)
        gnw = area(21040, 512)
        gate_columns = area(21552, 8, 24)
        gate_weights = (over_memory("gate_weights_hi", big_at + 4 * 21744, [128, 8, 24]),
                        over_memory("gate_weights_lo", big_at + 4 * 21552, [128, 8, 24]))
        gates_T = area(SCR + 10118, SEQ)
        ST_SQ, ST_INV, ST_RSTD = 0, 2, 4
        ST_GSUM, ST_GMEAN, ST_GVAR, ST_GRSTD = 8, 16, 24, 32
        ST_CMAX, ST_CSUM, ST_CREC, ST_MAX, ST_NMAX, ST_SUM, ST_REC = 40, 56, 72, 88, 96, 104, 136
        ST_UNUSED = 184
        CONV = area(SCR, 3, 2, 256)
        ffn_hi = over_memory("ffn_hi", big_at + 4 * (SCR + 1536), [128, 4, SEQ])
        ffn_lo = over_memory("ffn_lo", big_at + 4 * (SCR + 2560), [128, 4, SEQ])
        
        in_parts = (h_hi, h_lo)

        def dve_copies(u):
            return 2 * (u // 4) + max(0, u % 4 - 2)

        def Z(n, *dims):
            return area(2048 * n, *dims)

        lbs = sb("lower_bounds", [128, 40])
        LBE, LBM, LB, OML = lbs[:, 0:16].rearrange("p (c r) -> p c r", r=2), lbs[:, 16:24], lbs[:, 24:32], lbs[:, 32:40]
        levels = aux[:, 0:1024].rearrange("p (l c) -> p l c", l=8)
        ones_row = aux[:, 1024:1280]
        strip = aux[:, 1280:1295]
        XH = Z(2, 24, SEQ)
        X0, X1, U = Z(2, 8 * SEQ), Z(3, 8 * SEQ), Z(4, 8 * SEQ)
        UC = Z(4, 8, SEQ)
        UT = Z(3, TOK, D)
        UR, UI, YT = Z(5, 2 * D), Z(6, 2 * D), Z(7, 2 * D)
        YR, YI = Z(4, 2, D), Z(3, 2, D)
        DFT = Z(15, 8, SEQ)
        YB = Z(5, 8, SEQ)
        MERGED = Z(3, 8, SEQ)
        GB, Q, KF, KB = Z(8, 8, SEQ), Z(9, 8, SEQ), Z(10, 8, SEQ), Z(11, 8, SEQ)
        VT = Z(12, TOK, D)
        LF, LBW = Z(13, 8, SEQ), Z(14, 8, SEQ)
        OG, GA = Z(13, 8, SEQ), Z(14, 8, SEQ)
        BF, DB = Z(0, 8, SEQ), Z(1, 8, SEQ)
        LV = [Z(6, 2, 1024), Z(7, 2, 1024)]
        AT = [Z(15, 4, 2, SEQ), Z(2, 4, 2, SEQ)]
        OT = Z(4, 8, SEQ)
        SQ = Z(2, 8, SEQ)
        RS = Z(5, SEQ)
        BTMP = Z(7, 2, 512)
        NLV = 18

        def taken(idx):
            for first, name, per in ((52, "h_ready", 1), (44, "wq_taken", 1), (40, "ba_taken", 1), (36, "bb_taken", 1),
                                     (12, "channels_taken", 1), (0, "hy_dve", 2)):
                if idx >= first:
                    return S[name], per * (idx - first + 1)

        def slot_of(idx):
            return idx + (W_HY if idx < 28 else W_OG - 28 if idx < 44 else W_Q - 44)

        def refill(n):
            return 2 * (W_OG + 2 * ((n - 3) // 3) + n % 3) + RING

        def level_view(a, hg, m):
            f = a.rearrange("p h t -> p (h t)")[:, hg * 1024:(hg + 1) * 1024]
            return f.rearrange("p (n two m) -> p n two m", two=2, m=m)

        def split_view(f, m):
            return f.rearrange("p (n two m) -> p n two m", two=2, m=m)

        def level_dve(n):
            return n - n // 9

        H = area(0, NJ, SEQ)
        QT = Z(8, 16, SEQ)
        SK = Z(10, 2048)
        SC = Z(11, TOK, 16, 128)
        CS = Z(13, TOK, 8, 256)
        EQ = Z(15, 2048)
        T1V = aux[:, 0:512].rearrange("p (t g k) -> p t g k", t=2, g=16)
        T1I = aux[:, 512:1024].bitcast(u32).rearrange("p (t g k) -> p t g k", t=2, g=16)
        T1F = wrow[:, 0:512].rearrange("p (t g k) -> p t g k", t=2, g=16)
        TV = aux[:, 1024:1280].rearrange("p (g k) -> p g k", g=16)
        TP = aux[:, 1280:1536].bitcast(u32).rearrange("p (g k) -> p g k", g=16)
        PA = aux[:, 1536:2048].rearrange("p (s g) -> p s g", s=2)
        PAI = EQ[:, 0:512].bitcast(u32).rearrange("p (s g) -> p s g", s=2)
        iota = aux[:, 2048:2176]
        IX = wrow[:, 512:1024].rearrange("p (s t g) -> p s t g", s=2, t=2)
        ROUTE = over_memory("routes", wrow_at, [128, 5, SEQ], bf16)
        OA = over_memory("onehots_i", aux_at, [128, 2, 4, 128], bf16)
        OB = over_memory("onehots_j", aux_at + 2048, [128, 2, 3, 4, 64], bf16)
        ONEHOT_J = over_memory("onehot_j", vecs_at, [128, 4, 64], bf16)
        GATE = vecs[:, 0:256]
        iota_short = over_memory("iota_short", aux_at + 4 * 2176, [128, 128], bf16)
        PT = area(0, KC, SEQ)
        ONEHOT_J = vecs[:, 0:256].rearrange("p (t j) -> p t j", t=4)

        def two_parts(name, n_hi, n_lo):
            return tuple(over_memory(f"{name}_{part}", big_at + 4 * 2048 * n, [128, KC, SEQ])
                         for part, n in (("hi", n_hi), ("lo", n_lo)))

        hgrn_parts = two_parts("hgrn", 9, 10)
        merged_parts = two_parts("merged", 0, 1)

        def pool_second(pool, rests):
            pool.dma_start(aux[:, 0:1024], dram["levels"]).then_inc(S["levels_loaded"], 16)
            pool.dma_start(DFT.rearrange("p a b -> p (a b)"), dram["dft"]).then_inc(S["dft_loaded"], 16)
            P.memset(ones_row, 1.0).then_inc(S["ones_ready"], 1)
            P.memset(strip[:, 0:7], 0.0)
            P.memset(strip[:, 8:15], 0.0)
            P.memset(strip[:, 7:8], 1.0).then_inc(S["ones_ready"], 1)
            rests(2 * W_FFN + 6, 2 * W_OG + 6)
            pool.wait_ge(S["y_spectrum"], 2)
            pool.wait_ge(S["scanned"], 16)
            for n in range(NLV):
                hg, m = n // 9, 128 >> (n % 9)
                if n % 9 != 8:
                    if n >= 2:
                        pool.wait_ge(S["level_product"], n - 1)
                    v = split_view(LV[n % 2][:, 1, :], m)
                    f, d = level_view(BF, hg, m), level_view(DB, hg, m)
                    nb = 512 // m
                    P.tensor_tensor(v[:, :, 0, :], d[:, :, 1, 0:1].broadcast_to([128, nb, m]), d[:, :, 0, :],
                                    ALU.subtract).then_inc(S["level_eq"], 1)
                    P.tensor_tensor(v[:, :, 1, :], f[:, :, 1, :], f[:, :, 0, m - 1:m].broadcast_to([128, nb, m]),
                                    ALU.subtract).then_inc(S["level_eq"], 1)
                if n % 3 != 2 and n >= 3:
                    rests(refill(n), refill(n) + 2)
            rests(2 * (W_BA + 1), 2 * W_Q + 6)
            pool.wait_ge(S["xn_transposed"], 16)
            pool.dma_start(SK, dram["subkeys"]).then_inc(S["sk_loaded"], 16)
            pool.dma_start(iota, dram["iota"]).then_inc(S["sk_loaded"], 16)
            v_half = 2 * (W_PEER + 96)
            rests(2 * W_Q + 6, v_half + 2)
            pool.wait_ge(S["gated"], 128)
            pool.dma_start(wrow[:, :], dram["final"]).then_inc(S["rows_loaded"], 16)
            rests(v_half + 2, 2 * NSLOT)

        def pe_second(pe, weights, multiplied, parts, norm_transposes, wait_operand, wait_normed, token_product, out_product):
            def channels(idx, it=None, src=in_parts, ready=None):
                if idx >= 3:
                    sem, value = taken(idx - 3)
                    pe.wait_ge(sem, at(value, 3, it))
                for j in range(2):
                    w = weights(slot_of(idx), j, it)
                    for k in range(KC):
                        if ready and j == 0:
                            ready(k)
                        last = product(ps[:, idx % 3, j * 256:(j + 1) * 256], parts(w, ALL, tile(k)),
                                       parts(src, ALL, k, ALL), k == 0, k == KC - 1)
                    multiplied(last)

            norm_transposes(2)
            for idx in range(12):
                channels(idx, ready=None if idx else lambda k: wait_normed(2, k, 0))
            for idx in range(12, 16):
                channels(idx)
            pe.wait_ge(S["u_ready"], 1)
            for t in range(TOK):
                for c in range(KC):
                    last = nc.tensor.transpose(ps[:, 4 + 2 * t + c // 4, (c % 4) * 128:(c % 4 + 1) * 128],
                                               UC[:, c, t * 128:(t + 1) * 128], ident[:, :])
                last.then_inc(S["u_transposed"], 1)
            for idx in range(16, 20):
                channels(idx)
            pe.wait_ge(S["ut_copied"], 2)
            pe.wait_ge(S["dft_loaded"], 32)
            for part in range(2):
                if part:
                    pe.wait_ge(S["u_spectrum_copied"], 1)
                for ft in range(2):
                    for nh in range(2):
                        for t in range(TOK):
                            last = mm(ps[:, 4 + ft * 2 + nh, :], DFT[:, part * 2 + t, ft * 128:(ft + 1) * 128],
                                      UT[:, t, nh * 512:(nh + 1) * 512], t == 0, t == 1)
                last.then_inc(S["u_spectrum"], 1)
                for idx in range(20 + 2 * part, 22 + 2 * part):
                    channels(idx)
            for idx in range(24, 28):
                channels(idx)
            pe.wait_ge(S["u_spectrum_copied"], 2)
            token_product(W_V, 4, in_parts)
            token_product(W_V + 2, 6, in_parts)
            pe.wait_ge(S["v_copied"], 4)
            pe.wait_ge(S["y_spectrum"], 2)
            for c in range(KC):
                for n, (y, ft) in enumerate(((YR, 0), (YR, 1), (YI, 0), (YI, 1))):
                    last = mm(ps[:, 4 + c // 2, (c % 2) * 256:(c % 2 + 1) * 256], y[:, ft, c * 128:(c + 1) * 128],
                              DFT[:, 4 + n, :], n == 0, n == 3)
            last.then_inc(S["y_product"], 1)

            def level(n):
                hg = n // 9
                pe.wait_ge(S["level_ready"], n + 1)
                if n >= 2:
                    if (n - 2) % 9 == 0:
                        pe.wait_ge(S["level_act"], (n - 2) // 9 + 1)
                    else:
                        pe.wait_ge(S["level_dve"], level_dve(n - 2))
                for st in range(2):
                    tt = st if n % 9 else 1 - st
                    for h in range(4):
                        keys = LV[n % 2][:, 0, h * 256 + st * 128:h * 256 + st * 128 + 128]
                        if n % 9 == 8:
                            queries = Q[:, 4 * hg + h, tt * 128:(tt + 1) * 128]
                        else:
                            queries = LV[n % 2][:, 1, h * 256 + tt * 128:h * 256 + tt * 128 + 128]
                        last = mm(ps[:, 4 + 2 * (n % 2) + st, h * 128:(h + 1) * 128], keys, queries)
                last.then_inc(S["level_product"], 1)

            def values(hg):
                if hg == 0:
                    pe.wait_ge(S["level_act"], 1)
                    pe.wait_ge(S["level_dve"], 8)
                else:
                    pe.wait_ge(S["level_act"], 2)
                    pe.wait_ge(S["level_dve"], 16)
                for pair in range(2):
                    if hg or pair:
                        pe.wait_ge(S["o_copied"], 2 * hg + pair)
                    for hh in range(2):
                        h = 2 * pair + hh
                        for st in range(2):
                            last = mm(ps[:, 3, hh * 256:(hh + 1) * 256], VT[:, st, (4 * hg + h) * 128:(4 * hg + h + 1) * 128],
                                      AT[hg][:, h, st, :], st == 0, st == 1)
                    last.then_inc(S["o_product"], 1)

            idx = 28
            for n in range(NLV):
                if n:
                    level(n)
                if n % 3 != 2:
                    if idx == 36:
                        wait_operand("hyena", 1)
                    channels(idx)
                    idx += 1
                if n == 0:
                    pe.wait_ge(S["yb_ready"], 1)
                    level(n)
                if n == 11:
                    values(0)
            values(1)
            pe.wait_ge(S["o_squared"], 1)
            pe.wait_ge(S["ones_ready"], 2)
            pe.wait_ge(S["level_dve"], 16)
            for h in range(8):
                last = mm(ps[0:8, 4, 0:SEQ], strip[:, 7 - h:15 - h], SQ[:, h, :], h == 0, h == 7)
            last.then_inc(S["o_sums"], 1)
            pe.wait_ge(S["o_rstd"], 1)
            for h in range(8):
                last = mm(ps[:, 4 + h // 2, (h % 2) * 256:(h % 2 + 1) * 256],
                          ident[0:8, h:h + 1].broadcast_to([8, 128]), RS[0:8, :])
                if h % 2:
                    last.then_inc(S["o_scale"], 1)
            for idx in range(40, 44):
                channels(idx, src=hgrn_parts, ready=None if idx > 40 else lambda k: wait_operand("hgrn", k // 2 + 1))
            out_product(W_OUT2, merged_parts, lambda quarter: wait_operand("merged", quarter + 1))
            norm_transposes(3)
            for idx in range(44, 52):
                channels(idx, ready=None if idx > 44 else lambda k: wait_normed(3, k, 44 % 3))
            pe.wait_ge(S["wq_taken"], 8)
            pe.wait_ge(S["sk_loaded"], 32)
            for t in range(TOK):
                if t:
                    pe.wait_ge(S["sim_copied"], 1)
                for g in range(16):
                    last = mm(ps[:, 4 + g // 4, (g % 4) * 128:(g % 4 + 1) * 128], QT[:, g, t * 128:(t + 1) * 128],
                              SK[:, g * 128:(g + 1) * 128])
                last.then_inc(S["sim_product"], 1)
            def experts(s, it=None):
                channels(52 + s, it)

            for s in range(5):
                experts(s)
            with pe.Fori(0, 6) as it:
                for s in range(5, 8):
                    experts(s, it)
            pe.wait_ge(S["routes_ready"], 1)
            pe.wait_ge(S["sim_copied"], 2)
            for t in range(TOK):
                nc.tensor.transpose(ps[:, 4, t * 128:(t + 1) * 128], IX[:, 0, t, :], ident[:, :])
                nc.tensor.transpose(ps[:, 4, 256 + t * 128:256 + (t + 1) * 128], IX[:, 1, t, :], ident[:, :])
                last = nc.tensor.transpose(ps[:, 5, t * 128:(t + 1) * 128],
                                           TV[:, 8 * t:8 * t + 8, :].rearrange("p g k -> p (g k)"), ident[:, :])
            last.then_inc(S["routes_transposed"], 1)
            with pe.Fori(0, 3) as it:
                for s in range(23, 26):
                    experts(s, it)
            pe.wait_ge(S["gate_rest"], 1)

            def gates(q, parity, bank, it=None):
                pe.wait_ge(S["onehots"], at(q + 1, 6, it))
                if q >= 2:
                    pe.wait_ge(S["gated"], at(q - 1, 6, it))
                for tk in range(4):
                    for part in range(3):
                        last = mm(ps[:, bank, tk * 64:(tk + 1) * 64], OA[:, parity, tk, :], OB[:, parity, part, tk, :],
                                  part == 0, part == 2)
                last.then_inc(S["gate_product"], 1)

            for s in range(2):
                experts(32 + s)
                for e in range(2):
                    gates(2 * s + e, e, 3 + e)
            with pe.Fori(0, 10) as it:
                for s in range(2, 5):
                    experts(32 + s, it)
                    for e in range(2):
                        gates(2 * s + e, e, 3 + e, it)

            def down(s, it=None):
                for sem in ("operand_hi", "operand_lo"):
                    pe.wait_ge(S[sem], at(FIRST["experts"] + s + 1, 3, it))
                for jj in range(2):
                    w = weights(W_PEER + 64 + s, jj, it)
                    for c in range(KC):
                        first = s == 0 and jj == 0 and it is None
                        last = product(ps[:, 4 + c // 2, (c % 2) * 256:(c % 2 + 1) * 256], parts(w, ALL, tile(c)),
                                       parts(in_parts, ALL, 2 * (s % 3) + jj, ALL),
                                       first and c % 2 == 0, s == 63 and jj == 1)
                    multiplied(last)

            pe.wait_ge(S["gated"], 64)
            pe.wait_ge(S["h_ready"], 64)
            for s in range(2):
                down(s)
                for e in range(2):
                    gates(64 + 2 * s + e, e, e)
            with pe.Fori(0, 10) as it:
                for s in range(2, 5):
                    down(s, it)
                    for e in range(2):
                        gates(64 + 2 * s + e, e, e, it)
            pe.wait_ge(S["gated"], 128)
            with pe.Fori(0, 10) as it:
                for s in range(32, 35):
                    down(s, it)
            down(62)
            down(63)
            pe.wait_ge(S["pt_copied"], 2)
            for t in range(TOK):
                for c in range(KC):
                    last = nc.tensor.transpose(ps[:, 2 * t + c // 4, (c % 4) * 128:(c % 4 + 1) * 128],
                                               PT[:, c, t * 128:(t + 1) * 128], ident[:, :])
                last.then_inc(S["pt_transposed"], 1)

        def act_second(act, split, ahead, round_to, load_roots, reload, norm_act):
            norm_act(2)
            act.wait_ge(S["lb_shifted"], 1)
            A.activation(LBE, LBE, ACT.Exp).then_inc(S["lb_exp"], 1)

            def hyena(s):
                ahead(2 * slot_of(s) + 5)
                act.wait_ge(S["half_multiplied"], 2 * slot_of(s) + 2)
                for j in range(2):
                    c = 2 * s + j
                    A.activation(XH[:, c, :], ps[:, s % 3, j * 256:(j + 1) * 256], ACT.Identity,
                                 bias=vecs[:, V_HYB + c:V_HYB + c + 1],
                                 scale=vecs[:, V_HYW + 3 * c + 1:V_HYW + 3 * c + 2]).then_inc(S["hy_act"], 1)

            for s in range(12):
                hyena(s)

            def take(idx, dst, func, second=None):
                ahead(2 * slot_of(idx) + 5)
                act.wait_ge(S["half_multiplied"], 2 * slot_of(idx) + 2)
                src = ps[:, idx % 3, :]
                s = 2 * (idx % 4)
                if second is not None:
                    A.activation(second[:, s:s + 2, :].rearrange("p a b -> p (a b)"), src, func, scale=-1.0)
                A.activation(dst[:, s:s + 2, :].rearrange("p a b -> p (a b)"), src, func).then_inc(S["channels_taken"], 1)

            for idx in range(12, 16):
                take(idx, GB, ACT.Sigmoid)
            act.wait_ge(S["u_transposed"], 1)
            act.wait_ge(S["u_transposed"], 2)
            A.copy(UT[:, 0, :], ps[:, 4:6, :].rearrange("p a b -> p (a b)")).then_inc(S["ut_copied"], 1)
            for idx in range(16, 20):
                take(idx, Q, ACT.Silu)
            act.wait_ge(S["u_spectrum"], 1)
            A.copy(UR, ps[:, 4:8, :].rearrange("p a b -> p (a b)")).then_inc(S["u_spectrum_copied"], 1)
            take(20, LF, ACT.Sigmoid, KF)
            take(21, LF, ACT.Sigmoid, KF)
            act.wait_ge(S["u_spectrum"], 2)
            A.mul(UI, ps[:, 4:8, :].rearrange("p a b -> p (a b)"), -1.0).then_inc(S["u_spectrum_copied"], 1)
            take(22, LF, ACT.Sigmoid, KF)
            take(23, LF, ACT.Sigmoid, KF)
            for idx in range(24, 28):
                take(idx, LBW, ACT.Sigmoid, KB)
            act.wait_ge(S["lb_ready"], 1)
            act.wait_ge(S["channels_taken"], 16)
            for logs in (LF, LBW):
                ahead(2 * W_V + (5 if logs is LF else 7))
                for c in range(8):
                    A.activation(logs[:, c, :], logs[:, c, :], ACT.Ln, bias=LB[:, c:c + 1],
                                 scale=OML[:, c:c + 1]).then_inc(S["logs_ready"], 1)
            for g in range(2):
                ahead(2 * (W_V + 2 * g) + 9)
                act.wait_ge(S["half_multiplied"], 2 * (W_V + 2 * g + 2))
                for t in range(TOK):
                    A.copy(VT[:, t, g * 512:(g + 1) * 512], ps[:, 4 + 2 * g + t, :]).then_inc(S["v_copied"], 1)
            idx = 28
            for n in range(NLV):
                if n % 9 != 8:
                    for part, ready in enumerate(("level_ek", "level_eq")):
                        act.wait_ge(S[ready], 2 * (n - n // 9) + 2)
                        lv = LV[n % 2][:, part, :]
                        A.activation(lv, lv, ACT.Exp).then_inc(S["level_exp"], 1)
                if n == 12:
                    for pair in range(2):
                        act.wait_ge(S["o_product"], pair + 1)
                        A.copy(OT[:, 2 * pair:2 * pair + 2, :].rearrange("p a b -> p (a b)"),
                               ps[:, 3, :]).then_inc(S["o_copied"], 1)
                if n % 3 != 2 and n >= 3:
                    ahead(refill(n) + 1)
                if n % 9 == 1:
                    hg = n // 9
                    act.wait_ge(S["level_product"], n)
                    if hg == 0:
                        act.wait_ge(S["scanned"], 16)
                    b = 4 + 2 * ((n - 1) % 2)
                    for st in range(2):
                        ins = A.copy(AT[hg][:, :, st, (1 - st) * 128:(2 - st) * 128],
                                     ps[:, b + st, :].rearrange("p (h c) -> p h c", h=4))
                    ins.then_inc(S["level_act"], 1)
                if n >= 2 and (n - 2) % 3 != 2 and idx < 36:
                    if idx == 28:
                        act.wait_ge(S["scanned"], 16)
                    take(idx, OG if idx < 32 else GA, ACT.Copy)
                    idx += 1
                if n == 15:
                    act.wait_ge(S["channels_taken"], 24)
                    A.activation(GA, GA, ACT.Sigmoid).then_inc(S["gates2_ready"], 1)
                    A.activation(OG, OG, ACT.Silu).then_inc(S["gates2_ready"], 1)
            ahead(2 * W_BA + 3)
            reload(dram["residual"], 2 * W_BA)
            load_roots(3)
            for pair in range(2, 4):
                act.wait_ge(S["o_product"], pair + 1)
                A.copy(OT[:, 2 * pair:2 * pair + 2, :].rearrange("p a b -> p (a b)"), ps[:, 3, :]).then_inc(S["o_copied"], 1)
            act.wait_ge(S["o_copied"], 4)
            act.wait_ge(S["level_product"], NLV)
            A.activation(SQ, OT, ACT.Square).then_inc(S["o_squared"], 1)
            act.wait_ge(S["o_inverse"], 1)
            A.activation(RS[0:8, :], RS[0:8, :], ACT.Sqrt).then_inc(S["o_rstd"], 1)
            for n in range(4):
                act.wait_ge(S["o_ready"], n + 1)
                round_to(hgrn_parts[0][:, 2 * n:2 * n + 2, :], OT[:, 2 * n:2 * n + 2, :])
            for s in range(4):
                ahead(2 * (W_BA + s) + 5)
                act.wait_ge(S["merged_ready"], s + 1)
                round_to(merged_parts[0][:, 2 * s:2 * s + 2, :], MERGED[:, 2 * s:2 * s + 2, :])
            ahead(2 * W_Q + 3)
            norm_act(3)
            for s in range(8):
                ahead(2 * (W_Q + s) + 5)
                act.wait_ge(S["half_multiplied"], 2 * (W_Q + s + 1))
                A.copy(QT[:, 2 * s:2 * s + 2, :].rearrange("p a b -> p (a b)"), ps[:, (44 + s) % 3, :]).then_inc(S["wq_taken"], 1)
            for t in range(TOK):
                act.wait_ge(S["sim_product"], t + 1)
                A.copy(SC[:, t].rearrange("p a b -> p (a b)"), ps[:, 4:8, :].rearrange("p a b -> p (a b)")).then_inc(S["sim_copied"], 1)

            def activations(s, it=None):
                n = W_PEER + s
                for h in (2 * n + 4, 2 * n + 5):
                    split(h, it)
                act.wait_ge(S["half_multiplied"], at(2 * n + 2, 6, it))
                j = at(2 * s, 6, it)
                A.activation(H[:, bass.ds(j, 2), :].rearrange("p a b -> p (a b)"), ps[:, (52 + s) % 3, :],
                             ACT.Gelu_apprx_tanh).then_inc(S["h_ready"], 1)

            for s in range(5):
                activations(s)
            with act.Fori(0, 5) as it:
                for s in range(5, 8):
                    activations(s, it)
            act.wait_ge(S["routes_shifted"], 1)
            A.activation(TV, TV, ACT.Exp).then_inc(S["routes_exp"], 1)
            for s in range(20, 23):
                activations(s)
            act.wait_ge(S["routes_transposed"], 1)
            A.copy(ROUTE[:, 0:2, :].rearrange("p s t -> p (s t)"), ps[:, 4, :]).then_inc(S["routes_copied"], 1)
            A.copy(ROUTE[:, 2, :], ps[:, 5, 0:256]).then_inc(S["routes_copied"], 1)
            with act.Fori(0, 3) as it:
                for s in range(23, 26):
                    activations(s, it)
            for s in range(32, 34):
                activations(s)
            with act.Fori(0, 10) as it:
                for s in range(34, 37):
                    activations(s, it)

            def round_activations(s, it=None):
                act.wait_ge(S["half_multiplied"], at(2 * (W_PEER + 64 + max(s - 2, 0)), 6, it))
                round_to(h_hi[:, 2 * (s % 3):2 * (s % 3) + 2, :].rearrange("p a b -> p (a b)"),
                         H[:, bass.ds(at(2 * s, 6, it), 2), :].rearrange("p a b -> p (a b)"))
                if s not in (0, 63):
                    split(2 * (W_PEER + 64 + s) + 2, it)
                    split(2 * (W_PEER + 64 + s) + 3, it)

            act.wait_ge(S["gated"], 64)
            round_activations(0)
            round_activations(1)
            with act.Fori(0, 10) as it:
                for s in range(2, 5):
                    round_activations(s, it)
            act.wait_ge(S["gated"], 128)
            with act.Fori(0, 10) as it:
                for s in range(32, 35):
                    round_activations(s, it)
            round_activations(62)
            round_activations(63)
            load_roots(4)
            reload(dram["residual"], 2 * NSLOT)
            act.wait_ge(S["half_multiplied"], 2 * NSLOT)
            A.copy(PT[:, 0:4, :].rearrange("p a b -> p (a b)"), ps[:, 4:6, :].rearrange("p a b -> p (a b)")).then_inc(S["pt_copied"], 1)
            junk = area(4096, TOK, D)
            for t in range(TOK):
                act.wait_ge(S["peer_added"], t + 1)
                A.activation(junk[:, t, :], x[:, t, :], ACT.Square,
                             accum_out=stat[:, ST_SQ + t:ST_SQ + t + 1]).then_inc(S["squares_summed"], 1)
            act.wait_ge(S["inv_ready"], 5)
            A.activation(stat[:, ST_RSTD:ST_RSTD + 2], stat[:, ST_INV:ST_INV + 2], ACT.Sqrt).then_inc(S["rstd_ready"], 1)

        def dve_second(dve, step, inverse, wait_rounded, rest_of, norm_dve):
            norm_dve(2)
            logits = vecs[:, V_LB:V_LB + 16].rearrange("p (c r) -> p c r", r=2)
            step(V.tensor_tensor(LBM, logits[:, :, 0], logits[:, :, 1], ALU.max))
            V.tensor_tensor(LBE, logits, LBM.unsqueeze(2).broadcast_to([128, 8, 2]), ALU.subtract).then_inc(S["lb_shifted"], 1)
            dve.wait_ge(S["lb_exp"], 1)
            step(V.tensor_tensor(LBM, LBE[:, :, 0], LBE[:, :, 1], ALU.add))
            step(V.reciprocal(LBM, LBM))
            step(V.tensor_tensor(LB, LBE[:, :, 0], LBM, ALU.mult))
            V.tensor_scalar(OML, LB, -1.0, 1.0, ALU.mult, ALU.add).then_inc(S["lb_ready"], 1)
            for s in range(12):
                dve.wait_ge(S["hy_act"], 2 * s + 2)
                for tap, sem in ((0, "hy_tap"), (2, "hy_dve")):
                    for j in range(2):
                        c = 2 * s + j
                        if tap:
                            dve.wait_ge(S["hy_tap"], 2 * s + j + 1)
                        lo, hi = (1, 0) if tap == 0 else (0, 1)
                        y = XH[:, c, lo:lo + 255]
                        V.scalar_tensor_tensor(y, ps[:, s % 3, j * 256 + hi:j * 256 + hi + 255],
                                               vecs[:, V_HYW + 3 * c + tap:V_HYW + 3 * c + tap + 1], y,
                                               ALU.mult, ALU.add).then_inc(S[sem], 1)
            dve.wait_ge(S["hy_dve"], 24)
            V.tensor_tensor(U, U, X1, ALU.mult).then_inc(S["u_ready"], 1)
            dve.wait_ge(S["u_transposed"], 2)
            V.tensor_copy(UT[:, 1, :], ps[:, 6:8, :].rearrange("p a b -> p (a b)")).then_inc(S["ut_copied"], 1)
            dve.wait_ge(S["u_spectrum_copied"], 2)
            flat = lambda a: a.rearrange("p a b -> p (a b)")
            step(V.tensor_tensor(YT, UI, flat(KI), ALU.mult))
            step(V.tensor_tensor(flat(YR), UR, flat(KR), ALU.mult))
            V.tensor_tensor(flat(YR), flat(YR), YT, ALU.subtract).then_inc(S["y_spectrum"], 1)
            dve.wait_ge(S["y_spectrum"], 1)
            step(V.tensor_tensor(flat(YI), UR, flat(KI), ALU.mult))
            step(V.tensor_tensor(YT, UI, flat(KR), ALU.mult))
            V.tensor_tensor(flat(YI), flat(YI), YT, ALU.add).then_inc(S["y_spectrum"], 1)
            dve.wait_ge(S["y_spectrum"], 2)
            dve.wait_ge(S["channels_taken"], 16)
            for keys in (KF, KB):
                for c in range(8):
                    V.tensor_scalar(keys[:, c, :], keys[:, c, :], OML[:, c:c + 1], None, ALU.mult).then_inc(S["keys_ready"], 1)
            step(V.memset(DB[:, :, 0:1], 0.0))
            dve.wait_ge(S["ones_ready"], 1)
            for c in range(8):
                dve.wait_ge(S["logs_ready"], c + 1)
                V.tensor_tensor_scan(BF[:, c, :], ones_row, LF[:, c, :], 0.0, ALU.mult, ALU.add).then_inc(S["scanned"], 1)
            for c in range(8):
                dve.wait_ge(S["logs_ready"], 9 + c)
                V.tensor_tensor_scan(DB[:, c, 1:256], ones_row[:, 0:255], LBW[:, c, 0:255], 0.0, ALU.mult,
                                     ALU.add).then_inc(S["scanned"], 1)
            dve.wait_ge(S["keys_ready"], 16)
            dve.wait_ge(S["scanned"], 16)
            dve.wait_ge(S["levels_loaded"], 16)

            def exponents(n):
                hg, m = n // 9, 128 >> (n % 9)
                if n >= 2:
                    dve.wait_ge(S["level_product"], n - 1)
                if n % 9 == 8:
                    V.tensor_tensor(LV[n % 2][:, 0, :], KF.rearrange("p h t -> p (h t)")[:, hg * 1024:(hg + 1) * 1024],
                                    KB.rearrange("p h t -> p (h t)")[:, hg * 1024:(hg + 1) * 1024],
                                    ALU.add).then_inc(S["level_ready"], 1)
                    return
                v = split_view(LV[n % 2][:, 0, :], m)
                f, d = level_view(BF, hg, m), level_view(DB, hg, m)
                nb = 512 // m
                V.tensor_tensor(v[:, :, 0, :], f[:, :, 0, m - 1:m].broadcast_to([128, nb, m]), f[:, :, 0, :],
                                ALU.subtract).then_inc(S["level_ek"], 1)
                V.tensor_tensor(v[:, :, 1, :], d[:, :, 1, :], d[:, :, 1, 0:1].broadcast_to([128, nb, m]),
                                ALU.subtract).then_inc(S["level_ek"], 1)

            def decayed(n):
                if n % 9 == 8:
                    return
                hg, m = n // 9, 128 >> (n % 9)
                dve.wait_ge(S["level_exp"], 2 * (n - n // 9) + 1)
                v = split_view(LV[n % 2][:, 0, :], m)
                V.tensor_tensor(v[:, :, 0, :], v[:, :, 0, :], level_view(KF, hg, m)[:, :, 0, :], ALU.mult)
                V.tensor_tensor(v[:, :, 1, :], v[:, :, 1, :], level_view(KB, hg, m)[:, :, 1, :], ALU.mult)
                dve.wait_ge(S["level_exp"], 2 * (n - n // 9) + 2)
                V.tensor_tensor(LV[n % 2][:, 1, :], LV[n % 2][:, 1, :],
                                Q.rearrange("p h t -> p (h t)")[:, hg * 1024:(hg + 1) * 1024],
                                ALU.mult).then_inc(S["level_ready"], 1)

            def select(n):
                if n % 9 == 0:
                    return
                hg = n // 9
                dve.wait_ge(S["level_product"], n + 1)
                if n % 9 >= 2:
                    dve.wait_ge(S["level_dve"], level_dve(n - 1))
                mask = levels[:, n % 9 - 1, :].bitcast(u32).unsqueeze(1).broadcast_to([128, 4, 128])
                for st in range(2):
                    last = V.copy_predicated(AT[hg][:, :, st, st * 128:(st + 1) * 128], mask,
                                             ps[:, 4 + 2 * (n % 2) + st, :].rearrange("p (h c) -> p h c", h=4))
                last.then_inc(S["level_dve"], 1)

            def branch_b(s):
                dve.wait_ge(S["half_multiplied"], 2 * (W_BB + s + 1))
                c = slice(2 * s, 2 * s + 2)
                V.tensor_tensor(flat(MERGED[:, c, :]), ps[:, (36 + s) % 3, :], flat(GB[:, c, :]), ALU.mult).then_inc(S["bb_taken"], 1)

            exponents(0)
            exponents(1)
            decayed(0)
            dve.wait_ge(S["y_product"], 1)
            V.tensor_tensor(flat(YB), flat(ps[:, 4:8, :]), X0, ALU.mult).then_inc(S["yb_ready"], 1)
            dve.wait_ge(S["yb_ready"], 1)
            for n in range(NLV):
                if n:
                    decayed(n)
                    if n + 1 < NLV:
                        exponents(n + 1)
                if n:
                    select(n - 1)
                if n == 11:
                    dve.wait_ge(S["half_multiplied"], 2 * W_BB)
                    V.tensor_copy(h_hi[:, :, :], YB).then_inc(S["operand_hi"], 1)
                    wait_rounded("hyena", 1)
                    rest_of(YB, h_hi[:, :, :], h_lo[:, :, :])
                if n in (13, 14, 16, 17):
                    branch_b((13, 14, 16, 17).index(n))
            select(NLV - 1)
            dve.wait_ge(S["o_sums"], 1)
            step(V.tensor_scalar(RS[0:8, :], ps[0:8, 4, 0:SEQ], 1.0 / 128, 1e-6, ALU.mult, ALU.add))
            V.reciprocal(RS[0:8, :], RS[0:8, :]).then_inc(S["o_inverse"], 1)
            dve.wait_ge(S["gates2_ready"], 2)
            step(V.scalar_tensor_tensor(flat(OT), flat(OT), vecs[:, V_GN:V_GN + 1], flat(OG), ALU.mult, ALU.mult))
            def pairs(tensor, n):
                return tensor[:, 2 * n:2 * n + 2, :]

            for n in range(4):
                dve.wait_ge(S["o_scale"], n + 1)
                V.tensor_tensor(flat(pairs(OT, n)), flat(pairs(OT, n)), ps[:, 4 + n, :], ALU.mult).then_inc(S["o_ready"], 1)
            for n in range(4):
                dve.wait_ge(S["o_ready"], n + 1)
                wait_rounded("hgrn", n + 1)
                rest_of(pairs(OT, n), *(pairs(part, n) for part in hgrn_parts))
            dve.wait_ge(S["bb_taken"], 4)
            for s in range(4):
                dve.wait_ge(S["half_multiplied"], 2 * (W_BA + s + 1))
                c = slice(2 * s, 2 * s + 2)
                V.tensor_tensor(BTMP[:, s % 2, :], ps[:, (40 + s) % 3, :], flat(GA[:, c, :]), ALU.mult).then_inc(S["ba_taken"], 1)
                dve.wait_ge(S["ba_taken"], s + 1)
                V.tensor_tensor(flat(MERGED[:, c, :]), flat(MERGED[:, c, :]), BTMP[:, s % 2, :],
                                ALU.add).then_inc(S["merged_ready"], 1)
                dve.wait_ge(S["merged_ready"], s + 1)
                wait_rounded("merged", s + 1)
                rest_of(pairs(MERGED, s), *(pairs(part, s) for part in merged_parts))
            dve.wait_ge(S["half_multiplied"], 2 * (W_OUT2 + 4))
            dve.wait_ge(S["x_reloaded"], 48)
            for t in range(TOK):
                V.tensor_tensor(x[:, t, :], x[:, t, :], flat(ps[:, 4 + 2 * t:6 + 2 * t, :]), ALU.add).then_inc(S["mixer_added"], 1)
            norm_dve(3)

            def best(rows, values, indices, low=-3e38):
                for first in (0, 8):
                    for r, v, i in zip(rows, values, indices):
                        last = V.max(v[:, first:first + 8], r)
                    step(last)
                    for r, v, i in zip(rows, values, indices):
                        last = V.max_index(i[:, first:first + 8], v[:, first:first + 8], r)
                    step(last)
                    if first == 0:
                        for r, v, i in zip(rows, values, indices):
                            last = V.match_replace(r, v[:, 0:8], r, low)
                        step(last)

            for t in range(TOK):
                dve.wait_ge(S["sim_copied"], t + 1)
                g = range(16)
                best([SC[:, t, n, :] for n in g], [T1V[:, t, n, :] for n in g], [T1I[:, t, n, :] for n in g])
                halves = T1V[:, t].rearrange("p (h s) k -> p h s k", s=2)
                step(V.tensor_tensor(CS[:, t].rearrange("p h (a b) -> p h a b", a=16),
                                     halves[:, :, 0, :].unsqueeze(3).broadcast_to([128, 8, 16, 16]),
                                     halves[:, :, 1, :].unsqueeze(2).broadcast_to([128, 8, 16, 16]), ALU.add))
                g = range(8)
                best([CS[:, t, n, :] for n in g], [TV[:, 8 * t + n, :] for n in g], [TP[:, 8 * t + n, :] for n in g])
            tp = TP.rearrange("p g k -> p (g k)")
            V.tensor_scalar(PAI[:, 0, :], tp, 4, None, ALU.logical_shift_right)
            step(V.tensor_scalar(PAI[:, 1, :], tp, 15, None, ALU.bitwise_and))
            step(V.tensor_copy(PA, PAI))
            step(V.tensor_copy(T1F, T1I))
            dve.wait_ge(S["sk_loaded"], 32)
            for t in range(TOK):
                for side in range(2):
                    place = PA[:, side, t * 128:(t + 1) * 128].unsqueeze(2).broadcast_to([128, 128, 16])
                    step(V.tensor_tensor(EQ.rearrange("p (g a) -> p g a", a=16), place,
                                         iota[:, 0:16].unsqueeze(1).broadcast_to([128, 128, 16]), ALU.is_equal))
                    eq = EQ.rearrange("p (h k a) -> p h k a", h=8, k=16)
                    index = T1F[:, t].rearrange("p (h s) k -> p h s k", s=2)[:, :, side, :].unsqueeze(2).broadcast_to([128, 8, 16, 16])
                    step(V.tensor_tensor(eq, eq, index, ALU.mult))
                    step(V.tensor_reduce(IX[:, side, t, :], EQ.rearrange("p (g a) -> p g a", a=16), AX, ALU.add))
            top, total, inv = (stat[:, c:c + 16] for c in (ST_CMAX, ST_CSUM, ST_CREC))
            wide = lambda a: a.unsqueeze(2).broadcast_to([128, 16, 16])
            step(V.tensor_copy(top, TV[:, :, 0]))
            V.tensor_tensor(TV, TV, wide(top), ALU.subtract).then_inc(S["routes_shifted"], 1)
            dve.wait_ge(S["routes_exp"], 1)
            step(V.tensor_reduce(total, TV, AX, ALU.add))
            step(V.reciprocal(inv, total))
            V.tensor_tensor(TV, TV, wide(inv), ALU.mult).then_inc(S["routes_ready"], 1)
            dve.wait_ge(S["routes_copied"], 2)
            step(V.tensor_copy(iota_short[:, :], iota))
            step(V.tensor_tensor(GATE, ps[:, 5, 0:256], ROUTE[:, 2, :], ALU.subtract))
            step(V.tensor_copy(ROUTE[:, 3, :], GATE))
            V.tensor_tensor(ROUTE[:, 4, :], GATE, ROUTE[:, 3, :], ALU.subtract).then_inc(S["gate_rest"], 1)
            dve.wait_ge(S["gate_rest"], 1)

            def onehots(half, q, parity, it=None, step=2):
                tok = at(4 * (q - 64 * half), 4 * step, it)
                if q >= 2:
                    dve.wait_ge(S["gate_product"], at(q - 1, step, it))
                first, second = (ROUTE[:, n, bass.ds(tok, 4)] for n in range(2))
                gate = ROUTE[:, 2:5, bass.ds(tok, 4)]
                V.tensor_tensor(OA[:, parity], first.unsqueeze(2).broadcast_to([128, 4, 128]),
                                iota_short[:, :].unsqueeze(1).broadcast_to([128, 4, 128]), ALU.is_equal)
                if q:
                    dve.wait_ge(S["onehots"], at(q, step, it))
                V.tensor_tensor(ONEHOT_J[:, :, :], second.unsqueeze(2).broadcast_to([128, 4, 64]),
                                iota_short[:, 64 * half:64 * half + 64].unsqueeze(1).broadcast_to([128, 4, 64]),
                                ALU.is_equal).then_inc(S["onehot_j"], 1)
                dve.wait_ge(S["onehot_j"], at(q + 1, step, it))
                V.tensor_tensor(OB[:, parity], ONEHOT_J[:, :, :].unsqueeze(1).broadcast_to([128, 3, 4, 64]),
                                gate.unsqueeze(3).broadcast_to([128, 3, 4, 64]), ALU.mult).then_inc(S["onehots"], 1)

            def gated(half, q, parity, it=None, step=2):
                tok = at(4 * (q - 64 * half), 4 * step, it)
                dve.wait_ge(S["gate_product"], at(q + 1, step, it))
                h = H[:, 64 * half:64 * half + 64, bass.ds(tok, 4)].rearrange("p j t -> p t j")
                bank = (parity if half else 3 + parity)
                V.tensor_tensor(h, ps[:, bank, 0:256].rearrange("p (t j) -> p t j", t=4), h, ALU.mult).then_inc(S["gated"], 1)

            def turn(half, q, it=None, step=2, s=None):
                onehots(half, q + 2, 0, it, step)
                gated(half, q + 1, 1, it, step)
                if s is not None:
                    rest(s, it)
                onehots(half, q + 3, 1, it, step)
                gated(half, q + 2, 0, it, step)

            def rest(s, it=None):
                dve.wait_ge(S["operand_hi"], at(FIRST["experts"] + s + 1, 3, it))
                place = slice(2 * (s % 3), 2 * (s % 3) + 2)
                rest_of(flat(H[:, bass.ds(at(2 * s, 6, it), 2), :]), flat(h_hi[:, place, :]), flat(h_lo[:, place, :]))

            for half in range(2):
                q = 64 * half
                onehots(half, q, 0)
                onehots(half, q + 1, 1)
                dve.wait_ge(S["h_ready"], 32 + 32 * half)
                if half:
                    rest(0)
                    rest(1)
                gated(half, q, 0)
                if half == 0:
                    with dve.Fori(0, 31) as it:
                        turn(half, q, it)
                else:
                    turn(half, q, s=2)
                    with dve.Fori(0, 9) as it:
                        for n in range(3):
                            turn(half, q + 2 + 2 * n, it, 6, 3 + n)
                    for n in range(28, 31):
                        turn(half, q + 2 * n, s=2 + n if n < 30 else None)
                gated(half, q + 63, 1)
            with dve.Fori(0, 10) as it:
                for s in range(32, 35):
                    rest(s, it)
            rest(62)
            rest(63)
            dve.wait_ge(S["half_multiplied"], 2 * NSLOT)
            V.tensor_copy(flat(PT[:, 4:8, :]), flat(ps[:, 6:8, :])).then_inc(S["pt_copied"], 1)
            dve.wait_ge(S["x_reloaded"], 64)
            for t in range(TOK):
                dve.wait_ge(S["pt_transposed"], t + 1)
                V.tensor_tensor(x[:, t, :], x[:, t, :], flat(ps[:, 2 * t:2 * t + 2, :]), ALU.add).then_inc(S["peer_added"], 1)
            inverse("squares_summed", 10, "inv_ready", 5)
            dve.wait_ge(S["rstd_ready"], 5)
            dve.wait_ge(S["rows_loaded"], 48)
            for t in range(TOK):
                V.scalar_tensor_tensor(x[:, t, :], x[:, t, :], stat[:, ST_RSTD + t:ST_RSTD + t + 1], wrow[:, :],
                                       ALU.mult, ALU.mult).then_inc(S["x_final"], 1)

        def mm(out, lhsT, rhs, start=True, stop=True):
            return nc.tensor.matmul(out, lhsT, rhs, start=start, stop=stop, skip_group_check=True)

        def product(out, stationary, moving, start=True, stop=True):
            if len(stationary) == 1:
                return mm(out, stationary[0], moving[0], start, stop)
            mm(out, stationary[0], moving[0], start, False)
            mm(out, stationary[0], moving[1], False, False)
            return mm(out, stationary[1], moving[0], False, stop)

        ALL = slice(None)

        def tile(t):
            return slice(t * 128, (t + 1) * 128)

        def split_count(h):
            return h + 1 if h < WHOLE[0] else h + 1 - (WHOLE[1] - WHOLE[0])

        def at(base, step, it):
            return base if it is None else it * step + base

        block = ctx.enter_context(nc.Block())

        @block.sync
        def _(sp):
            sp.dma_start(ident[:, :], dram["ident"]).then_inc(S["ident_loaded"], 16)
            sp.dma_start(x[:, :, :], dram["x"]).then_inc(S["x_loaded"], 16)
            sp.dma_start(vecs[:, :], dram["vecs"]).then_inc(S["consts_loaded"], 16)
            def half(r):
                return slice(r % 2 * HALF, (r % 2 + 1) * HALF)

            for r in range(RING):
                sp.dma_start(ring[:, r, :], dram["stream"][r // 2, :, half(r)]).then_inc(arrived[r], 16)
            with sp.Fori(1, 2 * NSLOT // RING) as turn:
                for r in range(RING):
                    sp.wait_ge(S["half_multiplied"], turn * RING + (r + 1 - RING))
                    sp.dma_start(ring[:, r, :], dram["stream"][turn * (RING // 2) + r // 2, :, half(r)]).then_inc(arrived[r], 16)
            for t in range(TOK):
                sp.wait_ge(S["x_final"], t + 1)
                sp.dma_start(dram["out"][:, t, :], x[:, t, :]).then_inc(S["out_stored"], 16)
            sp.wait_ge(S["out_stored"], 16 * TOK)

        @block.gpsimd
        def _(pool):
            def rest(h, it=None):
                pool.wait_ge(S["split_hi"], at(split_count(h), RING, it))
                P.tensor_tensor(ring_lo[:, h % RING, :], ring[:, h % RING, :], ring_hi[:, h % RING, :].bitcast(fp32),
                                ALU.subtract).then_inc(S["split_lo"], 1)

            def rests(first, end):
                turns = max(end - first, 0) // RING
                if turns > 1:
                    with pool.Fori(0, turns) as it:
                        for n in range(RING):
                            rest(first + n, it)
                    first += turns * RING
                for h in range(first, end):
                    rest(h)

            pool.dma_start(ZT, dram["zt"]).then_inc(S["filt_loaded"], 16)
            pool.dma_start(FT, dram["filt"]).then_inc(S["filt_loaded"], 16)
            pool.dma_start(FW[:, 0, :], dram["fdecay"]).then_inc(S["fdecay_loaded"], 16)
            pool.dma_start(aux[:, 0:2040], dram["tab1"]).then_inc(S["tab_loaded"], 16)
            pool.dma_start(W3[0:64, :], dram["w3"]).then_inc(S["w3_loaded"], 16)
            pool.dma_start(DF1.rearrange("p a b -> p (a b)"), dram["dft"][:, 0:1024]).then_inc(S["dft_loaded"], 16)
            pool.dma_start(wrow[0:1, :], dram["bias"]).then_inc(S["w3_loaded"], 16)
            rests(0, 8)
            pool.wait_ge(S["xn_transposed"], 4)
            pool.dma_start(gate_columns.rearrange("p k c -> p (k c)"), dram["gate_columns"]).then_inc(S["gnw_loaded"], 16)
            pool.dma_start(gnw, dram["gnw"]).then_inc(S["gnw_loaded"], 16)

            rests(8, 16)
            pool.wait_ge(S["tab_loaded"], 16)
            pool.wait_ge(S["p1_act"], 3)
            src = P1[:, 0, 0:1280].rearrange("p (h c) -> p h c", h=20)
            lo, hi = src[:, :, 0:32], src[:, :, 32:64]
            c = cosT[:, 0, :].unsqueeze(1).broadcast_to([128, 20, 32])
            s = sinT[:, 0, :].unsqueeze(1).broadcast_to([128, 20, 32])
            P.tensor_tensor(RC, lo, c, ALU.mult).then_inc(S["pool_step"], 1)
            P.tensor_tensor(RD, hi, s, ALU.mult).then_inc(S["pool_step"], 1)
            rests(16, 18)
            pool.wait_ge(S["pool_step"], 2)
            P.tensor_tensor(R[:, 0, :, 0:32], RC, RD, ALU.subtract).then_inc(S["pool_step"], 1)
            rests(18, 20)
            pool.wait_ge(S["pool_step"], 3)
            P.tensor_tensor(RC, lo, s, ALU.mult).then_inc(S["pool_step"], 1)
            P.tensor_tensor(RD, hi, c, ALU.mult).then_inc(S["pool_step"], 1)
            rests(20, 22)
            pool.wait_ge(S["pool_step"], 5)
            P.tensor_tensor(R[:, 0, :, 32:64], RC, RD, ALU.add).then_inc(S["rope_ready"], 1)
            pool.wait_ge(S["filt_ab"], 2)
            pool.wait_ge(S["p1_dve"], 3)
            for t in range(TOK):
                heads = P1[:, t, 1280:1536].rearrange("p (i c) -> p i c", i=4).unsqueeze(2).broadcast_to([128, 4, 2, 64])
                P.tensor_copy(DUP[:, t], heads).then_inc(S["dup_ready"], 1)
            pool.wait_ge(S["kernel_spectrum"], 2)
            pool.dma_start(cmps[:, :], dram["cmps"]).then_inc(S["cmps_loaded"], 16)
            pool.dma_start(wrow[:, :], dram["post1"]).then_inc(S["rows_loaded"], 16)
            rests(2 * W_OUT, 2 * W_FFN + 6)
            pool.wait_ge(S["wrow_free"], 2)
            pool.dma_start(wrow[:, :], dram["post2"]).then_inc(S["rows_loaded"], 16)
            pool_second(pool, rests)

        @block.tensor
        def _(pe):
            def weights(n, half, it=None, span=3):
                h = 2 * n + half
                if WHOLE[0] <= h < WHOLE[1]:
                    pe.wait_ge(arrived[h % RING], at(16 * (h // RING + 1), 16 * span // 3, it))
                    return (ring[:, h % RING, :],)
                pe.wait_ge(S["split_hi"], at(split_count(h), 2 * span, it))
                pe.wait_ge(S["split_lo"], at(split_count(h), 2 * span, it))
                return (ring_hi[:, h % RING, :], ring_lo[:, h % RING, :])

            def multiplied(instruction):
                instruction.then_inc(S["half_multiplied"], 1)

            def parts(tensors, *index):
                return [t[index] for t in tensors]

            def norm_transposes(k):
                pe.wait_ge(S["xn_ready"], 2 * k + 2)
                for c in range(KC):
                    for t in range(TOK):
                        last = nc.tensor.transpose(ps[:, c // 2, (c % 2) * 256 + t * 128:(c % 2) * 256 + t * 128 + 128],
                                                   xn[:, t, c * 128:(c + 1) * 128], ident[:, :])
                    if c % 2:
                        last.then_inc(S["xn_transposed"], 1)

            def wait_operand(name, count):
                pe.wait_ge(S["operand_hi"], FIRST[name] + count)
                pe.wait_ge(S["operand_lo"], FIRST[name] + count)

            def wait_normed(k, c, bank):
                wait_operand(f"norm{k}", max(c, 2 * bank + 1) + 1)

            def token_product(n, bank, src):
                for kq in range(4):
                    w = weights(n + kq // 2, kq % 2)
                    for t in range(TOK):
                        for k in range(2):
                            last = product(ps[:, bank + t, :], parts(src, ALL, 2 * kq + k, tile(t)),
                                           parts(w, ALL, slice(k * 512, (k + 1) * 512)), kq + k == 0, kq == 3 and k == 1)
                    multiplied(last)

            pe.wait_ge(S["filt_loaded"], 32)
            mm(ps[0:64, 7, 0:256], FT[0:33, 0:64], ZT[0:33, 0:256]).then_inc(S["filt_hidden"], 1)
            pe.wait_ge(S["ident_loaded"], 16)
            norm_transposes(0)
            wait_operand("norm0", 8)

            def p1_group(g):
                if g >= 2:
                    pe.wait_ge(S["p1_act"], g - 1)
                    pe.wait_ge(S["p1_dve"], g - 1)
                token_product(2 * g, 4 + 2 * (g % 2), in_parts)

            p1_group(0)
            pe.wait_ge(S["filt_sine"], 1)
            mm(ps[0:64, 0, 0:256], FT[0:64, 64:128], FHID[0:64, 0, :]).then_inc(S["filt_hidden"], 1)
            p1_group(1)
            pe.wait_ge(S["filt_sine"], 2)
            pe.wait_ge(S["w3_loaded"], 32)
            for pt in range(TOK):
                if pt:
                    pe.wait_ge(S["filt_windowed"], 1)
                for n in range(4):
                    last = mm(ps[:, n, :], FHID[0:64, 1, pt * 128:(pt + 1) * 128], W3[0:64, n * 512:(n + 1) * 512])
                last.then_inc(S["filt_product"], 1)
                p1_group(2 + pt)
            p1_group(4)
            pe.wait_ge(S["dft_loaded"], 16)
            pe.wait_ge(S["filt_ab"], 2)
            for part in range(2):
                if part:
                    pe.wait_ge(S["spectrum_copied"], 1)
                for ft in range(2):
                    for nh in range(2):
                        for pt in range(TOK):
                            last = mm(ps[:, ft * 2 + nh, :], DF1[:, part * 2 + pt, ft * 128:(ft + 1) * 128],
                                      FAB[:, part, pt, nh * 512:(nh + 1) * 512], pt == 0, pt == 1)
                last.then_inc(S["kernel_spectrum"], 1)
                if part == 0:
                    pe.wait_ge(S["p1_act"], 4)
                    pe.wait_ge(S["p1_dve"], 4)
                    for kh in range(2):
                        w = weights(10, kh)
                        for t in range(TOK):
                            for k in range(4):
                                last = product(ps[:, 6 + t, 0:256], parts(in_parts, ALL, 4 * kh + k, tile(t)),
                                               parts(w, ALL, slice(k * 256, (k + 1) * 256)), kh + k == 0, kh == 1 and k == 3)
                        multiplied(last)
            pe.wait_ge(S["p1_act"], 5)
            pe.wait_ge(S["p1_dve"], 5)
            pe.wait_ge(S["gate_weights_ready"], 2)
            for k in range(KC):
                last = product(ps[0:24, 4, 0:SEQ], parts(gate_weights, ALL, k, ALL), parts(in_parts, ALL, k, ALL),
                               k == 0, k == KC - 1)
            last.then_inc(S["gates_product"], 1)

            pe.wait_ge(S["rope_ready"], 2)
            pe.wait_ge(S["spectrum_copied"], 2)
            for b in range(10):
                if b >= 4:
                    pe.wait_ge(S["heads_dve"] if b % 2 else S["heads_act"], (b - 4) // 2 + 1)
                if b == 4:
                    pe.wait_ge(S["gates_sigmoid"], 1)
                    for t in range(TOK):
                        last = nc.tensor.transpose(ps[:, 5, t * 24:(t + 1) * 24], gates_T[0:24, tile(t)], ident[0:24, 0:24])
                    last.then_inc(S["gates_transposed"], 1)
                for h in range(2):
                    for t in range(TOK):
                        last = nc.tensor.transpose(ps[0:64, b % 4, h * 256 + t * 128:h * 256 + t * 128 + 128],
                                                   R[:, t, 2 * b + h, :], ident[:, :])
                last.then_inc(S["heads_transposed"], 1)
            pe.wait_ge(S["dup_ready"], 2)
            pe.wait_ge(S["gates_ready"], 1)
            for i in range(4):
                for t in range(TOK):
                    last = nc.tensor.transpose(ps[:, 4 + i // 2, (i % 2) * 256 + t * 128:(i % 2) * 256 + t * 128 + 128],
                                               DUP[:, t, i].rearrange("p a c -> p (a c)"), ident[:, :])
            last.then_inc(S["dup_transposed"], 1)
            pe.wait_ge(S["heads_act"], 5)
            pe.wait_ge(S["heads_dve"], 5)
            for h in range(4):
                mm(ps[:, h, 0:256], RT[0:64, 4 + h, 0:128], RT[0:64, h, :])
                mm(ps[:, h, 256:384], RT[0:64, 4 + h, 128:256], RT[0:64, h, 128:256]).then_inc(S["ret_scores"], 1)
            pe.wait_ge(S["blocks_ready"], 4)
            pe.wait_ge(S["p1_act"], 6)
            pe.wait_ge(S["p1_dve"], 6)
            for kv in range(2):
                for bh in range(4):
                    w = weights(W_CMP + 2 * kv + bh // 2, bh % 2)
                    for half in range(2):
                        for b in range(4):
                            last = product(ps[:, 6 + half, kv * 30:kv * 30 + 30],
                                           parts(w, ALL, slice(b * 256 + half * 128, b * 256 + half * 128 + 128)),
                                           parts((BLK,), ALL, kv, bh * 4 + b, ALL), bh + b == 0, bh == 3 and b == 3)
                    multiplied(last)
            pe.wait_ge(S["hid_ready"], 4)
            for n, w2 in enumerate((w2k, w2r)):
                for half in range(2):
                    mm(ps[0:64, 4, n * 30:n * 30 + 30], w2[:, half, :], HID[:, 0, half, :], half == 0, half == 1)
            for g in range(2):
                for half in range(2):
                    last = mm(ps[0:NCMP, 5, g * 64:g * 64 + 64], HID[:, 1, half, g * NCMP:(g + 1) * NCMP],
                              w2v[:, half, :], half == 0, half == 1)
            last.then_inc(S["cmp_product"], 1)
            pe.wait_ge(S["ret_decayed"], 4)
            for h in range(4):
                v0, v1 = (P1[:, t, 1536 + h * 128:1536 + (h + 1) * 128] for t in range(2))
                mm(ps[:, 6, h * 128:(h + 1) * 128], SD[:, h, 0:128], v0)
                mm(ps[:, 7, h * 128:(h + 1) * 128], SD[:, h, 128:256], v0, True, False)
                last = mm(ps[:, 7, h * 128:(h + 1) * 128], SD[:, h, 256:384], v1, False, True)
            last.then_inc(S["ret_out"], 1)
            pe.wait_ge(S["kc_ready"], 1)
            for t in range(TOK):
                for h in range(8):
                    last = mm(ps[:, 4, (t * 8 + h) * NCMP:(t * 8 + h + 1) * NCMP], RT[0:64, 8 + h, t * 128:(t + 1) * 128],
                              KCT[0:64, (h // 4) * NCMP:(h // 4 + 1) * NCMP])
            last.then_inc(S["cmp_scores"], 1)
            pe.wait_ge(S["cmp_probs"], 1)
            for n in range(16):
                last = nc.tensor.transpose(ps[0:NCMP, n // 4, (n % 4) * 128:(n % 4 + 1) * 128],
                                           CE[:, n // 8, n % 8, :], ident[:, :])
            last.then_inc(S["cmp_ptrans"], 1)
            pe.wait_ge(S["cmp_pcopied"], 1)
            pe.wait_ge(S["vc_copied"], 1)
            for n in range(16):
                last = mm(ps[:, 4 + n // 8, (n % 8) * 64:(n % 8 + 1) * 64], CET[0:NCMP, n * 128:(n + 1) * 128],
                          VC[0:NCMP, (n % 8) // 4, :])
            last.then_inc(S["cmp_out"], 1)

            def scores(u):
                br, qt, g = u // 4, u // 2 % 2, u % 2
                nk = 128 * (qt + 1)
                for r in range(4):
                    col = r * nk
                    last = mm(ps[:, 2 * (u % 2) + col // 512, col % 512:col % 512 + nk],
                              RT[0:64, 8 + 4 * g + r, qt * 128:(qt + 1) * 128], RT[0:64, 16 + 2 * br + g, 0:nk])
                last.then_inc(S["att_scores"], 1)

            scores(0)
            scores(1)
            pe.wait_ge(S["cmp_done"], 2)
            pe.wait_ge(S["ret_normed"], 1)
            for u in range(8):
                br, qt, g = u // 4, u // 2 % 2, u % 2
                nj = qt + 1
                pe.wait_ge(S["att_exp"], 4 * u + 4)
                if u:
                    pe.wait_ge(S["att_copied_act"], u)
                    if dve_copies(u):
                        pe.wait_ge(S["att_copied_dve"], dve_copies(u))
                for r in range(4):
                    for jt in range(nj):
                        n = r * nj + jt
                        last = nc.tensor.transpose(ps[:, 4 + n // 4, (n % 4) * 128:(n % 4 + 1) * 128],
                                                   SM[:, u % 2, r, jt * 128:(jt + 1) * 128], ident[:, :])
                last.then_inc(S["att_transposed"], 1)
                if u + 2 < 8:
                    scores(u + 2)
                pe.wait_ge(S["att_copied_act"], u + 1)
                if dve_copies(u + 1):
                    pe.wait_ge(S["att_copied_dve"], dve_copies(u + 1))
                if g == 0 and u >= 4:
                    pe.wait_ge(S["att_done"], u // 2 - 1)
                vcol = 2560 + 128 * br + 64 * g
                for r in range(4):
                    for jt in range(nj):
                        last = mm(ps[:, 6 + u // 2 % 2, (4 * g + r) * 64:(4 * g + r + 1) * 64],
                                  ET[:, u % 2, (r * nj + jt) * 128:(r * nj + jt + 1) * 128], P1[:, jt, vcol:vcol + 64],
                                  jt == 0, jt == nj - 1)
                last.then_inc(S["att_out"], 1)
            pe.wait_ge(S["att_done"], 4)
            for c in range(KC):
                for t in range(TOK):
                    last = nc.tensor.transpose(ps[:, c // 2, (c % 2) * 256 + t * 128:(c % 2) * 256 + t * 128 + 128],
                                               mix[:, t, c * 128:(c + 1) * 128], ident[:, :])
                if c % 2:
                    last.then_inc(S["mix_transposed"], 1)

            def out_product(n, src, ready):
                for nh in range(2):
                    for kq in range(4):
                        w = weights(n + 2 * nh + kq // 2, kq % 2)
                        if nh == 0:
                            ready(kq)
                        for t in range(TOK):
                            for k in range(2):
                                last = product(ps[:, 4 + 2 * t + nh, :], parts(src, ALL, 2 * kq + k, tile(t)),
                                               parts(w, ALL, slice(k * 512, (k + 1) * 512)), kq + k == 0, kq == 3 and k == 1)
                        multiplied(last)

            out_product(W_OUT, in_parts, lambda quarter: wait_operand("mixed", quarter + 1))
            norm_transposes(1)

            def ffn_up(i, n, it=None):
                if i >= 4:
                    pe.wait_ge(S["ffn_conv_dve"], at(2 * (i - 3), 8, it))
                for j in range(2):
                    w = weights(n, j, it, 6)
                    for k in range(KC):
                        if i == 0 and j == 0:
                            wait_normed(1, k, 0)
                        last = product(ps[:, i % 4, j * 256:(j + 1) * 256], parts(w, ALL, tile(k)),
                                       parts(in_parts, ALL, k, ALL), k == 0, k == KC - 1)
                    multiplied(last)

            def ffn_down(p, n, it=None):
                for ii in range(2):
                    w = weights(n, ii, it, 6)
                    pe.wait_ge(S["ffn_gated"], at(2 * p + ii + 1, 4, it))
                    for t in range(TOK):
                        for nh in range(2):
                            last = product(ps[:, 4 + 2 * t + nh, :], parts((ffn_hi, ffn_lo), ALL, (2 * p + ii) % 4, tile(t)),
                                           parts(w, ALL, slice(nh * 512, (nh + 1) * 512)),
                                           p == 0 and ii == 0, p == 10 and ii == 1)
                    multiplied(last)

            def ffn_pair(p, it=None):
                n = W_FFN + 2 + 3 * (p - 1)
                ffn_up(2 * p, n, it)
                ffn_up(2 * p + 1, n + 1, it)
                ffn_down(p - 1, n + 2, it)

            ffn_up(0, W_FFN)
            ffn_up(1, W_FFN + 1)
            ffn_pair(1)
            ffn_pair(2)
            with pe.Fori(0, 4) as it:
                ffn_pair(3, it)
                ffn_pair(4, it)
            ffn_down(10, W_FFN + 32)
            pe_second(pe, weights, multiplied, parts, norm_transposes, wait_operand, wait_normed, token_product, out_product)

        @block.scalar
        def _(act):
            def split(h, it=None, span=3):
                act.wait_ge(arrived[h % RING], at(16 * (h // RING + 1), 16 * span // 3, it))
                A.copy(ring_hi[:, h % RING, :], ring[:, h % RING, :]).then_inc(S["split_hi"], 1)

            split_next = [0]

            def ahead(last):
                for h in range(split_next[0], last + 1):
                    if not WHOLE[0] <= h < WHOLE[1]:
                        split(h)
                split_next[0] = max(split_next[0], last + 1)

            def round_to(dst, src, scale=1.0):
                A.activation(dst, src, ACT.Copy, scale=scale).then_inc(S["operand_hi"], 1)

            def load_roots(n):
                A.activation(stat[:, ST_UNUSED + n:ST_UNUSED + n + 1], ident[:, 0:1], ACT.Sqrt)

            def reload(source, n):
                act.wait_ge(S["half_multiplied"], n)
                act.dma_start(x[:, :, :], source).then_inc(S["x_reloaded"], 16)

            def norm_act(k):
                for t in range(TOK):
                    if k:
                        act.wait_ge(S["mixer_added"] if k == 3 else S["post_done"], (0, 0, 2, 0)[k] + t + 1)
                    A.activation(xn[:, t, :], x[:, t, :], ACT.Square,
                                 accum_out=stat[:, ST_SQ + t:ST_SQ + t + 1]).then_inc(S["squares_summed"], 1)
                if k:
                    act.dma_start(dram["residual"], x[:, :, :]).then_inc(S["x_stored"], 16)
                act.wait_ge(S["inv_ready"], k + 1)
                A.activation(stat[:, ST_RSTD:ST_RSTD + 2], stat[:, ST_INV:ST_INV + 2], ACT.Sqrt).then_inc(S["rstd_ready"], 1)
                if k == 0:
                    ahead(0)
                else:
                    act.wait_ge(S["x_stored"], 16 * k)
                for c in range(KC):
                    act.wait_ge(S["xn_transposed"], 4 * k + c // 2 + 1)
                    round_to(h_hi[:, c, :], ps[:, c // 2, c % 2 * 256:c % 2 * 256 + 256],
                             vecs[:, V_NORM + 8 * k + c:V_NORM + 8 * k + c + 1])

            act.wait_ge(S["ident_loaded"], 16)
            load_roots(0)
            act.wait_ge(S["x_loaded"], 16)
            act.wait_ge(S["consts_loaded"], 16)
            norm_act(0)
            ahead(3)
            act.wait_ge(S["filt_reduced"], 1)
            A.activation(FHID[0:64, 0, :], FTMP[0:64, 0, :], ACT.Sin).then_inc(S["filt_sine"], 1)

            def p1_copy(g):
                ahead(min(4 * g + 7, WHOLE[0] - 1))
                act.wait_ge(S["half_multiplied"], 4 * g + 4)
                A.copy(P1[:, 0, g * 512:(g + 1) * 512], ps[:, 4 + 2 * (g % 2), :]).then_inc(S["p1_act"], 1)

            p1_copy(0)
            act.wait_ge(S["filt_reduced"], 2)
            A.activation(FHID[0:64, 1, :], FTMP[0:64, 0, :], ACT.Sin).then_inc(S["filt_sine"], 1)
            act.wait_ge(S["fdecay_loaded"], 16)
            act.wait_ge(S["filt_loaded"], 32)
            A.activation(FW[:, 0, :], FW[:, 0, :], ACT.Abs).then_inc(S["act_step"], 1)
            act.wait_ge(S["act_step"], 1)
            A.activation(FW[:, 1, :], FW[:, 0, :], ACT.Exp, scale=ZT[:, 257:258]).then_inc(S["act_step"], 1)
            act.wait_ge(S["act_step"], 2)
            A.activation(FW[:, 0, :], FW[:, 0, :], ACT.Exp, scale=ZT[:, 256:257]).then_inc(S["filt_window"], 1)
            p1_copy(1)
            p1_copy(2)
            p1_copy(3)
            p1_copy(4)
            act.wait_ge(S["kernel_spectrum"], 1)
            A.copy(KR.rearrange("p a b -> p (a b)"), ps[:, 0:4, :].rearrange("p a b -> p (a b)")).then_inc(S["spectrum_copied"], 1)
            act.wait_ge(S["half_multiplied"], 22)
            A.copy(P1[:, 0, 2560:2816], ps[:, 6, 0:256]).then_inc(S["p1_act"], 1)
            act.wait_ge(S["kernel_spectrum"], 2)
            A.copy(KI.rearrange("p a b -> p (a b)"), ps[:, 0:4, :].rearrange("p a b -> p (a b)")).then_inc(S["spectrum_copied"], 1)
            act.wait_ge(S["gates_product"], 1)
            A.activation(gates_T[0:24, :], ps[0:24, 4, 0:SEQ], ACT.Sigmoid).then_inc(S["gates_sigmoid"], 1)
            act.wait_ge(S["p1_dve"], 5)
            A.activation(P1[:, :, 2048:2560], P1[:, :, 2048:2560], ACT.Silu).then_inc(S["silu_ready"], 1)
            for b in range(0, 10, 2):
                act.wait_ge(S["heads_transposed"], b + 1)
                A.mul(RT[0:64, 2 * b:2 * b + 2, :].rearrange("p a b -> p (a b)"), ps[0:64, b % 4, :],
                      0.125 if 4 <= b < 8 else 1.0).then_inc(S["heads_act"], 1)
                if b == 2:
                    act.wait_ge(S["gates_transposed"], 1)
                    A.copy(P1[:, :, 2816:2840], ps[:, 5, 0:48].rearrange("p (t c) -> p t c", t=2)).then_inc(S["gates_ready"], 1)
            act.wait_ge(S["half_multiplied"], 2 * (W_CMP + 4))
            for kv in range(2):
                for half in range(2):
                    A.activation(HID[:, kv, half, :], ps[:, 6 + half, kv * 30:kv * 30 + 30],
                                 ACT.Gelu_apprx_tanh).then_inc(S["hid_ready"], 1)
            act.wait_ge(S["cmp_product"], 1)
            A.copy(VC[0:NCMP].rearrange("p a b -> p (a b)"), ps[0:NCMP, 5, 0:128]).then_inc(S["vc_copied"], 1)
            act.wait_ge(S["cmp_shifted"], 1)
            A.activation(CE, CE, ACT.Exp).then_inc(S["cmp_exp"], 1)
            act.wait_ge(S["gn_inv"], 1)
            A.activation(stat[:, ST_GRSTD:ST_GRSTD + 8], stat[:, ST_GVAR:ST_GVAR + 8], ACT.Sqrt).then_inc(S["gn_rstd"], 1)
            act.wait_ge(S["cmp_ptrans"], 1)
            A.copy(CET[0:NCMP, :], ps[0:NCMP, 0:4, :].rearrange("p a b -> p (a b)")).then_inc(S["cmp_pcopied"], 1)

            def exps(u):
                qt = u // 2 % 2
                act.wait_ge(S["att_max"], u + 1)
                for r in range(4):
                    col = ST_SUM + 8 * (u // 2) + 4 * (u % 2) + r
                    e = SM[:, u % 2, r, 0:128 * (qt + 1)]
                    A.activation(e, e, ACT.Exp, bias=stat[:, ST_NMAX + 4 * (u % 2) + r:ST_NMAX + 4 * (u % 2) + r + 1],
                                 accum_out=stat[:, col:col + 1]).then_inc(S["att_exp"], 1)

            exps(0)
            exps(1)
            for u in range(8):
                act.wait_ge(S["att_transposed"], u + 1)
                A.copy(ET[:, u % 2, 0:512], ps[:, 4, :]).then_inc(S["att_copied_act"], 1)
                if u + 2 < 8:
                    exps(u + 2)
                if u < 6:
                    ahead(2 * W_OUT + u)
            for b in range(4):
                act.wait_ge(S["mix_transposed"], b + 1)
                round_to(h_hi[:, 2 * b:2 * b + 2, :].rearrange("p a b -> p (a b)"), ps[:, b, :])
            ahead(2 * W_FFN - 1)
            load_roots(1)
            reload(dram["x"], 2 * W_FFN)

            def post_act(k, n, further):
                act.wait_ge(S["half_multiplied"], 2 * n)
                for t in range(TOK):
                    A.activation(xn[:, t, :], ps[:, 4 + 2 * t:6 + 2 * t, :].rearrange("p a b -> p (a b)"), ACT.Square,
                                 accum_out=stat[:, ST_SQ + t:ST_SQ + t + 1]).then_inc(S["post_squares"], 1)
                act.wait_ge(S["post_inv"], k + 1)
                A.activation(stat[:, ST_RSTD:ST_RSTD + 2], stat[:, ST_INV:ST_INV + 2], ACT.Sqrt).then_inc(S["post_rstd"], 1)
                ahead(further)

            post_act(0, W_OUT + 4, 2 * W_FFN + 2)
            norm_act(1)

            def ffn_act(i, n, it=None):
                if it is None:
                    ahead(2 * n + 5)
                else:
                    for h in range(2 * n + 4 - 2 * (i % 2 == 0), 2 * n + 6):
                        split(h, it, 6)
                act.wait_ge(S["half_multiplied"], at(2 * n + 2, 12, it))
                if i >= 2:
                    act.wait_ge(S["ffn_gated"], at(i - 1, 4, it))
                for j in range(2):
                    col = at(V_CONV + (j * NFF + i) * 3 + 2, 12, it)
                    A.activation(CONV[:, i % 2, j, :], ps[:, i % 4, j * 256:(j + 1) * 256], ACT.Copy,
                                 scale=vecs[:, bass.ds(col, 1)]).then_inc(S["ffn_conv_act"], 1)
                act.wait_ge(S["ffn_conv_dve"], at(2 * i + 1, 8, it))
                A.activation(CONV[:, i % 2, 0, :], CONV[:, i % 2, 0, :], ACT.Gelu_apprx_tanh).then_inc(S["ffn_gelu"], 1)

            def ffn_act_pair(p, it=None):
                n = W_FFN + 2 + 3 * (p - 1)
                ffn_act(2 * p, n, it)
                ffn_act(2 * p + 1, n + 1, it)

            ffn_act(0, W_FFN)
            ffn_act(1, W_FFN + 1)
            ffn_act_pair(1)
            ffn_act_pair(2)
            with act.Fori(0, 4) as it:
                ffn_act_pair(3, it)
                ffn_act_pair(4, it)
            split_next[0] = 2 * W_HY
            load_roots(2)
            reload(dram["residual"], 2 * (W_HY - 2))
            post_act(1, W_HY, 2 * W_HY + 2)
            act_second(act, split, ahead, round_to, load_roots, reload, norm_act)

        @block.vector
        def _(dve):
            steps = [0]

            def step(instruction):
                steps[0] += 1
                instruction.then_inc(S["dve_step"], 1)
                dve.wait_ge(S["dve_step"], steps[0])

            def inverse(squares, n_squares, done, n_done):
                dve.wait_ge(S[squares], n_squares)
                step(V.tensor_scalar(stat[:, ST_INV:ST_INV + 2], stat[:, ST_SQ:ST_SQ + 2], 1.0 / D, 1e-6, ALU.mult, ALU.add))
                V.reciprocal(stat[:, ST_INV:ST_INV + 2], stat[:, ST_INV:ST_INV + 2]).then_inc(S[done], 1)

            def wait_rounded(name, count):
                dve.wait_ge(S["operand_hi"], FIRST[name] + count)

            def rest_of(src, hi, lo):
                V.tensor_tensor(lo, src, hi.bitcast(fp32), ALU.subtract).then_inc(S["operand_lo"], 1)

            def norm_dve(k):
                inverse("squares_summed", 2 * k + 2, "inv_ready", k + 1)
                dve.wait_ge(S["rstd_ready"], k + 1)
                for t in range(TOK):
                    V.tensor_scalar(xn[:, t, :], x[:, t, :], stat[:, ST_RSTD + t:ST_RSTD + t + 1], None,
                                    ALU.mult).then_inc(S["xn_ready"], 1)
                for c in range(KC):
                    wait_rounded(f"norm{k}", c // 2 * 2 + 2)
                    V.scalar_tensor_tensor(h_lo[:, c, :], ps[:, c // 2, c % 2 * 256:c % 2 * 256 + 256],
                                           vecs[:, V_NORM + 8 * k + c:V_NORM + 8 * k + c + 1],
                                           h_hi[:, c, :].bitcast(fp32), ALU.mult, ALU.subtract).then_inc(S["operand_lo"], 1)

            def reduce_angle(src, layer):
                y, k = FTMP[0:64, 0, :], FTMP[0:64, 1, :]
                b, f = (FT[0:64, 128 + 2 * layer + n:129 + 2 * layer + n] for n in range(2))
                step(V.tensor_scalar(y, src, b, f, ALU.add, ALU.mult))
                step(V.tensor_scalar(k, y, INV_2PI, ROUND, ALU.mult, ALU.add))
                step(V.tensor_scalar(k, k, -ROUND, None, ALU.add))
                for part in (PI2_A, PI2_B, PI2_C):
                    step(V.scalar_tensor_tensor(y, k, -part, y, ALU.mult, ALU.add))
                V.tensor_scalar(y, y, SIN_MAX, -SIN_MAX, ALU.min, ALU.max).then_inc(S["filt_reduced"], 1)

            dve.wait_ge(S["x_loaded"], 16)
            dve.wait_ge(S["consts_loaded"], 16)
            norm_dve(0)
            dve.wait_ge(S["filt_hidden"], 1)
            reduce_angle(ps[0:64, 7, 0:256], 0)

            def p1_copy(g):
                dve.wait_ge(S["half_multiplied"], 4 * g + 4)
                V.tensor_copy(P1[:, 1, g * 512:(g + 1) * 512], ps[:, 5 + 2 * (g % 2), :]).then_inc(S["p1_dve"], 1)

            dve.wait_ge(S["filt_sine"], 1)
            p1_copy(0)
            dve.wait_ge(S["filt_hidden"], 2)
            reduce_angle(ps[0:64, 0, 0:256], 1)
            p1_copy(1)
            dve.wait_ge(S["gnw_loaded"], 32)
            V.tensor_copy(gate_weights[0][:, :, :], gate_columns).then_inc(S["gate_weights_ready"], 1)
            dve.wait_ge(S["gate_weights_ready"], 1)
            V.tensor_tensor(gate_weights[1][:, :, :], gate_columns, gate_weights[0][:, :, :].bitcast(fp32),
                            ALU.subtract).then_inc(S["gate_weights_ready"], 1)
            dve.wait_ge(S["filt_window"], 1)
            for pt in range(TOK):
                dve.wait_ge(S["filt_product"], pt + 1)
                V.tensor_tensor(FH[:, pt, :], ps[:, 0:4, :].rearrange("p a b -> p (a b)"), FW[:, pt, :],
                                ALU.mult).then_inc(S["filt_windowed"], 1)
                p1_copy(2 + pt)
            dve.wait_ge(S["filt_windowed"], 2)
            dve.wait_ge(S["w3_loaded"], 32)
            step(V.memset(FH[0:1, 0, D:2 * D], 0.0))
            step(V.tensor_tensor(FH[0:1, 0, 0:D], FH[0:1, 0, 0:D], wrow[0:1, :], ALU.add))
            V.tensor_tensor(FAB[:, 0], FH[:, :, 0:D], FH[:, :, D:2 * D], ALU.add).then_inc(S["filt_ab"], 1)
            V.tensor_tensor(FAB[:, 1], FH[:, :, D:2 * D], FH[:, :, 0:D], ALU.subtract).then_inc(S["filt_ab"], 1)
            dve.wait_ge(S["tab_loaded"], 16)
            dve.wait_ge(S["p1_dve"], 3)
            src = P1[:, 1, 0:1280].rearrange("p (h c) -> p h c", h=20)
            lo, hi = src[:, :, 0:32], src[:, :, 32:64]
            c = cosT[:, 1, :].unsqueeze(1).broadcast_to([128, 20, 32])
            s = sinT[:, 1, :].unsqueeze(1).broadcast_to([128, 20, 32])
            V.tensor_tensor(RA, lo, c, ALU.mult)
            step(V.tensor_tensor(RB, hi, s, ALU.mult))
            step(V.tensor_tensor(R[:, 1, :, 0:32], RA, RB, ALU.subtract))
            V.tensor_tensor(RA, lo, s, ALU.mult)
            step(V.tensor_tensor(RB, hi, c, ALU.mult))
            V.tensor_tensor(R[:, 1, :, 32:64], RA, RB, ALU.add).then_inc(S["rope_ready"], 1)
            p1_copy(4)
            dve.wait_ge(S["half_multiplied"], 22)
            V.tensor_copy(P1[:, 1, 2560:2816], ps[:, 7, 0:256]).then_inc(S["p1_dve"], 1)
            for b in range(1, 10, 2):
                dve.wait_ge(S["heads_transposed"], b + 1)
                V.tensor_scalar(RT[0:64, 2 * b:2 * b + 2, :].rearrange("p a b -> p (a b)"), ps[0:64, b % 4, :],
                                0.125 if 4 <= b < 8 else 1.0, None, ALU.mult).then_inc(S["heads_dve"], 1)
            dve.wait_ge(S["dup_transposed"], 1)
            dve.wait_ge(S["cmps_loaded"], 16)
            for kv in range(2):
                for a in range(2):
                    rows = slice(a * 64, a * 64 + 64)
                    tokens = ps[rows, 4 + kv, :].rearrange("p (g n b) -> p g n b", g=2, b=16)[:, :, a:a + NCMP, :]
                    pos = cmps[rows, kv * 16:kv * 16 + 16].unsqueeze(1).unsqueeze(1).broadcast_to([64, 2, NCMP, 16])
                    V.tensor_tensor(BLK[rows, kv].rearrange("p b (g n) -> p g n b", g=2), tokens, pos,
                                    ALU.add).then_inc(S["blocks_ready"], 1)
            for h in range(4):
                dve.wait_ge(S["ret_scores"], h + 1)
                V.tensor_tensor(SD[:, h, :], ps[:, h, 0:384], decay[:, h, :], ALU.mult).then_inc(S["ret_decayed"], 1)
            dve.wait_ge(S["cmp_product"], 1)
            V.tensor_tensor(KCR[0:64, :], ps[0:64, 4, 30:60], aux[0:64, T_CC + 30:T_CC + 60], ALU.mult)
            step(V.tensor_tensor(KCT[0:64, :], ps[0:64, 4, 0:30], aux[0:64, T_CC:T_CC + 30], ALU.mult))
            V.tensor_tensor(KCT[0:64, :], KCT[0:64, :], KCR[0:64, :], ALU.add).then_inc(S["kc_ready"], 1)
            dve.wait_ge(S["ret_out"], 1)
            o = ps[:, 6:8, :].rearrange("p a (h c) -> p (a h) c", h=4)

            def over(col, n, width):
                return stat[:, col:col + n].unsqueeze(2).broadcast_to([128, n, width])

            step(V.tensor_reduce(stat[:, ST_GSUM:ST_GSUM + 8], o, AX, ALU.add))
            step(V.tensor_scalar(stat[:, ST_GMEAN:ST_GMEAN + 8], stat[:, ST_GSUM:ST_GSUM + 8], 1.0 / 128, None, ALU.mult))
            V.tensor_tensor(gn, o, over(ST_GMEAN, 8, 128), ALU.subtract).then_inc(S["ret_normed"], 1)
            dve.wait_ge(S["cmp_scores"], 1)
            step(V.tensor_tensor(CE.rearrange("p t h n -> p t h n"),
                                 ps[:, 4, 0:240].rearrange("p (t h n) -> p t h n", t=2, h=8),
                                 drop.unsqueeze(2).broadcast_to([128, 2, 8, NCMP]), ALU.add))
            ce = CE.rearrange("p t h n -> p (t h) n")
            step(V.tensor_reduce(stat[:, ST_CMAX:ST_CMAX + 16], ce, AX, ALU.max))
            V.tensor_tensor(ce, ce, over(ST_CMAX, 16, NCMP), ALU.subtract).then_inc(S["cmp_shifted"], 1)
            step(V.tensor_tensor(gn2, gn, gn, ALU.mult))
            step(V.tensor_reduce(stat[:, ST_GVAR:ST_GVAR + 8], gn2, AX, ALU.add))
            step(V.tensor_scalar(stat[:, ST_GVAR:ST_GVAR + 8], stat[:, ST_GVAR:ST_GVAR + 8], 1.0 / 128, 1e-5, ALU.mult, ALU.add))
            V.reciprocal(stat[:, ST_GVAR:ST_GVAR + 8], stat[:, ST_GVAR:ST_GVAR + 8]).then_inc(S["gn_inv"], 1)
            dve.wait_ge(S["cmp_exp"], 1)
            V.tensor_tensor(CE, CE, keep.unsqueeze(2).broadcast_to([128, 2, 8, NCMP]), ALU.mult).then_inc(S["cmp_probs"], 1)
            dve.wait_ge(S["cmp_probs"], 1)
            step(V.tensor_reduce(stat[:, ST_CSUM:ST_CSUM + 16], ce, AX, ALU.add))
            step(V.tensor_scalar(stat[:, ST_CSUM:ST_CSUM + 16], stat[:, ST_CSUM:ST_CSUM + 16], 1e-30, None, ALU.max))
            step(V.reciprocal(stat[:, ST_CREC:ST_CREC + 16], stat[:, ST_CSUM:ST_CSUM + 16]))
            dve.wait_ge(S["gates_ready"], 1)
            step(V.tensor_tensor(stat[:, ST_CREC:ST_CREC + 16].rearrange("p (t h) -> p t h", t=2),
                                 stat[:, ST_CREC:ST_CREC + 16].rearrange("p (t h) -> p t h", t=2),
                                 P1[:, :, 2816:2824], ALU.mult))
            dve.wait_ge(S["gn_rstd"], 1)
            step(V.tensor_tensor(gn, gn, over(ST_GRSTD, 8, 128), ALU.mult))
            dve.wait_ge(S["gnw_loaded"], 32)
            g2 = gn.rearrange("p (t h) c -> p t (h c)", t=2)
            step(V.tensor_tensor(g2, g2, gnw.unsqueeze(1).broadcast_to([128, 2, 512]), ALU.mult))
            dve.wait_ge(S["silu_ready"], 1)
            V.tensor_tensor(mix[:, :, 0:512], g2, P1[:, :, 2048:2560], ALU.mult)

            causal = aux[:, T_CAUSAL:T_CAUSAL + 256]

            def maxima(u):
                qt = u // 2 % 2
                nk = 128 * (qt + 1)
                dve.wait_ge(S["att_scores"], u + 1)
                if u >= 2:
                    dve.wait_ge(S["att_transposed"], u - 1)
                for r in range(4):
                    col = r * nk
                    m = ST_MAX + 4 * (u % 2) + r
                    V.tensor_tensor_reduce(out=SM[:, u % 2, r, 0:nk],
                                           in0=ps[:, 2 * (u % 2) + col // 512, col % 512:col % 512 + nk],
                                           in1=causal[:, 256 - nk:256], scale=1.0, scalar=-3e38, op0=ALU.add, op1=ALU.max,
                                           accum_out=stat[:, m:m + 1]).then_inc(S["att_rowmax"], 1)
                dve.wait_ge(S["att_rowmax"], 4 * u + 4)
                m = 4 * (u % 2)
                V.tensor_scalar(stat[:, ST_NMAX + m:ST_NMAX + m + 4], stat[:, ST_MAX + m:ST_MAX + m + 4], -1.0, None,
                                ALU.mult).then_inc(S["att_max"], 1)

            maxima(0)
            dve.wait_ge(S["cmp_out"], 1)
            for t in range(TOK):
                V.tensor_tensor(mix[:, t, 512:1024].rearrange("p (h c) -> p h c", h=8),
                                ps[:, 4 + t, :].rearrange("p (h c) -> p h c", h=8),
                                over(ST_CREC + 8 * t, 8, 64), ALU.mult).then_inc(S["cmp_done"], 1)
            maxima(1)
            for u in range(8):
                if u // 2 % 2:
                    dve.wait_ge(S["att_transposed"], u + 1)
                    V.tensor_copy(ET[:, u % 2, 512:1024], ps[:, 5, :]).then_inc(S["att_copied_dve"], 1)
                if u + 2 < 8:
                    maxima(u + 2)
                if u % 2:
                    n = u // 2
                    qt, branch = n % 2, 1 + n // 2
                    rec, tmp = ST_REC + 8 * n, gn2[:, 0:4, :].rearrange("p a b -> p (a b)")
                    dve.wait_ge(S["att_exp"], 4 * u + 4)
                    step(V.reciprocal(stat[:, rec:rec + 8], stat[:, ST_SUM + 8 * n:ST_SUM + 8 * n + 8]))
                    step(V.tensor_tensor(stat[:, rec:rec + 8], stat[:, rec:rec + 8],
                                         P1[:, qt, 2816 + 8 * branch:2824 + 8 * branch], ALU.mult))
                    dve.wait_ge(S["att_out"], u + 1)
                    step(V.tensor_tensor(tmp.rearrange("p (h c) -> p h c", h=8),
                                         ps[:, 6 + n % 2, :].rearrange("p (h c) -> p h c", h=8), over(rec, 8, 64), ALU.mult))
                    dve.wait_ge(S["cmp_done"], 2)
                    V.tensor_tensor(mix[:, qt, 512:1024], mix[:, qt, 512:1024], tmp, ALU.add).then_inc(S["att_done"], 1)
                    dve.wait_ge(S["att_done"], n + 1)
            for b in range(4):
                wait_rounded("mixed", b + 1)
                rest_of(ps[:, b, :], *(part[:, 2 * b:2 * b + 2, :].rearrange("p a b -> p (a b)") for part in in_parts))

            def post_dve(k):
                inverse("post_squares", 2 * k + 2, "post_inv", k + 1)
                dve.wait_ge(S["rows_loaded"], 16 * k + 16)
                dve.wait_ge(S["post_rstd"], k + 1)
                for t in range(TOK):
                    V.scalar_tensor_tensor(xn[:, t, :], ps[:, 4 + 2 * t:6 + 2 * t, :].rearrange("p a b -> p (a b)"),
                                           stat[:, ST_RSTD + t:ST_RSTD + t + 1], wrow[:, :], ALU.mult,
                                           ALU.mult).then_inc(S["wrow_free"], 1)
                    if t == 0:
                        dve.wait_ge(S["x_reloaded"], 16 * k + 16)
                    dve.wait_ge(S["wrow_free"], 2 * k + t + 1)
                    V.tensor_tensor(x[:, t, :], x[:, t, :], xn[:, t, :], ALU.add).then_inc(S["post_done"], 1)

            post_dve(0)
            norm_dve(1)

            def ffn_dve(i, it=None):
                dve.wait_ge(S["ffn_conv_act"], at(2 * i + 2, 8, it))
                for tap in (1, 0):
                    s = 2 - tap
                    for j in range(2):
                        col = at(V_CONV + (j * NFF + i) * 3 + tap, 12, it)
                        y = CONV[:, i % 2, j, s:256]
                        if tap == 0:
                            dve.wait_ge(S["ffn_tap"], at(2 * i + j + 1, 8, it))
                        V.scalar_tensor_tensor(y, ps[:, i % 4, j * 256:j * 256 + 256 - s], vecs[:, bass.ds(col, 1)], y,
                                               ALU.mult, ALU.add).then_inc(S["ffn_tap"] if tap else S["ffn_conv_dve"], 1)
                dve.wait_ge(S["ffn_gelu"], at(i + 1, 4, it))
                dve.wait_ge(S["ffn_conv_dve"], at(2 * i + 2, 8, it))
                V.tensor_tensor(CONV[:, i % 2, 0, :], CONV[:, i % 2, 0, :], CONV[:, i % 2, 1, :],
                                ALU.mult).then_inc(S["ffn_product"], 1)
                dve.wait_ge(S["ffn_product"], at(i + 1, 4, it))
                if i >= 4:
                    down = W_FFN + 4 + 3 * ((i - 4) // 2)
                    dve.wait_ge(S["half_multiplied"], at(2 * down + i % 2 + 1, 12, it))
                V.tensor_copy(ffn_hi[:, i % 4, :], CONV[:, i % 2, 0, :]).then_inc(S["ffn_rounded"], 1)
                dve.wait_ge(S["ffn_rounded"], at(i + 1, 4, it))
                V.tensor_tensor(ffn_lo[:, i % 4, :], CONV[:, i % 2, 0, :], ffn_hi[:, i % 4, :].bitcast(fp32),
                                ALU.subtract).then_inc(S["ffn_gated"], 1)

            for i in range(6):
                ffn_dve(i)
            with dve.Fori(0, 4) as it:
                for i in range(6, 10):
                    ffn_dve(i, it)
            post_dve(1)
            dve_second(dve, step, inverse, wait_rounded, rest_of, norm_dve)



def shape_constants():
    import numpy as np
    f32 = np.float32
    t = np.arange(SEQ)
    inv = 1.0 / (10000.0 ** (np.arange(0, 64, 2) / 64.0))
    ang = t[:, None] * inv[None, :]
    cos = np.cos(ang).reshape(2, 128, 32).transpose(1, 0, 2)
    sin = np.sin(ang).reshape(2, 128, 32).transpose(1, 0, 2)
    decay = np.zeros((128, 4, 384))
    j, i = np.arange(128)[:, None], np.arange(256)[None, :]
    for h in range(4):
        lg = np.log(1.0 - 2.0 ** (-5.0 - h))
        full = np.where(i >= j, np.exp(lg * np.maximum(i - j, 0)), 0.0) * 64 ** -0.5
        decay[:, h, :256] = full
        decay[:, h, 256:] = full[:, :128]
    r = np.arange(128)
    tri = np.where(r[None, :] <= r[:, None], 0.0, -1e30)
    causal = np.concatenate([np.zeros((128, 128)), tri], 1)
    end = np.arange(NCMP) * 16 + 31
    keep = (end[None, None, :] <= (r[:, None] + 128 * np.arange(2)[None, :])[:, :, None]).astype(float)
    drop = np.where(keep > 0, 0.0, -1e30)
    cang = inv[:, None] * end[None, :]
    ccos = np.tile(np.cos(cang), (2, 2))
    csin = np.concatenate([-np.tile(np.sin(cang), (1, 2)), np.tile(np.sin(cang), (1, 2))], 0)
    cc = np.zeros((128, 60)); cc[:64, :30] = ccos; cc[:64, 30:] = csin
    tab1 = np.concatenate([a.reshape(128, -1) for a in (cos, sin, decay, causal, keep, drop, cc)], 1).astype(f32)
    ident = np.eye(128, dtype=f32)
    th = 2 * np.pi * np.outer(np.arange(256), np.arange(256) + 0.5) / 512
    def split(m):
        return m.reshape(2, 128, 256).transpose(1, 0, 2).reshape(128, 512)
    dft = np.concatenate([split(np.cos(th)), split(np.sin(th)), split(np.cos(th).T / 256), split(-np.sin(th).T / 256)], 1).astype(f32)
    bands = np.linspace(1e-4, 15, 16, dtype=f32).astype(float)
    fa = (2.0 * np.pi / SEQ) * t[:, None] * bands[None, :]
    tt = t / (SEQ - 1)
    z = np.concatenate([tt[:, None], np.cos(fa), -np.sin(fa)], 1)
    zt = np.zeros((128, 256 + 2)); zt[:33, :256] = z.T
    zt[:, 256:] = -tt.reshape(2, 128).T
    lv = np.zeros((128, 8, 128))
    for n, m in enumerate((64, 32, 16, 8, 4, 2, 1)):
        same = (r[:, None] // (2 * m)) == (r[None, :] // (2 * m))
        lv[:, n] = same & ((r[:, None] // m) != (r[None, :] // m))
    lv[:, 7] = np.eye(128)
    iota = np.tile(np.arange(128), (128, 1))
    return {"tab1": tab1, "ident": ident, "dft": dft, "zt": zt.astype(f32),
            "levels": lv.reshape(128, -1).astype(f32), "iota": iota.astype(f32)}


def lay_out(a):
    import numpy as np
    f32 = np.float32

    def token_major(w):
        n = w.shape[1] // 512
        return w.reshape(2, 4, 128, n, 512).transpose(3, 0, 2, 1, 4).reshape(2 * n, 128, 2048)

    def channel_major(w):
        n = w.shape[1] // 256
        return w.reshape(8, 128, n, 2, 128).transpose(2, 1, 3, 0, 4).reshape(n, 128, 2048)

    w = a["w_in"][0]
    c = np.cumsum([0, 256, 256, 512, 512, 512] + [128] * 6 + [24])
    rq, rk, rv, rg, nq, kcm, vcm, ksl, vsl, kwn, vwn, ng = [w[:, c[i]:c[i + 1]] for i in range(12)]
    head = np.concatenate([rq, rk, nq, ksl, kwn, kcm, vcm, rv, rg], 1)
    tail = np.concatenate([vsl, vwn], 1).reshape(8, 128, 256).transpose(1, 0, 2).reshape(1, 128, 2048)
    cmp1 = [a[n][0].reshape(2, 2, 8, 64, 256).transpose(1, 0, 3, 2, 4).reshape(2, 128, 2048)
            for n in ("cmp_k_w1", "cmp_v_w1")]
    up = a["ffn_w_up"][0].reshape(8, 128, 2, 22, 128).transpose(3, 1, 2, 0, 4).reshape(22, 128, 2048)
    down = a["ffn_w_down"][0].reshape(11, 2, 128, 1024).transpose(0, 2, 1, 3).reshape(11, 128, 2048)
    ffn = [up[0:2]]
    for p in range(1, 11):
        ffn += [up[2 * p:2 * p + 2], down[p - 1:p]]
    ffn += [down[10:11]]
    w2 = a["w_in_2"][0]
    q, zf, zb, inp, og, hy, gates = [w2[:, i:j] for i, j in ((0, 1024), (1024, 2048), (2048, 3072), (3072, 4096),
                                                             (4096, 5120), (5120, 8192), (8192, 10240))]
    peer_u = a["peer_u_2"][0].reshape(128, 64, 2, 8, 128).transpose(1, 4, 2, 3, 0).reshape(64, 128, 2048)
    peer_v = a["peer_v_2"][0].reshape(128, 64, 2048).transpose(1, 0, 2)
    stream = np.concatenate([token_major(head), tail] + cmp1 + [token_major(a["w_out"][0])] + ffn
                            + [channel_major(hy), channel_major(gates[:, 1024:]), channel_major(q), channel_major(zf),
                               channel_major(zb), token_major(inp), channel_major(og), channel_major(gates[:, :1024]),
                               channel_major(a["w_branch_b_2"][0]), channel_major(a["w_branch_a_2"][0]),
                               token_major(a["w_out_2"][0]), channel_major(a["peer_w_q_2"][0]), peer_u, peer_v], 0)

    def cols(v, n):
        return v.reshape(-1, n, 128).transpose(2, 1, 0).reshape(128, -1)

    pos = [a[n][0].reshape(2, 16, 64).transpose(0, 2, 1).reshape(128, 16) for n in ("cmp_k_pos", "cmp_v_pos")]
    w2k, w2v = a["cmp_k_w2"][0].reshape(2, 128, 64), a["cmp_v_w2"][0].reshape(2, 128, 64)
    w2r = np.concatenate([w2k[:, :, 32:], w2k[:, :, :32]], 2)
    filt = np.zeros((128, 132), f32)
    filt[:33, 0:64] = a["filt_w1_2"][0]
    filt[:64, 64:128] = a["filt_w2_2"][0]
    for n, name in enumerate(("filt_b1_2", "filt_freq1_2", "filt_b2_2", "filt_freq2_2")):
        filt[:64, 128 + n] = a[name][0]
    vecs = np.concatenate([
        cols(a["norm_mix_pre"][0], 8), cols(a["norm_ffn_pre"][0], 8), cols(a["norm_mix_g_2"][0], 8),
        cols(a["norm_ffn_g_2"][0], 8), cols(a["ffn_conv"][0], 44), cols(a["hyena_conv_w_2"][0], 24),
        cols(a["hyena_conv_b_2"][0], 24), cols(a["hgrn_lb_logits_2"], 8), a["hgrn_norm_g_2"][0].reshape(128, 1)], 1)
    cmps = np.concatenate(pos + [m.transpose(1, 0, 2).reshape(128, 128) for m in (w2k, w2r, w2v)], 1)
    rows = {n: np.broadcast_to(a[k].reshape(1, -1), (128, a[k].size)) for n, k in
            (("post1", "norm_mix_post"), ("post2", "norm_ffn_post"), ("final", "norm_final_g_2"), ("gnw", "ret_gn_w"),
             ("fdecay", "filt_decay_2"))}
    return {"x": a["x"][0].reshape(2, 128, 1024).transpose(1, 0, 2), "stream": stream, "vecs": vecs, "cmps": cmps,
            "gate_columns": ng.reshape(8, 128, 24).transpose(1, 0, 2).reshape(128, 192),
            "filt": filt, "w3": a["filt_w3_2"][0], "bias": a["hyena_bias_2"].reshape(1, 1024),
            "subkeys": a["peer_subkeys_2"][0].transpose(3, 0, 1, 2).reshape(128, 2048), **rows}


def kernel(**inputs):
    import numpy as np
    import concourse.bacc as bacc
    from concourse import mybir
    from concourse.bass_utils import run_bass_kernel_spmd

    arrays = lay_out({k: np.asarray(v) for k, v in inputs.items()})
    arrays.update(shape_constants())
    nc = bacc.Bacc("TRN2", target_bir_lowering=False, num_devices=1)
    sent, dram = {}, {}
    for name, value in arrays.items():
        value = np.ascontiguousarray(value)
        sent[f"in_{name}"] = value
        dram[name] = nc.dram_tensor(f"in_{name}", value.shape, mybir.dt.float32, kind="ExternalInput").ap()
    dram["out"] = nc.dram_tensor("out_y", (128, 2, 1024), mybir.dt.float32, kind="ExternalOutput").ap()
    dram["residual"] = nc.dram_tensor("residual", (128, 2, 1024), mybir.dt.float32, kind="Internal").ap()
    build(nc, dram)
    y = run_bass_kernel_spmd(nc, [sent], core_ids=[0]).results[0]["out_y"]
    return np.asarray(y).reshape(128, 2, 1024).transpose(1, 0, 2).reshape(1, 256, 1024)
```
